# Optimizing a Trainium2 kernel written in Bass

```python
import math
import jax
import jax.numpy as jnp
from jax import lax
import numpy as np
import jax, jax.numpy as jnp

D_MODEL = 1024
BATCH = 1
SEQ = 512
DEPTH = 1

N_META = 16
EPS = 1e-6
DA_HEADS = 4
DA_HEAD_DIM = 64
DA_V_DIM = 2 * DA_HEAD_DIM
DA_WIDTH = DA_HEADS * DA_V_DIM
ROPE_THETA = 500000.0
ROPE_DIM = DA_HEAD_DIM // 4
Q_BLOCK = 128
GLA_HEADS = 4
GLA_DK = 64
GLA_DV = 128
GLA_WIDTH = GLA_HEADS * GLA_DV
GLA_GATE_RANK = 16
GLA_TAU = 16.0
GLA_CHUNK = 64
MIX_WIDTH = DA_WIDTH + GLA_WIDTH
IN_SIZES = (DA_HEADS * 2 * DA_HEAD_DIM, DA_HEADS * 2 * DA_HEAD_DIM, DA_WIDTH, GLA_HEADS * GLA_DK, GLA_HEADS * GLA_DK, GLA_WIDTH, GLA_WIDTH, GLA_GATE_RANK, GLA_GATE_RANK)
IN_WIDTH = sum(IN_SIZES)
PEER_HEADS = 8
PEER_NKEYS = 128
PEER_EXPERTS = PEER_NKEYS * PEER_NKEYS
PEER_KEY_DIM = 128
PEER_TOPK = 16
PEER_BLOCK = 256


def rmsnorm(x, w):
    xf = x.astype(jnp.float32)
    y = xf * lax.rsqrt(jnp.mean(xf * xf, axis=-1, keepdims=True) + EPS)
    return (y * w.astype(jnp.float32)).astype(x.dtype)

def partial_rope(x, pos):
    inv = jnp.power(ROPE_THETA, -jnp.arange(0, ROPE_DIM, 2, dtype=jnp.float32) / ROPE_DIM)
    ang = pos.astype(jnp.float32)[:, None] * inv[None, :]
    cos = jnp.cos(ang)[None, :, None, None, :]
    sin = jnp.sin(ang)[None, :, None, None, :]
    xr = x[..., :ROPE_DIM].astype(jnp.float32)
    x1, x2 = xr[..., :ROPE_DIM // 2], xr[..., ROPE_DIM // 2:]
    rot = jnp.concatenate([x1 * cos - x2 * sin, x2 * cos + x1 * sin], axis=-1)
    return jnp.concatenate([rot.astype(x.dtype), x[..., ROPE_DIM:]], axis=-1)

def diff_attention(q, k, v, lam, pos):
    B, T = q.shape[0], q.shape[1]
    q = partial_rope(q, pos) * (DA_HEAD_DIM ** -0.5)
    k = partial_rope(k, pos)
    nb = -(-T // Q_BLOCK)
    qp = jnp.pad(q, ((0, 0), (0, nb * Q_BLOCK - T), (0, 0), (0, 0), (0, 0)))
    qb = qp.reshape(B, nb, Q_BLOCK, DA_HEADS, 2, DA_HEAD_DIM).transpose(1, 0, 2, 3, 4, 5)

    def block(qi):
        s = jnp.einsum('bqhcd,bkhcd->bhcqk', qi, k).astype(jnp.float32)
        p = jax.nn.softmax(s, axis=-1)
        a = p[:, :, 0] - lam * p[:, :, 1]
        return jnp.einsum('bhqk,bkhv->bqhv', a.astype(v.dtype), v)

    o = lax.map(block, qb)
    return o.transpose(1, 0, 2, 3, 4).reshape(B, nb * Q_BLOCK, DA_HEADS, DA_V_DIM)[:, :T]

def gla_chunk_scan(q, k, v, g):
    B, L = q.shape[0], q.shape[1]
    n = L // GLA_CHUNK

    def to_chunks(a):
        return a.reshape(B, n, GLA_CHUNK, a.shape[2], a.shape[3]).transpose(1, 0, 3, 2, 4)

    mask = jnp.tril(jnp.ones((GLA_CHUNK, GLA_CHUNK), dtype=bool))[:, :, None]

    def step(state, inp):
        qc, kc, vc, gc = inp
        b = jnp.cumsum(gc, axis=2)
        rel = b[:, :, :, None, :] - b[:, :, None, :, :]
        decay = jnp.exp(jnp.where(mask, rel, -jnp.inf))
        attn = jnp.einsum('bhid,bhjd,bhijd->bhij', qc, kc, decay)
        o = jnp.einsum('bhij,bhjv->bhiv', attn, vc) + jnp.einsum('bhid,bhdv->bhiv', qc * jnp.exp(b), state)
        b_last = b[:, :, -1]
        state = state * jnp.exp(b_last)[..., None] + jnp.einsum('bhjd,bhjv->bhdv', kc * jnp.exp(b_last[:, :, None] - b), vc)
        return state, o

    state0 = jnp.zeros((B, q.shape[2], q.shape[3], v.shape[3]), jnp.float32)
    _, o = lax.scan(step, state0, (to_chunks(q), to_chunks(k), to_chunks(v), to_chunks(g)))
    return o.transpose(1, 0, 3, 2, 4).reshape(B, L, q.shape[2], v.shape[3])

def gla_bidirectional(q, k, v, g_f, g_b):
    pad = (-N_META) % GLA_CHUNK
    padf = lambda a: jnp.pad(a, ((0, 0), (pad, 0), (0, 0), (0, 0)))
    flip = lambda a: a[:, ::-1]
    qp, kp, vp = padf(q), padf(k), padf(v)
    o_f = gla_chunk_scan(qp, kp, vp, padf(g_f))
    o_b = flip(gla_chunk_scan(flip(qp), flip(kp), flip(vp), flip(padf(g_b))))
    return (o_f + o_b)[:, pad:]

def peer_ffn(x, w_q, sub_keys, u, v):
    N, D = x.shape
    nb = -(-N // PEER_BLOCK)
    xb = jnp.pad(x, ((0, nb * PEER_BLOCK - N), (0, 0))).reshape(nb, PEER_BLOCK, D)

    def block(xi):
        n = xi.shape[0]
        q = (xi @ w_q).reshape(n, PEER_HEADS, 2, PEER_KEY_DIM)
        s = jnp.einsum('nhpc,hpkc->nhpk', q, sub_keys).astype(jnp.float32)
        ts, ti = lax.top_k(s, PEER_TOPK)
        cand_s = (ts[:, :, 0, :, None] + ts[:, :, 1, None, :]).reshape(n, PEER_HEADS, PEER_TOPK * PEER_TOPK)
        cand_i = (ti[:, :, 0, :, None] * PEER_NKEYS + ti[:, :, 1, None, :]).reshape(n, PEER_HEADS, PEER_TOPK * PEER_TOPK)
        best_s, best_p = lax.top_k(cand_s, PEER_TOPK)
        idx = jnp.take_along_axis(cand_i, best_p, axis=-1)
        gate = jax.nn.softmax(best_s, axis=-1)
        act = jax.nn.gelu(jnp.einsum('nd,nhkd->nhk', xi, u[idx]).astype(jnp.float32), approximate=False)
        return jnp.einsum('nhk,nhkd->nd', (gate * act).astype(xi.dtype), v[idx])

    return lax.map(block, xb).reshape(nb * PEER_BLOCK, D)[:N]

def first_inputs(seed: int = 0) -> dict:
    key = jax.random.key(seed)
    ks = jax.random.split(key, 24)
    nrm = lambda k, shape, s: jax.random.normal(k, shape, jnp.float32) * s
    gain = lambda k, shape: 1.0 + 0.02 * jax.random.normal(k, shape, jnp.float32)
    return {
        'x': nrm(ks[0], (BATCH, SEQ, D_MODEL), 1.0),
        'meta_tokens': nrm(ks[1], (N_META, D_MODEL), 1.0),
        'ln1_w': gain(ks[2], (DEPTH, D_MODEL)),
        'w_in': nrm(ks[3], (DEPTH, D_MODEL, IN_WIDTH), D_MODEL ** -0.5),
        'da_lambda_q1': nrm(ks[4], (DEPTH, DA_HEAD_DIM), 0.1),
        'da_lambda_k1': nrm(ks[5], (DEPTH, DA_HEAD_DIM), 0.1),
        'da_lambda_q2': nrm(ks[6], (DEPTH, DA_HEAD_DIM), 0.1),
        'da_lambda_k2': nrm(ks[7], (DEPTH, DA_HEAD_DIM), 0.1),
        'da_subln_w': gain(ks[8], (DEPTH, DA_V_DIM)),
        'gla_gate_w2_f': nrm(ks[9], (DEPTH, GLA_GATE_RANK, GLA_HEADS * GLA_DK), GLA_GATE_RANK ** -0.5),
        'gla_gate_b_f': nrm(ks[10], (DEPTH, GLA_HEADS * GLA_DK), 0.1),
        'gla_gate_w2_b': nrm(ks[11], (DEPTH, GLA_GATE_RANK, GLA_HEADS * GLA_DK), GLA_GATE_RANK ** -0.5),
        'gla_gate_b_b': nrm(ks[12], (DEPTH, GLA_HEADS * GLA_DK), 0.1),
        'gla_norm_w': gain(ks[13], (DEPTH, GLA_DV)),
        'w_out': nrm(ks[14], (DEPTH, MIX_WIDTH, D_MODEL), MIX_WIDTH ** -0.5),
        'ln2_w': gain(ks[15], (DEPTH, D_MODEL)),
        'peer_w_q': nrm(ks[16], (DEPTH, D_MODEL, PEER_HEADS * 2 * PEER_KEY_DIM), D_MODEL ** -0.5),
        'peer_sub_keys': nrm(ks[17], (DEPTH, PEER_HEADS, 2, PEER_NKEYS, PEER_KEY_DIM), PEER_KEY_DIM ** -0.5),
        'peer_u': nrm(ks[18], (DEPTH, PEER_EXPERTS, D_MODEL), D_MODEL ** -0.5),
        'peer_v': nrm(ks[19], (DEPTH, PEER_EXPERTS, D_MODEL), PEER_HEADS ** -0.5),
        'final_norm_w': gain(ks[20], (D_MODEL,)),
    }

def first_block(x, meta_tokens, ln1_w, w_in, da_lambda_q1, da_lambda_k1, da_lambda_q2, da_lambda_k2, da_subln_w, gla_gate_w2_f, gla_gate_b_f, gla_gate_w2_b, gla_gate_b_b, gla_norm_w, w_out, ln2_w, peer_w_q, peer_sub_keys, peer_u, peer_v, final_norm_w):
    B = x.shape[0]
    meta = jnp.broadcast_to(meta_tokens.astype(x.dtype)[None], (B, N_META, D_MODEL))
    h = jnp.concatenate([meta, x], axis=1)
    T = h.shape[1]
    pos = jnp.arange(T)
    splits = np.cumsum(IN_SIZES)[:-1].tolist()
    for l in range(DEPTH):
        xn = rmsnorm(h, ln1_w[l])
        proj = xn @ w_in[l]
        dq, dk, dv, gq, gk, gv, gr, zf, zb = jnp.split(proj, splits, axis=-1)

        lam_init = 0.8 - 0.6 * math.exp(-0.3 * l)
        lam = (jnp.exp(jnp.sum(da_lambda_q1[l].astype(jnp.float32) * da_lambda_k1[l].astype(jnp.float32)))
               - jnp.exp(jnp.sum(da_lambda_q2[l].astype(jnp.float32) * da_lambda_k2[l].astype(jnp.float32))) + lam_init)
        da = diff_attention(dq.reshape(B, T, DA_HEADS, 2, DA_HEAD_DIM), dk.reshape(B, T, DA_HEADS, 2, DA_HEAD_DIM),
                            dv.reshape(B, T, DA_HEADS, DA_V_DIM), lam, pos)
        da = (rmsnorm(da, da_subln_w[l]) * (1.0 - lam_init)).reshape(B, T, DA_WIDTH)

        f32 = jnp.float32
        log_g_f = jax.nn.log_sigmoid((zf @ gla_gate_w2_f[l] + gla_gate_b_f[l]).astype(f32)) / GLA_TAU
        log_g_b = jax.nn.log_sigmoid((zb @ gla_gate_w2_b[l] + gla_gate_b_b[l]).astype(f32)) / GLA_TAU
        go = gla_bidirectional((gq.astype(f32) * (GLA_DK ** -0.5)).reshape(B, T, GLA_HEADS, GLA_DK),
                               gk.astype(f32).reshape(B, T, GLA_HEADS, GLA_DK),
                               gv.astype(f32).reshape(B, T, GLA_HEADS, GLA_DV),
                               log_g_f.reshape(B, T, GLA_HEADS, GLA_DK),
                               log_g_b.reshape(B, T, GLA_HEADS, GLA_DK))
        go = rmsnorm(go, gla_norm_w[l]).reshape(B, T, GLA_WIDTH).astype(h.dtype) * jax.nn.silu(gr)

        h = h + jnp.concatenate([da, go], axis=-1) @ w_out[l]
        if l == DEPTH - 1:
            h = h[:, N_META:]

        hn = rmsnorm(h, ln2_w[l])
        h = h + peer_ffn(hn.reshape(-1, D_MODEL), peer_w_q[l], peer_sub_keys[l], peer_u[l], peer_v[l]).reshape(h.shape)
    return rmsnorm(h, final_norm_w)


POOL_WINDOWS = (2, 4, 8, 16)
POOL_GROUPS = len(POOL_WINDOWS)
POOL_WIDTH = D_MODEL
POOL_GROUP = POOL_WIDTH // POOL_GROUPS
SGU_CHUNK = 128
SGU_WIDTH = D_MODEL
SGU_HEADS = 8
SGU_HEAD_DIM = SGU_WIDTH // SGU_HEADS
N_BRANCHES = 2
IN_WIDTH_2 = POOL_WIDTH + 2 * SGU_WIDTH + N_BRANCHES * D_MODEL
D_FF = 2816
CONV_WIDTH = 3
PLE_DIM = 256


def rmsnorm_2(x, g):
    xf = x.astype(jnp.float32)
    y = xf * lax.rsqrt(jnp.mean(xf * xf, axis=-1, keepdims=True) + EPS)
    return (y * g.astype(jnp.float32)).astype(x.dtype)

def pool_mixer(h, w_pool, pool_scale):
    T = h.shape[1]
    hf = h.astype(jnp.float32)
    c = jnp.cumsum(hf, axis=1)
    t = jnp.arange(T)
    outs = []
    for gi, w in enumerate(POOL_WINDOWS):
        sl = slice(gi * POOL_GROUP, (gi + 1) * POOL_GROUP)
        cg = c[..., sl]
        prev = jnp.pad(cg, ((0, 0), (w, 0), (0, 0)))[:, :T]
        cnt = jnp.minimum(t + 1, w).astype(jnp.float32)[None, :, None]
        outs.append((cg - prev) / cnt - hf[..., sl])
    pooled = jnp.stack(outs, axis=2).astype(h.dtype)
    y = jnp.einsum('btgc,gcd->btgd', pooled, w_pool)
    return y.reshape(h.shape) * pool_scale

def spatial_gating(z_uv, sgu_norm, w_spatial, b_spatial):
    B, T, _ = z_uv.shape
    z = jax.nn.gelu(z_uv, approximate=False)
    u, v = z[..., :SGU_WIDTH], z[..., SGU_WIDTH:]
    v = rmsnorm_2(v, sgu_norm)
    nc = T // SGU_CHUNK
    v = v.reshape(B, nc, SGU_CHUNK, SGU_HEADS, SGU_HEAD_DIM)
    mask = jnp.tril(jnp.ones((SGU_CHUNK, SGU_CHUNK), dtype=w_spatial.dtype))
    ws = w_spatial * mask[None]
    mixed = jnp.einsum('hts,bnshd->bnthd', ws, v)
    mixed = mixed + jnp.transpose(b_spatial)[None, None, :, :, None]
    return u * mixed.reshape(B, T, SGU_WIDTH)

def conv_ffn(h, w_up, conv_w, conv_b, w_down):
    T = h.shape[1]
    up = h @ w_up
    up_pad = jnp.pad(up, ((0, 0), (CONV_WIDTH - 1, 0), (0, 0)))
    conv = conv_b
    for k in range(CONV_WIDTH):
        conv = conv + conv_w[k] * up_pad[:, k:k + T]
    a, b = conv[..., :D_FF], conv[..., D_FF:]
    return (jax.nn.gelu(a, approximate=False) * b) @ w_down

def second_inputs(seed: int = 0) -> dict:
    key = jax.random.key(seed)
    ks = jax.random.split(key, 24)
    f32 = jnp.float32
    L, D = DEPTH, D_MODEL

    def nrm(k, shape, scale):
        return jax.random.normal(k, shape, f32) * scale

    def gain(k, shape):
        return 1.0 + 0.05 * jax.random.normal(k, shape, f32)

    return {
        "x": nrm(ks[0], (BATCH, SEQ, D), 1.0),
        "p": nrm(ks[1], (DEPTH, BATCH, SEQ, PLE_DIM), 1.0),
        "mix_norm": gain(ks[2], (L, D)),
        "w_in": nrm(ks[3], (L, D, IN_WIDTH_2), D ** -0.5),
        "w_pool": nrm(ks[4], (L, POOL_GROUPS, POOL_GROUP, POOL_GROUP), POOL_GROUP ** -0.5),
        "pool_scale": gain(ks[5], (L, POOL_WIDTH)),
        "sgu_norm": gain(ks[6], (L, SGU_WIDTH)),
        "w_spatial": nrm(ks[7], (L, SGU_HEADS, SGU_CHUNK, SGU_CHUNK), 0.5 * SGU_CHUNK ** -0.5),
        "b_spatial": gain(ks[8], (L, SGU_HEADS, SGU_CHUNK)),
        "w_branch_a": nrm(ks[9], (L, POOL_WIDTH, D), POOL_WIDTH ** -0.5),
        "w_branch_b": nrm(ks[10], (L, SGU_WIDTH, D), SGU_WIDTH ** -0.5),
        "w_out": nrm(ks[11], (L, D, D), D ** -0.5),
        "ffn_norm": gain(ks[12], (L, D)),
        "w_up": nrm(ks[13], (L, D, 2 * D_FF), D ** -0.5),
        "conv_w": nrm(ks[14], (L, CONV_WIDTH, 2 * D_FF), CONV_WIDTH ** -0.5),
        "conv_b": nrm(ks[15], (L, 2 * D_FF), 0.02),
        "w_down": nrm(ks[16], (L, D_FF, D), D_FF ** -0.5),
        "ple_norm": gain(ks[17], (L, D)),
        "w_ple_gate": nrm(ks[18], (L, D, D), D ** -0.5),
        "w_ple": nrm(ks[19], (L, PLE_DIM, D), PLE_DIM ** -0.5),
        "final_norm": gain(ks[20], (D,)),
    }

def second_block(x, p, mix_norm, w_in, w_pool, pool_scale, sgu_norm, w_spatial, b_spatial,
              w_branch_a, w_branch_b, w_out, ffn_norm, w_up, conv_w, conv_b, w_down,
              ple_norm, w_ple_gate, w_ple, final_norm):
    o_uv = POOL_WIDTH
    o_gate = POOL_WIDTH + 2 * SGU_WIDTH
    for i in range(DEPTH):
        h = rmsnorm_2(x, mix_norm[i])
        z = h @ w_in[i]
        z_pool = z[..., :o_uv]
        z_uv = z[..., o_uv:o_gate]
        z_gate = z[..., o_gate:]
        y_a = pool_mixer(z_pool, w_pool[i], pool_scale[i]) @ w_branch_a[i]
        y_b = spatial_gating(z_uv, sgu_norm[i], w_spatial[i], b_spatial[i]) @ w_branch_b[i]
        gates = jax.nn.sigmoid(z_gate.astype(jnp.float32)).astype(x.dtype)
        g_a, g_b = gates[..., :D_MODEL], gates[..., D_MODEL:]
        x = x + (g_a * y_a + g_b * y_b) @ w_out[i]
        h = rmsnorm_2(x, ffn_norm[i])
        x = x + conv_ffn(h, w_up[i], conv_w[i], conv_b[i], w_down[i])
        gate = jax.nn.sigmoid((rmsnorm_2(x, ple_norm[i]) @ w_ple_gate[i]).astype(jnp.float32)).astype(x.dtype)
        x = x + gate * (p[i] @ w_ple[i])
    return rmsnorm_2(x, final_norm)


def setup_inputs(seed=0):
    out = dict(first_inputs(seed))
    for name, value in second_inputs(seed + 1).items():
        if name != "x":
            out[name + "_2"] = value
    return out


def reference(
    x, meta_tokens, ln1_w, w_in, da_lambda_q1, da_lambda_k1, da_lambda_q2, da_lambda_k2,
    da_subln_w, gla_gate_w2_f, gla_gate_b_f, gla_gate_w2_b, gla_gate_b_b, gla_norm_w, w_out,
    ln2_w, peer_w_q, peer_sub_keys, peer_u, peer_v, final_norm_w, p_2, mix_norm_2, w_in_2,
    w_pool_2, pool_scale_2, sgu_norm_2, w_spatial_2, b_spatial_2, w_branch_a_2, w_branch_b_2,
    w_out_2, ffn_norm_2, w_up_2, conv_w_2, conv_b_2, w_down_2, ple_norm_2, w_ple_gate_2,
    w_ple_2, final_norm_2,
):
    x = first_block(
        x, meta_tokens, ln1_w, w_in, da_lambda_q1, da_lambda_k1, da_lambda_q2, da_lambda_k2,
        da_subln_w, gla_gate_w2_f, gla_gate_b_f, gla_gate_w2_b, gla_gate_b_b, gla_norm_w, w_out,
        ln2_w, peer_w_q, peer_sub_keys, peer_u, peer_v, final_norm_w,
    )
    return second_block(
        x, p_2, mix_norm_2, w_in_2, w_pool_2, pool_scale_2, sgu_norm_2, w_spatial_2,
        b_spatial_2, w_branch_a_2, w_branch_b_2, w_out_2, ffn_norm_2, w_up_2, conv_w_2,
        conv_b_2, w_down_2, ple_norm_2, w_ple_gate_2, w_ple_2, final_norm_2,
    )


_drawn_inputs = setup_inputs


def setup_inputs(seed=0):
    import zlib

    import numpy as np

    out = dict(_drawn_inputs(seed))
    spreads = {}
    factors = {'da_subln_w': 9.078,
     'gla_gate_b_f': 2.71,
     'gla_gate_b_b': 2.886,
     'gla_norm_w': 12.014,
     'final_norm_w': 7.257,
     'pool_scale_2': 8.485,
     'sgu_norm_2': 30.489,
     'b_spatial_2': 10.177,
     'conv_b_2': 4.41,
     'ple_norm_2': 200.0,
     'ln2_w': 12.604,
     'ffn_norm_2': 3.987}
    for name, (base, spread) in spreads.items():
        noise = np.random.default_rng([zlib.crc32(name.encode()), seed]).standard_normal(out[name].shape)
        drawn = base * np.exp(spread * noise) if base else spread * noise
        out[name] = jnp.asarray(drawn.astype(out[name].dtype))
    for name, factor in factors.items():
        out[name] = (out[name] * factor).astype(out[name].dtype)
    return out
```

```python
from contextlib import ExitStack

import concourse.bass as bass
import numpy as np
from concourse import mybir

P = 128
D = 1024
KC = D // P
T = 512
TT = T // P
M = 16
TM = T + M
HEADS = 4
DH = 64
ROPE = 8
LEVELS = (1, 2, 4, 8, 16, 32, 64, 128, 256)
SMALL = [s for s in LEVELS if s < P]
PH = 8
TOP = 16
NK = 128
FF = 2816
FC = FF // P
WINDOWS = (2, 4, 8, 16)
EPS = 1e-6
LAM_INIT = 0.8 - 0.6 * float(np.exp(0.0))
WS = 64.0
ISW = 1.0 / WS

SLOTS = 4
N_Q, N_K, N_V, N_GV, N_GQ, N_GK, N_GR = 0, 4, 8, 12, 16, 18, 20
N_WO = 24
N_PQ = 32
N_U = 48
N_POOL = N_U + NK
N_WP = N_POOL + 8
N_SV = N_WP + 4
N_SU = N_SV + 8
N_GA = N_SU + 8
N_GB = N_GA + 16
N_WO2 = N_GB + 16
N_UP = N_WO2 + 8
N_DN = N_UP + 2 * FC
N_PG = N_DN + FC
N_PP = N_PG + 8
N_END = N_PP + 2

VEC = {}
_at = 0
for _name, _n in (("ln1", 8), ("ln2", 8), ("final1", 8), ("mixn", 8), ("pscale", 8), ("sgun", 8), ("ffnn", 8),
                  ("plen", 8), ("final2", 8), ("convw", 6 * FC), ("convb", 2 * FC), ("subln", 1), ("glan", 1),
                  ("gateb", 4), ("lam", 4)):
    VEC[_name] = _at
    _at += _n
NVEC = _at

GRP = 4
GROUPS = NK // GRP
NT = 64
GT = T // NT


def build(nc, io, out):
    f32, f16, u32, i32 = mybir.dt.float32, mybir.dt.float16, mybir.dt.uint32, mybir.dt.int32
    ALU, ACT, AX = mybir.AluOpType, mybir.ActivationFunctionType, mybir.AxisListType
    ctx = ExitStack()
    with ctx:
        sem_names = {}

        def sem(name):
            sem_names[name] = 1
            return ctx.enter_context(nc.semaphore(name))

        WORDS = 48000
        arena = ctx.enter_context(nc.sbuf_tensor("arena", [P, WORDS], f32))
        psum = ctx.enter_context(nc.psum_tensor("psum", [P, 8 * 512], f32))

        class Region:
            def __init__(self, start):
                self.at = self.top = start

            def take(self, n, dt=f32):
                words = n if dt in (f32, u32, i32) else (n + 1) // 2
                v = arena[:, self.at:self.at + words]
                self.at += words
                assert self.at <= WORDS, self.at
                return v if dt is f32 else v.bitcast(dt)

        def v3(ap, a):
            return ap.rearrange("p (a b) -> p a b", a=a)

        def bank(b, n=512, off=0):
            return psum[:, b * 512 + off:b * 512 + off + n]

        base = Region(0)
        ident = base.take(P)
        ones = base.take(P)
        iota = base.take(P)
        perm = base.take(P)
        masks = v3(base.take((len(SMALL) + 1) * P, u32), len(SMALL) + 1)
        ropec = base.take(TM)
        ropes = base.take(TM)
        vec = base.take(NVEC)
        icnt = base.take(16)
        io16 = base.take(16)
        w2 = v3(base.take(HEADS * P), HEADS)
        wz = base.take(KC * 32)
        wzh = v3(base.take(KC * 32, f16), KC)
        wzl = v3(base.take(KC * 32, f16), KC)
        small = base.take(64)
        wraw = v3(base.take(SLOTS * D), SLOTS)
        wh = v3(base.take(SLOTS * D, f16), SLOTS)
        wl = v3(base.take(SLOTS * D, f16), SLOTS)
        xh = v3(base.take(KC * TM, f16), KC)
        xl = v3(base.take(KC * TM, f16), KC)
        X = v3(base.take(KC * TM), KC)
        FREE = base.at

        r = Region(FREE)
        q = v3(r.take(HEADS * T), HEADS)
        k = v3(r.take(HEADS * TM), HEADS)
        dv = v3(r.take(5 * T), 5)
        pr = v3(r.take(4 * TM), 4)
        pa = v3(r.take(2 * TM), 2)
        aT = v3(r.take(5 * T), 5)
        rtmp = v3(r.take(2 * T), 2)
        gla_top = r.at
        rz = Region(FREE + HEADS * (T + TM) + 5 * T)
        z32 = rz.take(TM)
        gtmp = v3(rz.take(4 * TM), 4)
        gv = v3(r.take(5 * T), 5)
        gq = v3(r.take(HEADS * T), HEADS)
        gk = v3(r.take(HEADS * TM), HEADS)
        sgr = v3(r.take(HEADS * T), HEADS)
        B = v3(r.take(HEADS * TM), HEADS)
        otmp = v3(r.take(4 * T), 4)
        first_end = r.at
        r = Region(FREE)
        KT = v3(r.take(len(LEVELS) * T), len(LEVELS))
        QT = v3(r.take(len(LEVELS) * T), len(LEVELS))
        Aflat = r.take(TT * (T + P))
        A = v3(Aflat[:, 0:TT * T], TT)
        Adiag = v3(Aflat, TT)[:, :, 0:P]
        Am = r.take(T)
        E = v3(r.take(2 * T), 2)
        KTm = r.take(M)
        assert r.at <= gla_top, (r.at, gla_top)
        Em = Region(first_end).take(TM)
        QTm = Em[:, 0:T]
        r = Region(FREE)
        NB = WORDS - 5400
        r = Region(FREE)
        nsq1 = v3(r.take(KC * TM), KC)
        nstd1 = r.take(TM)
        ninv1 = r.take(TM)
        r = Region(WORDS - 5300)
        nsq = v3(r.take(KC * TM), KC)
        nstd = r.take(TM)
        ninv = r.take(TM)

        r = Region(FREE)
        idx_tok = v3(r.take(3 * T), 3)
        idxT = v3(r.take(3 * T), 3)
        vraw = v3(r.take(SLOTS * D), SLOTS)
        hot = v3(r.take(16 * P), 16)
        region_g = r.at
        G = [v3(r.take(P * NT), P) for _ in range(2)]
        r = Region(region_g)
        pq = v3(r.take(2 * T), 2)
        keysT = v3(r.take(2 * PH * P), 2 * PH)
        s_ = [v3(r.take(2 * T), 2) for _ in range(2)]
        s2 = v3(r.take(2 * T), 2)
        ts = v3(r.take(2 * TT * TOP), 2)
        ti = v3(r.take(2 * TT * TOP, u32), 2)
        tif = v3(r.take(2 * TT * TOP), 2)
        cand = v3(r.take(TT * 256), TT)
        cand2 = v3(r.take(TT * 256), TT)
        best = v3(r.take(TT * TOP), TT)
        pos = v3(r.take(TT * TOP, u32), TT)
        posab = v3(r.take(2 * TT * TOP, u32), 2)
        posf = v3(r.take(2 * TT * TOP), 2)
        sel = r.take(TT * 256)
        gsm = r.take(TT * TOP)
        gsum = r.take(16)
        assert r.at <= WORDS
        r = Region(FREE + 6 * T + SLOTS * D)
        vh = v3(r.take(2 * GRP * D, f16), 2 * GRP)
        vl = v3(r.take(2 * GRP * D, f16), 2 * GRP)
        Ah = v3(r.take(2 * GRP * T, f16), 2 * GRP)
        Al = v3(r.take(2 * GRP * T, f16), 2 * GRP)
        GB = [v3(r.take(GT * GRP * NT), GT) for _ in range(2)]
        act_s = v3(r.take(2 * T), 2)
        at_s = v3(r.take(2 * T), 2)

        r = Region(FREE)
        ph_, pl_ = v3(r.take(KC * T, f16), KC), v3(r.take(KC * T, f16), KC)
        yh, yl = v3(r.take(KC * T, f16), KC), v3(r.take(KC * T, f16), KC)
        V2 = v3(r.take(KC * T), KC)
        U2 = v3(r.take(KC * T), KC)
        t2 = r.at
        zp = [r.take(T + 16) for _ in range(2)]
        win = [r.take(T + 16) for _ in range(2)]
        gat = v3(Region(t2).take(2 * T), 2)
        wsT = r.take(D)
        bsp = r.take(D)
        mtmp = v3(r.take(2 * T), 2)
        assert r.at <= WORDS - 5300
        r = Region(FREE)
        ggh, ggl = v3(r.take(FC * T, f16), FC), v3(r.take(FC * T, f16), FC)
        upb = [r.take(T + 2) for _ in range(4)]
        cv = v3(r.take(6 * T), 6)
        prw = v3(r.take(2 * T), 2)
        pth, ptl = v3(r.take(2 * T, f16), 2), v3(r.take(2 * T, f16), 2)
        assert r.at <= WORDS - 5300
        r = Region(FREE)
        pgs = v3(r.take(KC * T), KC)
        yout = v3(r.take(KC * T), KC)
        ptmp = v3(r.take(2 * T), 2)

        consts_in, vecs_in, x_in = sem("consts_in"), sem("vecs_in"), sem("x_in")
        slab_in = [sem(f"slab_in{i}") for i in range(SLOTS)]
        high_cut, low_cut, slab_done = sem("high_cut"), sem("low_cut"), sem("slab_done")
        vslab_in = [sem(f"vslab_in{i}") for i in range(SLOTS)]
        vhigh_cut, vlow_cut, vslab_done = sem("vhigh_cut"), sem("vlow_cut"), sem("vslab_done")
        wz_high, wz_low = sem("wz_high"), sem("wz_low")
        dve_step, act_step, pool_step = sem("dve_step"), sem("act_step"), sem("pool_step")

        def slot(n):
            return n % SLOTS

        gmat = nc.dram_tensor("gate_matrix", [GT, P, NK * NT], f32, kind="Internal").ap()

        class Chain:

            def __init__(self, eng, s):
                self.eng, self.s, self.n, self.off = eng, s, 0, 0

            def link(self, ins):
                ins.then_inc(self.s, 1)
                self.n += 1
                self.eng.wait_ge(self.s, self.off + self.n)

            def enter(self, off):
                self.off, self.first = off, self.n

            def leave(self, per, times):
                assert self.n - self.first == per, (self.n - self.first, per)
                self.n, self.off = self.first + per * times, 0

        dchain = Chain(None, dve_step)

        sq_act, sq_dve, ss_done, std_done = sem("sq_act"), sem("sq_dve"), sem("ss_done"), sem("std_done")
        xn_done, xh_done, xl_done = sem("xn_done"), sem("xh_done"), sem("xl_done")
        NORMS = ("ln1", "ln2", "final1", "mixn", "ffnn", "plen", "final2")

        class Norm:

            def __init__(self, name):
                self.i = NORMS.index(name)
                self.w, self.meta = VEC[name], name == "ln1"
                self.cut = name not in ("final1", "final2")
                self.nth = sum(n not in ("final1", "final2") for n in NORMS[:self.i])
                self.cols = TM if self.meta else T
                self.sq = nsq1 if self.meta else nsq
                self.std = nstd1 if self.meta else nstd
                self.inv = ninv1 if self.meta else ninv

            def act(self, act, ready):
                h = KC // 2
                ready()
                for c in range(0, KC, 2):
                    nc.scalar.activation(self.sq[:, c, 0:self.cols], X[:, c, 0:self.cols],
                                         ACT.Square).then_inc(sq_act, 1)
                act.wait_ge(ss_done, self.i + 1)
                nc.scalar.activation(self.std[:, 0:self.cols], psum[:, 0:self.cols], ACT.Sqrt, bias=EPSC,
                                     scale=1.0 / D).then_inc(std_done, 1)
                if self.cut:
                    for c in range(KC):
                        act.wait_ge(xn_done, self.nth * KC + c + 1)
                        nc.scalar.activation(xh[:, c, 0:self.cols], self.sq[:, c, 0:self.cols],
                                             ACT.Copy).then_inc(xh_done, 1)

            def pe(self, pe):
                for c in range(KC):
                    if c % 2 == 0:
                        pe.wait_ge(sq_act, self.i * KC // 2 + c // 2 + 1)
                    else:
                        pe.wait_ge(sq_dve, self.i * KC // 2 + c // 2 + 1)
                    last = nc.tensor.matmul(bank(0), ones, self.sq[:, c, 0:T], start=c == 0, stop=c == KC - 1)
                    if self.meta:
                        last = nc.tensor.matmul(bank(1, M), ones, self.sq[:, c, T:TM], start=c == 0,
                                                stop=c == KC - 1)
                last.then_inc(ss_done, 1)

            def dve(self, dve, dst=None, done=None):
                for c in range(1, KC, 2):
                    nc.vector.tensor_tensor(self.sq[:, c, 0:self.cols], X[:, c, 0:self.cols],
                                            X[:, c, 0:self.cols], ALU.mult).then_inc(sq_dve, 1)
                dve.wait_ge(std_done, self.i + 1)
                dchain.link(nc.vector.reciprocal(self.inv[:, 0:self.cols], self.std[:, 0:self.cols]))
                for c in range(KC):
                    o = dst[:, c, 0:T] if dst is not None else self.sq[:, c, 0:self.cols]
                    ins = nc.vector.scalar_tensor_tensor(
                        out=o, in0=X[:, c, 0:self.cols], scalar=vec[:, self.w + c:self.w + c + 1],
                        in1=self.inv[:, 0:self.cols], op0=ALU.mult, op1=ALU.mult)
                    if self.cut:
                        ins.then_inc(xn_done, 1)
                    elif done is not None:
                        ins.then_inc(done, 1)
                    else:
                        dchain.link(ins)
                if self.cut:
                    for c in range(KC):
                        dve.wait_ge(xh_done, self.nth * KC + c + 1)
                        nc.vector.tensor_tensor(xl[:, c, 0:self.cols], self.sq[:, c, 0:self.cols],
                                                xh[:, c, 0:self.cols], ALU.subtract).then_inc(xl_done, 1)

            def wait_cut(self, pe):
                pe.wait_ge(xl_done, (self.nth + 1) * KC)

        EPSC = small[:, 0:1]
        NLAM = small[:, 1:2]
        SUBW = small[:, 2:3]
        LAMP = small[:, 4:6]
        LAME = small[:, 6:8]
        nmx = small[:, 8:12]
        zs = small[:, 12:16]
        rzs = small[:, 16:24]
        vss = small[:, 24:32]
        vrs = small[:, 32:40]
        one = ones[:, 0:1]

        def wait(eng, s, v):
            if not isinstance(v, int) or v > 0:
                eng.wait_ge(s, v)

        def cut_high(act, g, s):
            act.wait_ge(slab_in[s], g * 16 + 16)
            wait(act, slab_done, g * SLOTS + (s + 1 - SLOTS))
            nc.scalar.activation(wh[:, s, :], wraw[:, s, :], ACT.Copy, scale=WS).then_inc(high_cut, 1)

        def cut_low(dve, g, s):
            dve.wait_ge(high_cut, g * SLOTS + (s + 1))
            nc.vector.scalar_tensor_tensor(out=wl[:, s, :], in0=wraw[:, s, :], scalar=WS, in1=wh[:, s, :],
                                           op0=ALU.mult, op1=ALU.subtract).then_inc(low_cut, 1)

        class Cuts:

            def __init__(self, eng, cut):
                self.eng, self.cut, self.n = eng, cut, 0

            def upto(self, n):
                while self.n <= min(n, N_END - 1):
                    self.cut(self.eng, self.n // SLOTS, slot(self.n))
                    self.n += 1

            def ahead(self, g, s):
                s += SLOTS - 1
                self.cut(self.eng, g + s // SLOTS, s % SLOTS)

        def parts(ps, a_h, a_l, b_h, b_l, first, last):
            nc.tensor.matmul(ps, a_h, b_h, start=first, stop=False)
            nc.tensor.matmul(ps, a_h, b_l, start=False, stop=False)
            return nc.tensor.matmul(ps, a_l, b_h, start=False, stop=last)

        def wslab(sl, c, n=P):
            return wh[:, sl, c * n:(c + 1) * n], wl[:, sl, c * n:(c + 1) * n]

        def chunk(pe, n, sl, ps, sh=None, slo=None, kc=KC, meta=None):
            sh = xh if sh is None else sh
            slo = xl if slo is None else slo
            pe.wait_ge(low_cut, n + 1)
            for c in range(kc):
                a = wslab(sl, c)
                last = parts(ps, *a, sh[:, c, 0:T], slo[:, c, 0:T], c == 0, c == kc - 1)
                if meta is not None:
                    last = parts(meta, *a, sh[:, c, T:TM], slo[:, c, T:TM], c == 0, c == kc - 1)
            last.then_inc(slab_done, 1)

        proj_out, proj_meta_out = sem("proj_out"), sem("proj_meta_out")
        rope_in, rope_mul, rope_out = sem("rope_in"), sem("rope_mul"), sem("rope_out")
        values_out = sem("values_out")
        z_done, z_out, gate_mm, gate_abs, gate_pre, gate_ln, gate_out = (
            sem("z_done"), sem("z_out"), sem("gate_mm"), sem("gate_abs"), sem("gate_pre"), sem("gate_ln"),
            sem("gate_out"))
        sig_out, silu_out = sem("sig_out"), sem("silu_out")
        lam_prod, lam_sum, lam_exp, lam_out = sem("lam_prod"), sem("lam_sum"), sem("lam_exp"), sem("lam_out")
        score_done, max_done, exp_done, diff_done = (sem("score_done"), sem("max_done"), sem("exp_done"),
                                                     sem("diff_done"))
        turn_done, turn_out, av_done, av_out = sem("turn_done"), sem("turn_out"), sem("av_done"), sem("av_out")
        osq_out, oss_done, ostd_out, mixh_out, mixl_out = (sem("osq_out"), sem("oss_done"), sem("ostd_out"),
                                                           sem("mixh_out"), sem("mixl_out"))
        zeroed, e_in, e_exp, kt_out, qt_out, lev_done, lev_out = (
            sem("zeroed"), sem("e_in"), sem("e_exp"), sem("kt_out"), sem("qt_out"), sem("lev_done"),
            sem("lev_out"))
        em_in, em_exp, ktm_out, wide_done, wide_out, gav_done, gav_out = (
            sem("em_in"), sem("em_exp"), sem("ktm_out"), sem("wide_done"), sem("wide_out"), sem("gav_done"),
            sem("gav_out"))
        res_out = sem("res_out")
        NL = len(LEVELS)
        NS = len(SMALL)
        keys_in, pq_out, s_done, s_out, head_done, gsub_out, gexp_out = (
            sem("keys_in"), sem("pq_out"), sem("s_done"), sem("s_out"), sem("head_done"), sem("gsub_out"),
            sem("gexp_out"))
        idx_turned, idxT_out = sem("idx_turned"), sem("idxT_out")
        hot_out, g_done, g_out = sem("hot_out"), sem("g_done"), sem("g_out")
        g_stored, g_in = [sem(f"g_stored{i}") for i in range(2)], [sem(f"g_in{i}") for i in range(2)]
        gelu_out, gated_out, a_cut, b_done, acc_out = (sem("gelu_out"), sem("gated_out"), sem("a_cut"),
                                                       sem("b_done"), sem("acc_out"))
        final1_out = sem("final1_out")
        pads, small_in, masked = sem("pads"), sem("small_in"), sem("masked")
        zpool_out, pool_cut, y_cut = sem("zpool_out"), sem("pool_cut"), sem("y_cut")
        v_out, vsq_out, vsum_out, vstd_out, v_normed = (sem("v_out"), sem("vsq_out"), sem("vsum_out"),
                                                        sem("vstd_out"), sem("v_normed"))
        u_out, mix_done, mix_read, sgu_cut = sem("u_out"), sem("mix_done"), sem("mix_read"), sem("sgu_cut")
        gsig_out, branch_out, m_cut, res2_out = (sem("gsig_out"), sem("branch_out"), sem("m_cut"),
                                                 sem("res2_out"))
        up_out, conv_out, cgelu_out, ffn_cut = (sem("up_out"), sem("conv_out"),
                                                           sem("cgelu_out"), sem("ffn_cut"))
        down_out, p_in, p_high, p_low = (sem("down_out"), sem("p_in"),
                                                    sem("p_high"), sem("p_low"))
        psig_out, ple_done, ple_out, y_out, stored = (sem("psig_out"), sem("ple_done"), sem("ple_out"),
                                                      sem("y_out"), sem("stored"))

        block = ctx.enter_context(nc.Block())

        @block.sync
        def _(sp):
            sp.dma_start(X[:, :, 0:T], io["xT"]).then_inc(x_in, 16)
            sp.dma_start(X[:, :, T:TM], io["metaT"]).then_inc(x_in, 16)
            sp.dma_start(ones, io["ones"]).then_inc(x_in, 16)
            sp.dma_start(vec, io["vec"]).then_inc(vecs_in, 16)
            for s in range(SLOTS):
                sp.dma_start(wraw[:, s, :], io["w"][s]).then_inc(slab_in[s], 16)
            for dst, name in ((ident, "ident"), (iota, "iota"), (perm, "perm"), (masks, "masks"), (ropec, "ropec"),
                              (ropes, "ropes"), (icnt, "icnt"), (io16, "io16"), (w2[0:32], "w2"), (wz, "wz")):
                sp.dma_start(dst, io[name]).then_inc(consts_in, 16)

            def slabs(lo, hi):
                with sp.Fori(lo // SLOTS, hi // SLOTS) as g:
                    for s in range(SLOTS):
                        sp.wait_ge(low_cut, g * SLOTS + (s + 1 - SLOTS))
                        sp.dma_start(wraw[:, s, :], io["w"][bass.ds(g * SLOTS + s, 1)].rearrange(
                            "a p n -> p (a n)")).then_inc(slab_in[s], 16)

            slabs(SLOTS, N_PQ + SLOTS)
            sp.wait_ge(res_out, KC)
            sp.dma_start(keysT, io["keysT"]).then_inc(keys_in, 16)
            slabs(N_PQ + SLOTS, N_U + SLOTS)
            def store_gates(tile, par):
                sp.wait_ge(g_out, tile * 16 + 16)
                sp.dma_start(gmat[bass.ds(tile, 1)].rearrange("a p n -> p (a n)"),
                             G[par].rearrange("p i n -> p (i n)")).then_inc(g_stored[par], 16)

            for s in range(GRP):
                sp.dma_start(vraw[:, s, :], io["v"][s]).then_inc(vslab_in[s], 16)
            with sp.Fori(0, GT // 2) as o:
                store_gates(o * 2, 0)
                store_gates(o * 2 + 1, 1)
            sp.wait_ge(g_stored[0], GT // 2 * 16)
            sp.wait_ge(g_stored[1], GT // 2 * 16)
            def load_gates(g, par):
                wait(sp, gated_out, (g - 1) * GRP)
                sp.dma_start(GB[par], gmat[:, :, bass.ds(g * (GRP * NT), GRP * NT)].rearrange(
                    "t p n -> p t n")).then_inc(g_in[par], 16)

            def load_group(g, par):
                load_gates(g, par)
                for s in range(GRP):
                    if not isinstance(g, int) or g > 0:
                        sp.wait_ge(vlow_cut, g * GRP + (s + 1 - GRP))
                        sp.dma_start(vraw[:, s, :], io["v"][bass.ds(g * GRP + s, 1)].rearrange(
                            "a p n -> p (a n)")).then_inc(vslab_in[s], 16)
                    n = g * GRP + (N_U + GRP + s)
                    sp.wait_ge(low_cut, n - (SLOTS - 1))
                    sp.dma_start(wraw[:, s, :], io["w"][bass.ds(n, 1)].rearrange(
                        "a p n -> p (a n)")).then_inc(slab_in[s], 16)

            load_group(0, 0)
            load_group(1, 1)
            with sp.Fori(1, GROUPS // 2) as o:
                load_group(o * 2, 0)
                load_group(o * 2 + 1, 1)
            sp.wait_ge(acc_out, GROUPS * KC)
            sp.wait_ge(final1_out, KC)
            sp.dma_start(wsT, io["wsT"]).then_inc(small_in, 16)
            sp.dma_start(bsp, io["bsp"].partition_broadcast(P)).then_inc(small_in, 16)
            slabs(N_POOL + SLOTS, N_UP + SLOTS)
            sp.wait_ge(res2_out, KC)
            sp.dma_start(prw, io["pT"]).then_inc(p_in, 16)
            slabs(N_UP + SLOTS, N_END)
            for c in range(KC):
                sp.wait_ge(y_out, c + 1)
                sp.dma_start(out[:, c, :], yout[:, c, :]).then_inc(stored, 16)
            sp.wait_ge(stored, 16 * KC)

        @block.tensor
        def _(pe):
            pe.wait_ge(x_in, 48)
            n1 = Norm("ln1")
            n1.pe(pe)
            pe.wait_ge(lam_prod, 1)
            nc.tensor.matmul(bank(2, 2), ones[0:DH, :], LAMP[0:DH, :], start=True, stop=True).then_inc(lam_sum, 1)
            pe.wait_ge(consts_in, 160)
            n1.wait_cut(pe)
            pe.wait_ge(std_done, 1)
            pe.wait_ge(lam_exp, 1)
            def rope_swap(n):
                pe.wait_ge(rope_in, n + 1)
                src = q[:, n, :] if n < HEADS else k[:, n - HEADS, 0:T]
                if n >= 1:
                    pe.wait_ge(rope_mul, n)
                last = nc.tensor.matmul(bank(6), perm, src, start=True, stop=True)
                if n >= HEADS:
                    last = nc.tensor.matmul(bank(7, M), perm, k[:, n - HEADS, T:TM], start=True, stop=True)
                last.then_inc(rope_out, 1)

            for n in range(N_Q, N_V):
                if n >= 4:
                    pe.wait_ge(rope_in, n - 3 if n < 6 else n - 1)
                chunk(pe, n, slot(n), bank(n % 4), meta=bank(4 + n % 2, M) if n >= N_K else None)
                if n >= 1:
                    rope_swap(n - 1)
            rope_swap(N_V - 1)
            for part in range(2):
                if part == 0:
                    pe.wait_ge(rope_in, 8)
                else:
                    pe.wait_ge(values_out, 5)
                for g in range(4):
                    n = N_V + 4 * part + g
                    pe.wait_ge(low_cut, n + 1)
                    for c in range(2):
                        w_h, w_l = wslab(slot(n), c, 512)
                        for t in range(5):
                            cols = slice(t * P, (t + 1) * P) if t < TT else slice(T, TM)
                            last = parts(psum[0:P if t < TT else M, t * 512:(t + 1) * 512],
                                         xh[:, 2 * g + c, cols], xl[:, 2 * g + c, cols], w_h, w_l,
                                         g == 0 and c == 0, g == 3 and c == 1)
                    last.then_inc(slab_done, 1)
            pe.wait_ge(values_out, 10)
            for n in range(N_GQ, N_GR):
                chunk(pe, n, slot(n), bank(n % 4), meta=bank(4 + n % 2, M) if n >= N_GK else None)
            pe.wait_ge(wz_low, 1)
            for c in range(KC):
                a = wzh[:, c, :], wzl[:, c, :]
                parts(psum[0:32, 6 * 512:7 * 512], *a, xh[:, c, 0:T], xl[:, c, 0:T], c == 0, c == KC - 1)
                last = parts(psum[0:32, 7 * 512:7 * 512 + M], *a, xh[:, c, T:TM], xl[:, c, T:TM], c == 0,
                             c == KC - 1)
            last.then_inc(z_done, 1)
            pe.wait_ge(proj_out, 4)
            for n in range(N_GR, N_WO):
                chunk(pe, n, slot(n), bank(n % 4))
            pe.wait_ge(z_out, 1)
            for h in range(HEADS):
                if h == 0:
                    pe.wait_ge(z_out, 2)
                if h >= 1:
                    pe.wait_ge(gate_mm, h)
                nc.tensor.matmul(bank(4), w2[0:32, h, :], z32[0:32, 0:T], start=True, stop=True)
                nc.tensor.matmul(bank(5, M), w2[0:32, h, :], z32[0:32, T:TM], start=True,
                                 stop=True).then_inc(gate_abs, 1)

            def scores(turn):
                h, t = divmod(turn, TT)
                for c in range(2):
                    u = 2 * turn + c
                    if u >= 2:
                        pe.wait_ge(exp_done, u - 1)
                    rows = slice(DH * c, DH * (c + 1))
                    a = q[rows, h, t * P:(t + 1) * P]
                    nc.tensor.matmul(bank(2 * c), a, k[rows, h, 0:T], start=True, stop=True)
                    nc.tensor.matmul(bank(2 * c + 1, M), a, k[rows, h, T:TM], start=True,
                                     stop=True).then_inc(score_done, 1)

            def turn_over(turn):
                par = turn % 2
                pe.wait_ge(diff_done, turn + 1)
                if turn >= 2:
                    pe.wait_ge(turn_out, turn - 1)
                for j in range(TT):
                    nc.tensor.transpose(bank(4 + par, P, j * P), pa[:, par, j * P:(j + 1) * P], ident)
                if turn >= 1:
                    pe.wait_ge(turn_out, turn)
                nc.tensor.transpose(psum[0:M, 6 * 512 + par * P:6 * 512 + (par + 1) * P],
                                    pa[:, par, T:TM], ident).then_inc(turn_done, 1)

            def mix_values(h):
                pe.wait_ge(turn_out, TT * (h + 1))
                if h >= 1:
                    pe.wait_ge(av_out, h)
                cols = slice(h * P, (h + 1) * P)
                for j in range(TT):
                    nc.tensor.matmul(bank(7), dv[:, j, cols], aT[:, j, :], start=j == 0, stop=False)
                nc.tensor.matmul(bank(7), dv[0:M, TT, cols], aT[0:M, TT, :], start=False,
                                 stop=True).then_inc(av_done, 1)

            pe.wait_ge(silu_out, HEADS)
            pe.wait_ge(gate_out, HEADS)
            for turn in range(HEADS * TT):
                scores(turn)
                if turn >= 1:
                    turn_over(turn - 1)
                    if turn % TT == 0:
                        mix_values(turn // TT - 1)
            turn_over(HEADS * TT - 1)
            mix_values(HEADS - 1)
            for h in range(HEADS):
                pe.wait_ge(osq_out, h + 1)
                nc.tensor.matmul(bank(h), ones, aT[:, h, :], start=True, stop=True).then_inc(oss_done, 1)

            units = [(h, li) for h in range(HEADS) for li in range(-1, NS + 1)]
            for u, (h, li) in enumerate(units):
                b = 4 + u % 3
                if u >= 3:
                    pe.wait_ge(lev_out, u - 2)
                if u == 0:
                    pe.wait_ge(av_out, HEADS)
                    pe.wait_ge(turn_out, HEADS * TT)
                if li >= 0:
                    pe.wait_ge(kt_out, 2 * (h * NL + li + 1))
                    pe.wait_ge(qt_out, 2 * (h * NL + li + 1))
                for j in range(TT):
                    jt = slice(j * P, (j + 1) * P)
                    i = j if li < NS else j ^ 1
                    it = slice(i * P, (i + 1) * P)
                    if li < 0:
                        last = nc.tensor.matmul(bank(b, P, j * P), gk[:, h, jt], gq[:, h, it], start=True,
                                                stop=True)
                    else:
                        last = nc.tensor.matmul(bank(b, P, j * P), KT[:, li, jt], QT[:, li, it], start=True,
                                                stop=True)
                last.then_inc(lev_done, 1)
                if li == NS:
                    pe.wait_ge(kt_out, 2 * (h * NL + NL))
                    pe.wait_ge(qt_out, 2 * (h * NL + NL))
                    if h == 0:
                        pe.wait_ge(ostd_out, HEADS)
                    else:
                        pe.wait_ge(wide_out, 3 * h)
                    for j in range(TT):
                        off = T // 2 if j < 2 else 0
                        last = nc.tensor.matmul(bank(j // 2, 256, 256 * (j % 2)),
                                                KT[:, NL - 1, j * P:(j + 1) * P],
                                                QT[:, NL - 1, off:off + 256], start=True, stop=True)
                    pe.wait_ge(ktm_out, 2 * (h + 1))
                    nc.tensor.matmul(psum[0:M, 2 * 512:3 * 512], KTm[0:DH, :], QTm[0:DH, :], start=True,
                                     stop=True).then_inc(wide_done, 1)
                    pe.wait_ge(lev_out, u + 1)
                    pe.wait_ge(wide_out, 3 * (h + 1))
                    if h >= 1:
                        pe.wait_ge(gav_out, h)
                    cols = slice(h * P, (h + 1) * P)
                    for j in range(TT):
                        nc.tensor.matmul(bank(3), gv[:, j, cols], A[:, j, :], start=j == 0, stop=False)
                    nc.tensor.matmul(bank(3), gv[0:M, TT, cols], Am[0:M, :], start=False,
                                     stop=True).then_inc(gav_done, 1)
            for h in range(HEADS):
                pe.wait_ge(osq_out, HEADS + h + 1)
                if h == 3:
                    pe.wait_ge(gav_out, HEADS)
                nc.tensor.matmul(bank(h), ones, A[:, h, :], start=True, stop=True).then_inc(oss_done, 1)

            pe.wait_ge(mixl_out, 2)
            pe.wait_ge(ostd_out, 2 * HEADS)
            for n in range(N_WO, N_PQ):
                i = n - N_WO
                if i >= 4:
                    pe.wait_ge(res_out, i - 3)
                chunk(pe, n, slot(n), bank(n % 4))

            n2 = Norm("ln2")
            n2.pe(pe)
            n2.wait_cut(pe)
            pe.wait_ge(std_done, 2)
            pe.wait_ge(keys_in, 16)

            def key_scores(m, side):
                pe.wait_ge(pq_out, m + 1)
                wait(pe, s_out, m - 1)
                for t in range(TT):
                    last = nc.tensor.matmul(bank(2 + side, P, t * P), pq[:, side, t * P:(t + 1) * P],
                                            keysT[:, bass.ds(m, 1), :].rearrange("p a n -> p (a n)"),
                                            start=True, stop=True)
                last.then_inc(s_done, 1)

            def query_turn(i):
                for kk in range(SLOTS):
                    m = i * SLOTS + kk
                    wait(pe, pq_out, m - 1)
                    chunk(pe, m + N_PQ, kk, bank(kk % 2))
                    if kk:
                        key_scores(m - 1, (kk - 1) % 2)
                key_scores(m, 1)

            query_turn(0)
            with pe.Fori(1, PH // 2) as i:
                query_turn(i)

            pe.wait_ge(head_done, PH)
            for v in range(3):
                for t in range(TT):
                    last = nc.tensor.transpose(bank(4 + v, P, t * P), idx_tok[:, v, t * P:(t + 1) * P], ident)
                last.then_inc(idx_turned, 1)

            def gate_octet(e):
                for tk in range(8):
                    pe.wait_ge(hot_out, e * 8 + (tk + 1))
                    if tk % 4 == 0:
                        wait(pe, g_out, e * 2 + (tk // 4 - 1))
                    nc.tensor.matmul(bank(tk // 4, P, tk % 4 * P), hot[:, 2 * tk, :], hot[:, 2 * tk + 1, :],
                                     start=True, stop=True).then_inc(g_done, 1)

            pe.wait_ge(s_out, 2 * PH)
            gate_octet(0)
            with pe.Fori(1, T // 8) as e:
                gate_octet(e)

            pe.wait_ge(g_out, T // 4)

            def expert_group(g, par, inputs=True, outputs=True):
                gp, pp = g - 1, 1 - par
                for s in range(GRP):
                    if inputs:
                        wait(pe, gelu_out, g * GRP + (s - 1))
                        chunk(pe, g * GRP + (N_U + s), s, bank(s % 2))
                    if outputs:
                        if s == 0:
                            pe.wait_ge(a_cut, gp * GRP + GRP)
                            pe.wait_ge(vlow_cut, gp * GRP + GRP)
                        for c in (2 * s, 2 * s + 1):
                            wait(pe, acc_out, gp * KC + (c - 3))
                            for t in range(GRP):
                                x = pp * GRP + t
                                cols = slice(c * P, (c + 1) * P)
                                last = parts(bank(2 + c % 4), vh[:, x, cols], vl[:, x, cols], Ah[:, x, :],
                                             Al[:, x, :], t == 0, t == GRP - 1)
                            last.then_inc(b_done, 1)

            expert_group(0, 0, outputs=False)
            expert_group(1, 1)
            expert_group(2, 0)
            with pe.Fori(1, GROUPS // 2 - 1) as o:
                expert_group(o * 2 + 1, 1)
                expert_group(o * 2 + 2, 0)
            expert_group(GROUPS - 1, 1)
            expert_group(GROUPS, 0, inputs=False)
            Norm("final1").pe(pe)

            n4 = Norm("mixn")
            n4.pe(pe)
            n4.wait_cut(pe)
            pe.wait_ge(std_done, n4.i + 1)
            for n in range(N_POOL, N_WP):
                wait(pe, zpool_out, n - N_POOL - 3)
                chunk(pe, n, slot(n), bank(n % 4))
            pe.wait_ge(zpool_out, KC)
            for n in range(N_WP, N_SV):
                g = n - N_WP
                pe.wait_ge(low_cut, n + 1)
                pe.wait_ge(pool_cut, 2 * g + 2)
                for o in range(2):
                    c = 2 * g + o
                    wait(pe, y_cut, c - 3)
                    for kk in range(2):
                        last = parts(bank(c % 4), *wslab(slot(n), 2 * o + kk), ph_[:, 2 * g + kk, :],
                                     pl_[:, 2 * g + kk, :], kk == 0, kk == 1)
                last.then_inc(slab_done, 1)
            for half in range(2):
                if half == 0:
                    pe.wait_ge(y_cut, KC)
                for g in range(4):
                    n = N_SV + 4 * half + g
                    pe.wait_ge(low_cut, n + 1)
                    for c in range(2):
                        w_h, w_l = wslab(slot(n), c, 512)
                        for t in range(TT):
                            cols = slice(t * P, (t + 1) * P)
                            last = parts(bank(4 * half + t), xh[:, 2 * g + c, cols], xl[:, 2 * g + c, cols],
                                         w_h, w_l, g == 0 and c == 0, g == 3 and c == 1)
                    last.then_inc(slab_done, 1)
            pe.wait_ge(v_out, 2 * TT)
            for n in range(N_SU, N_GA):
                h = n - N_SU
                wait(pe, u_out, h - 3)
                chunk(pe, n, slot(n), bank(n % 4))
                if h == 0:
                    pe.wait_ge(masked, 1)
                    pe.wait_ge(v_normed, TT)
                wait(pe, mix_read, h - 1)
                for t in range(TT):
                    last = nc.tensor.matmul(bank(4 + h % 2, P, t * P),
                                            V2[:, 2 * t + h // 4, h % 4 * P:(h % 4 + 1) * P],
                                            wsT[:, h * P:(h + 1) * P], start=True, stop=True)
                last.then_inc(mix_done, 1)
            pe.wait_ge(u_out, KC)
            for n in range(N_GA, N_WO2):
                i = n - N_GA
                b = i // 2
                if i % 2 == 0:
                    wait(pe, gsig_out, b - 1)
                    chunk(pe, n, slot(n), bank(n % 4))
                else:
                    if b == KC:
                        pe.wait_ge(sgu_cut, KC)
                    wait(pe, branch_out, b - 1)
                    a = (yh, yl) if b < KC else (ph_, pl_)
                    chunk(pe, n, slot(n), bank(n % 4), *a)
            pe.wait_ge(branch_out, 2 * KC)
            pe.wait_ge(m_cut, KC)
            for n in range(N_WO2, N_UP):
                wait(pe, res2_out, n - N_WO2 - 3)
                chunk(pe, n, slot(n), bank(n % 4), yh, yl)

            n5 = Norm("ffnn")
            n5.pe(pe)
            n5.wait_cut(pe)
            pe.wait_ge(std_done, n5.i + 1)

            def up_turn(i):
                for s in range(SLOTS):
                    wait(pe, up_out, i * SLOTS + (s - 3))
                    chunk(pe, i * SLOTS + (N_UP + s), s, bank(s))

            up_turn(0)
            with pe.Fori(1, FC // 2) as i:
                up_turn(i)

            def down(f, s, first=False, last=False):
                pe.wait_ge(low_cut, f + (N_DN + 1))
                fi = bass.ds(f, 1)
                b_h, b_l = (x[:, fi, :].rearrange("p a n -> p (a n)") for x in (ggh, ggl))
                for c in range(KC):
                    ins = parts(bank(c), *wslab(s, c), b_h, b_l, first, last)
                ins.then_inc(slab_done, 1)

            pe.wait_ge(up_out, 2 * FC)
            pe.wait_ge(ffn_cut, FC)
            for f in range(SLOTS):
                down(f, f, first=f == 0)
            with pe.Fori(1, FC // SLOTS) as i:
                for s in range(SLOTS):
                    down(i * SLOTS + s, s)
            for f in range(FC // SLOTS * SLOTS, FC):
                down(f, f % SLOTS, last=f == FC - 1)

            n6 = Norm("plen")
            n6.pe(pe)
            n6.wait_cut(pe)
            pe.wait_ge(std_done, n6.i + 1)
            pe.wait_ge(p_low, 1)
            for n in range(N_PG, N_PP):
                wait(pe, psig_out, n - N_PG - 3)
                chunk(pe, n, slot(n), bank(n % 4))
            for n in range(N_PP, N_END):
                pe.wait_ge(low_cut, n + 1)
                for o in range(4):
                    c = 4 * (n - N_PP) + o
                    wait(pe, ple_out, c - 3)
                    for kk in range(2):
                        last = parts(bank(4 + c % 4), *wslab(slot(n), 2 * o + kk), pth[:, kk, :],
                                     ptl[:, kk, :], kk == 0, kk == 1)
                    last.then_inc(ple_done, 1)
            Norm("final2").pe(pe)

        @block.scalar
        def _(act):
            chain = Chain(act, act_step)
            cuts = Cuts(act, cut_high)
            act.wait_ge(pool_step, 1)
            n1 = Norm("ln1")
            act.wait_ge(x_in, 48)
            n1.act(act, lambda: None)
            act.wait_ge(lam_sum, 1)
            nc.scalar.activation(LAME, bank(2, 2), ACT.Exp).then_inc(lam_exp, 1)
            cuts.upto(2)
            for n in range(N_Q, N_V):
                cuts.upto(n + 3)
                act.wait_ge(slab_done, n + 1)
                if n < N_K:
                    nc.scalar.activation(q[:, n, :], bank(n % 4), ACT.Copy, scale=ISW / 8).then_inc(rope_in, 1)
                else:
                    nc.scalar.activation(k[:, n - N_K, T:TM], bank(4 + n % 2, M), ACT.Copy, scale=ISW)
                    nc.scalar.activation(k[:, n - N_K, 0:T], bank(n % 4), ACT.Copy, scale=ISW).then_inc(rope_in, 1)
            act.wait_ge(consts_in, 160)
            nc.scalar.activation(wzh.rearrange("p a b -> p (a b)"), wz, ACT.Copy, scale=WS).then_inc(wz_high, 1)
            for part in range(2):
                cuts.upto(N_V + 4 * part + 7)
                act.wait_ge(slab_done, N_V + 4 * part + 4)
                dst = (dv, gv)[part]
                for t in range(5):
                    rows = P if t < TT else M
                    nc.scalar.activation(dst[0:rows, t, :], psum[0:rows, t * 512:(t + 1) * 512], ACT.Copy,
                                         scale=ISW).then_inc(values_out, 1)
            for n in range(N_GQ, N_GR):
                cuts.upto(n + 3)
                act.wait_ge(slab_done, n + 1)
                for c in range(2):
                    rows = slice(DH * c, DH * (c + 1))
                    for half in range(2):
                        d = slice(DH * half, DH * (half + 1))
                        if n < N_GK:
                            last = nc.scalar.activation(gq[d, 2 * (n - N_GQ) + c, :],
                                                        psum[rows, (n % 4) * 512:(n % 4 + 1) * 512], ACT.Copy,
                                                        scale=ISW / 8)
                        else:
                            h = 2 * (n - N_GK) + c
                            nc.scalar.activation(gk[d, h, T:TM],
                                                 bank(4 + n % 2, M)[rows],
                                                 ACT.Copy, scale=ISW)
                            last = nc.scalar.activation(gk[d, h, 0:T],
                                                        psum[rows, (n % 4) * 512:(n % 4 + 1) * 512], ACT.Copy,
                                                        scale=ISW)
                last.then_inc(proj_out, 1)
            act.wait_ge(z_done, 1)
            nc.scalar.activation(z32[0:32, 0:T], psum[0:32, 6 * 512:7 * 512], ACT.Copy, scale=ISW).then_inc(z_out, 1)
            nc.scalar.activation(z32[0:32, T:TM], psum[0:32, 7 * 512:7 * 512 + M], ACT.Copy,
                                 scale=ISW).then_inc(z_out, 1)
            for n in range(N_GR, N_WO):
                cuts.upto(n + 3)
                act.wait_ge(slab_done, n + 1)
                nc.scalar.activation(sgr[:, n - N_GR, :], bank(n % 4), ACT.Sigmoid, scale=ISW).then_inc(sig_out, 1)
            for h in range(HEADS):
                act.wait_ge(gate_abs, h + 1)
                bcol = vec[:, VEC["gateb"] + h:VEC["gateb"] + h + 1]
                nc.scalar.activation(B[:, h, 0:T], bank(4), ACT.Identity, bias=bcol)
                nc.scalar.activation(B[:, h, T:TM], bank(5, M), ACT.Identity, bias=bcol).then_inc(gate_mm, 1)
            act.wait_ge(gate_mm, HEADS)
            chain.link(nc.scalar.activation(gtmp, B, ACT.Abs))
            chain.link(nc.scalar.activation(gtmp, gtmp, ACT.Exp, scale=-1.0))
            nc.scalar.activation(gtmp, gtmp, ACT.Ln, bias=one).then_inc(gate_ln, 1)

            def turn_copy(turn):
                par, (h, t) = turn % 2, divmod(turn, TT)
                act.wait_ge(turn_done, turn + 1)
                if h >= 1 and t == 0:
                    act.wait_ge(av_done, h)
                nc.scalar.activation(aT[:, 0:TT, t * P:(t + 1) * P], v3(bank(4 + par), TT), ACT.Copy)
                nc.scalar.activation(aT[0:M, TT, t * P:(t + 1) * P],
                                     psum[0:M, 6 * 512 + par * P:6 * 512 + (par + 1) * P],
                                     ACT.Copy).then_inc(turn_out, 1)

            def head_out(h):
                act.wait_ge(av_done, h + 1)
                nc.scalar.activation(otmp[:, h, :], bank(7), ACT.Copy).then_inc(av_out, 1)

            for turn in range(HEADS * TT):
                for c in range(2):
                    u = 2 * turn + c
                    act.wait_ge(max_done, u + 1)
                    if turn >= 2:
                        act.wait_ge(diff_done, turn - 1)
                    nc.scalar.activation(pr[:, u % 4, :], psum[:, 2 * c * 512:2 * c * 512 + TM], ACT.Exp,
                                         bias=nmx[:, u % 4:u % 4 + 1],
                                         accum_out=zs[:, u % 4:u % 4 + 1]).then_inc(exp_done, 1)
                if turn >= 1:
                    turn_copy(turn - 1)
                    if turn % TT == 0:
                        head_out(turn // TT - 1)
            turn_copy(HEADS * TT - 1)
            head_out(HEADS - 1)

            def head_norms(lo, sqs, stds):
                for h in range(HEADS):
                    nc.scalar.activation(sqs[:, h, :], otmp[:, h, :], ACT.Square).then_inc(osq_out, 1)
                for h in range(HEADS):
                    act.wait_ge(oss_done, lo + h + 1)
                    nc.scalar.activation(stds[:, h, :], bank(h), ACT.Sqrt, bias=EPSC,
                                         scale=1.0 / P).then_inc(ostd_out, 1)

            act.wait_ge(av_out, HEADS)
            act.wait_ge(exp_done, 2 * HEADS * TT)
            head_norms(0, aT, v3(pr.rearrange("p a b -> p (a b)")[:, 0:4 * T], 4))

            for h in range(HEADS):
                for li in range(NL):
                    u = h * NL + li
                    act.wait_ge(e_in, 2 * (u + 1))
                    nc.scalar.activation(E[:, u % 2, :], E[:, u % 2, :], ACT.Exp,
                                         scale=1.0 / 16).then_inc(e_exp, 1)
                act.wait_ge(em_in, h + 1)
                nc.scalar.activation(Em[0:DH, T:TM], Em[0:DH, T:TM], ACT.Exp, scale=1.0 / 16)
                nc.scalar.activation(Em[0:DH, 0:T], B[0:DH, h, 0:T], ACT.Exp,
                                     scale=1.0 / 16).then_inc(em_exp, 1)
                act.wait_ge(wide_done, h + 1)
                if h >= 1:
                    act.wait_ge(gav_done, h)
                for half in range(2):
                    off = T // 2 if half == 0 else 0
                    nc.scalar.activation(A[:, 2 * half:2 * half + 2, off:off + 256], v3(bank(half), 2),
                                         ACT.Copy).then_inc(wide_out, 1)
                nc.scalar.activation(Am[0:M, :], psum[0:M, 2 * 512:3 * 512], ACT.Copy).then_inc(wide_out, 1)
                act.wait_ge(gav_done, h + 1)
                if h == 0:
                    act.wait_ge(mixl_out, 1)
                nc.scalar.activation(otmp[:, h, :], bank(3), ACT.Copy).then_inc(gav_out, 1)
            act.wait_ge(gav_out, HEADS)
            head_norms(HEADS, A, KT[:, 0:4, :])
            for n in range(N_WO, N_PQ):
                cuts.upto(n + 3)
                act.wait_ge(slab_done, n + 1)

            Norm("ln2").act(act, lambda: act.wait_ge(res_out, KC))

            def query_out(m, kk):
                act.wait_ge(slab_done, m + N_PQ + 1)
                wait(act, s_done, m - 1)
                nc.scalar.activation(pq[:, kk % 2, :], bank(kk % 2), ACT.Copy, scale=ISW).then_inc(pq_out, 1)

            def scores_out(m, head, kk):
                act.wait_ge(s_done, m + 1)
                wait(act, head_done, head - 1)
                nc.scalar.activation(s_[kk // 2][:, kk % 2, :], bank(2 + kk % 2), ACT.Copy).then_inc(s_out, 1)

            def gate_exp(head):
                act.wait_ge(gsub_out, head + 1)
                nc.scalar.activation(gsm, gsm, ACT.Exp).then_inc(gexp_out, 1)

            def query_turn(i):
                for kk in range(SLOTS):
                    cuts.ahead(i + N_PQ // SLOTS, kk)
                    m = i * SLOTS + kk
                    query_out(m, kk)
                    if kk:
                        scores_out(m - 1, i * 2 + (kk - 1) // 2, kk - 1)
                    if kk == 3:
                        gate_exp(i * 2)
                scores_out(m, i * 2 + 1, 3)
                gate_exp(i * 2 + 1)

            query_turn(0)
            with act.Fori(1, PH // 2) as i:
                query_turn(i)
            cuts.n += 2 * PH

            for v in range(3):
                act.wait_ge(idx_turned, v + 1)
                nc.scalar.activation(idxT[:, v, :], bank(4 + v), ACT.Copy).then_inc(idxT_out, 1)

            def gate_octet(e, par, j):
                for half in range(2):
                    act.wait_ge(g_done, e * 8 + (4 * half + 4))
                    nc.scalar.activation(G[par][:, :, bass.ds(j * 8 + 4 * half, 4)].rearrange("p i n -> p n i"),
                                         v3(bank(half), 4), ACT.Copy).then_inc(g_out, 1)

            act.wait_ge(head_done, PH)
            gate_octet(0, 0, 0)
            with act.Fori(1, 8) as j:
                gate_octet(j, 0, j)
            with act.Fori(0, 8) as j:
                gate_octet(j + 8, 1, j)
            with act.Fori(1, GT // 2) as o:
                for par in range(2):
                    act.wait_ge(g_stored[par], o * 16)
                    with act.Fori(0, 8) as j:
                        gate_octet(o * 16 + j + 8 * par, par, j)

            def expert_group(g, par):
                for s in range(GRP):
                    cuts.ahead(g + N_U // SLOTS, s)
                    act.wait_ge(vslab_in[s], g * 16 + 16)
                    wait(act, b_done, (g - 1) * KC)
                    nc.scalar.activation(vh[:, par * GRP + s, :], vraw[:, s, :], ACT.Copy,
                                         scale=WS).then_inc(vhigh_cut, 1)
                    act.wait_ge(slab_done, g * GRP + (N_U + s + 1))
                    wait(act, gated_out, g * GRP + (s - 1))
                    nc.scalar.activation(act_s[:, s % 2, :], bank(s % 2), ACT.Gelu,
                                         scale=ISW).then_inc(gelu_out, 1)

            act.wait_ge(g_stored[0], GT // 2 * 16)
            act.wait_ge(g_stored[1], GT // 2 * 16)
            for g in range(3):
                expert_group(g, g % 2)
            with act.Fori(1, GROUPS // 2 - 1) as o:
                expert_group(o * 2 + 1, 1)
                expert_group(o * 2 + 2, 0)
            expert_group(GROUPS - 1, 1)
            cuts.n += NK
            Norm("final1").act(act, lambda: act.wait_ge(acc_out, GROUPS * KC))

            Norm("mixn").act(act, lambda: act.wait_ge(final1_out, KC))
            act.wait_ge(pads, 2)
            for n in range(N_POOL, N_WP):
                c = n - N_POOL
                cuts.upto(n + 3)
                act.wait_ge(slab_done, n + 1)
                wait(act, pool_cut, c - 1)
                nc.scalar.activation(zp[c % 2][:, 16:16 + T], bank(n % 4), ACT.Copy,
                                     scale=ISW).then_inc(zpool_out, 1)
            for n in range(N_WP, N_SV):
                cuts.upto(n + 3)
            act.wait_ge(y_cut, KC)
            for half in range(2):
                cuts.upto(N_SV + 4 * half + 7)
                act.wait_ge(slab_done, N_SV + 4 * half + 4)
                for t in range(TT):
                    nc.scalar.activation(V2[:, 2 * t + half, :], bank(4 * half + t), ACT.Gelu,
                                         scale=ISW).then_inc(v_out, 1)
            act.wait_ge(v_out, 2 * TT)
            for t in range(TT):
                nc.scalar.activation(U2[:, 2 * (t % 2):2 * (t % 2) + 2, :], V2[:, 2 * t:2 * t + 2, :], ACT.Square,
                                     accum_out=vss[:, t:t + 1]).then_inc(vsq_out, 1)
                act.wait_ge(vsq_out, t + 1)
            nc.scalar.activation(vrs[:, 0:TT], vss[:, 0:TT], ACT.Sqrt, bias=EPSC,
                                 scale=1.0 / D).then_inc(vstd_out, 1)
            for n in range(N_SU, N_GA):
                cuts.upto(n + 3)
                act.wait_ge(slab_done, n + 1)
                nc.scalar.activation(U2[:, n - N_SU, :], bank(n % 4), ACT.Gelu, scale=ISW).then_inc(u_out, 1)
            act.wait_ge(sgu_cut, KC)
            for n in range(N_GA, N_WO2):
                i = n - N_GA
                b = i // 2
                cuts.upto(n + 3)
                if i % 2 == 0:
                    act.wait_ge(slab_done, n + 1)
                    wait(act, branch_out, b - 1)
                    nc.scalar.activation(gat[:, b % 2, :], bank(n % 4), ACT.Sigmoid,
                                         scale=ISW).then_inc(gsig_out, 1)
            for n in range(N_WO2, N_UP):
                cuts.upto(n + 3)

            Norm("ffnn").act(act, lambda: act.wait_ge(res2_out, KC))
            act.wait_ge(pads, 6)

            def up_turn(i):
                for pair in range(2):
                    for side in range(2):
                        s = 2 * pair + side
                        cuts.ahead(i + N_UP // SLOTS, s)
                        act.wait_ge(slab_done, i * SLOTS + (N_UP + s + 1))
                        wait(act, conv_out, i * SLOTS + (s - 3))
                        nc.scalar.activation(upb[s][:, 2:2 + T], bank(s), ACT.Copy,
                                             scale=ISW).then_inc(up_out, 1)
                    act.wait_ge(conv_out, i * SLOTS + (2 * pair + 1))
                    nc.scalar.activation(cv[:, 3 * pair + 2, :], cv[:, 3 * pair, :],
                                         ACT.Gelu).then_inc(cgelu_out, 1)

            up_turn(0)
            with act.Fori(1, FC // 2) as i:
                up_turn(i)
            cuts.n += 2 * FC
            cuts.upto(N_DN + 6)
            with act.Fori(1, FC // SLOTS) as i:
                for s in range(SLOTS):
                    cuts.ahead(i + N_DN // SLOTS, s)
            cuts.n += (FC // SLOTS - 1) * SLOTS
            act.wait_ge(p_in, 16)
            nc.scalar.activation(pth, prw, ACT.Copy).then_inc(p_high, 1)
            cuts.upto(N_PG + 2)
            Norm("plen").act(act, lambda: act.wait_ge(down_out, KC))
            for n in range(N_PG, N_PP):
                cuts.upto(n + 3)
                act.wait_ge(slab_done, n + 1)
                nc.scalar.activation(pgs[:, n - N_PG, :], bank(n % 4), ACT.Sigmoid,
                                     scale=ISW).then_inc(psig_out, 1)
            Norm("final2").act(act, lambda: act.wait_ge(ple_out, KC))

        @block.vector
        def _(dve):
            dchain.eng = dve
            cuts = Cuts(dve, cut_low)
            dve.wait_ge(vecs_in, 16)
            L = VEC["lam"]
            nc.vector.tensor_tensor(LAMP[0:DH, :], vec[0:DH, L:L + 4:2], vec[0:DH, L + 1:L + 4:2],
                                    ALU.mult).then_inc(lam_prod, 1)
            dve.wait_ge(x_in, 48)
            n1 = Norm("ln1")
            n1.dve(dve)
            dve.wait_ge(lam_exp, 1)
            dchain.link(nc.vector.tensor_tensor(NLAM, LAME[:, 1:2], LAME[:, 0:1], ALU.subtract))
            dchain.link(nc.vector.tensor_scalar(NLAM, NLAM, LAM_INIT, None, ALU.subtract))
            nc.vector.tensor_scalar(SUBW, vec[:, VEC["subln"]:VEC["subln"] + 1], 1.0 - LAM_INIT, None, ALU.mult)
            cuts.upto(2)
            dve.wait_ge(consts_in, 160)

            def rope(n):
                dve.wait_ge(rope_out, n + 1)
                if n < HEADS:
                    dst, m = q[:, n, :], None
                else:
                    dst, m = k[:, n - HEADS, 0:T], k[:, n - HEADS, T:TM]
                a = nc.vector.tensor_tensor(rtmp[:, 0, :], bank(6), ropes[:, 0:T], ALU.mult)
                if m is not None:
                    a = nc.vector.tensor_tensor(rtmp[:, 1, 0:M], bank(7, M), ropes[:, T:TM], ALU.mult)
                a.then_inc(rope_mul, 1)
                a = nc.vector.tensor_tensor(dst, dst, ropec[:, 0:T], ALU.mult)
                if m is not None:
                    a = nc.vector.tensor_tensor(m, m, ropec[:, T:TM], ALU.mult)
                dchain.link(a)
                dve.wait_ge(rope_mul, n + 1)
                a = nc.vector.tensor_tensor(dst, dst, rtmp[:, 0, :], ALU.add)
                if m is not None:
                    a = nc.vector.tensor_tensor(m, m, rtmp[:, 1, 0:M], ALU.add)
                dchain.link(a)

            for n in range(N_Q, N_V):
                cuts.upto(n + 3)
                if n >= 1:
                    rope(n - 1)
            rope(N_V - 1)
            dve.wait_ge(wz_high, 1)
            nc.vector.scalar_tensor_tensor(out=wzl.rearrange("p a b -> p (a b)"), in0=wz, scalar=WS,
                                           in1=wzh.rearrange("p a b -> p (a b)"), op0=ALU.mult,
                                           op1=ALU.subtract).then_inc(wz_low, 1)
            cuts.upto(N_V + 11)
            for n in range(N_GQ, N_GR):
                cuts.upto(n + 3)
            for n in range(N_GR, N_WO):
                cuts.upto(n + 3)
                dve.wait_ge(sig_out, n - N_GR + 1)
                nc.vector.scalar_tensor_tensor(out=sgr[:, n - N_GR, :], in0=bank(n % 4), scalar=ISW,
                                               in1=sgr[:, n - N_GR, :], op0=ALU.mult,
                                               op1=ALU.mult).then_inc(silu_out, 1)
            dve.wait_ge(gate_ln, 1)
            dchain.link(nc.vector.scalar_tensor_tensor(
                out=gtmp.rearrange("p a b -> p (a b)"), in0=B.rearrange("p a b -> p (a b)"), scalar=0.0,
                in1=gtmp.rearrange("p a b -> p (a b)"), op0=ALU.min, op1=ALU.subtract))
            for h in range(HEADS):
                nc.vector.tensor_tensor_scan(B[:, h, 0:T], one.to_broadcast([P, T]), gtmp[:, h, 0:T], 0.0,
                                             ALU.mult, ALU.add)
                a = nc.vector.tensor_tensor_scan(B[:, h, T:TM], one.to_broadcast([P, M]), gtmp[:, h, T:TM], 0.0,
                                                 ALU.mult, ALU.add)
            dchain.link(a)
            for h in range(HEADS):
                nc.vector.tensor_tensor(B[DH:P, h, 0:T], B[DH:P, h, 0:T], gtmp[DH:P, h, 0:T],
                                        ALU.subtract).then_inc(gate_out, 1)

            def scores_max(turn):
                for c in range(2):
                    u = 2 * turn + c
                    dve.wait_ge(score_done, u + 1)
                    nc.vector.tensor_reduce(nmx[:, u % 4:u % 4 + 1], psum[:, 2 * c * 512:2 * c * 512 + TM],
                                            AX.X, ALU.max, negate=True).then_inc(max_done, 1)

            def difference(turn):
                par = turn % 2
                dve.wait_ge(exp_done, 2 * turn + 2)
                rz_ = rzs[:, 4 * par:4 * par + 2]
                dchain.link(nc.vector.reciprocal(rz_, zs[:, 2 * par:2 * par + 2]))
                dchain.link(nc.vector.tensor_tensor(rz_[:, 1:2], rz_[:, 1:2], NLAM, ALU.mult))
                dchain.link(nc.vector.tensor_scalar(pr[:, 2 * par + 1, :], pr[:, 2 * par + 1, :],
                                                    rz_[:, 1:2], None, ALU.mult))
                if turn >= 2:
                    dve.wait_ge(turn_done, turn - 1)
                nc.vector.scalar_tensor_tensor(out=pa[:, par, :], in0=pr[:, 2 * par, :],
                                               scalar=rz_[:, 0:1], in1=pr[:, 2 * par + 1, :],
                                               op0=ALU.mult, op1=ALU.add).then_inc(diff_done, 1)

            for turn in range(HEADS * TT):
                scores_max(turn)
                if turn >= 1:
                    difference(turn - 1)
            difference(HEADS * TT - 1)

            def head_norms(lo, stds, w, times=None):
                dve.wait_ge(ostd_out, lo + HEADS)
                dchain.link(nc.vector.reciprocal(stds, stds))
                for h in range(HEADS):
                    a = nc.vector.scalar_tensor_tensor(out=otmp[:, h, :], in0=otmp[:, h, :], scalar=w,
                                                       in1=stds[:, h, :], op0=ALU.mult, op1=ALU.mult)
                dchain.link(a)
                if times is not None:
                    dchain.link(nc.vector.tensor_tensor(otmp, otmp, times, ALU.mult))
                dchain.link(nc.vector.tensor_copy(xh[:, lo:lo + HEADS, 0:T], otmp))
                nc.vector.tensor_tensor(xl[:, lo:lo + HEADS, 0:T], otmp, xh[:, lo:lo + HEADS, 0:T],
                                        ALU.subtract).then_inc(mixl_out, 1)

            head_norms(0, v3(pr.rearrange("p a b -> p (a b)")[:, 0:4 * T], 4), SUBW)

            dve.wait_ge(mixl_out, 1)
            dve.wait_ge(gate_out, HEADS)
            nc.vector.memset(KT, 0.0)
            nc.vector.memset(QT, 0.0).then_inc(zeroed, 1)
            dve.wait_ge(zeroed, 1)

            def blocks(ap, s, side):
                return ap.rearrange("p (n two s) -> p n two s", two=2, s=s)[:, :, side, :]

            def exponents(h, li):
                s, u = LEVELS[li], h * NL + li
                b = B[:, h, 0:T]
                ref = blocks(b, s, 0)[:, :, s - 1:s].to_broadcast([P, T // (2 * s), s])
                if u >= 2:
                    dve.wait_ge(kt_out, 2 * (u - 1))
                    dve.wait_ge(qt_out, 2 * (u - 1))
                nc.vector.tensor_tensor(blocks(E[:, u % 2, :], s, 0), ref, blocks(b, s, 0),
                                        ALU.subtract).then_inc(e_in, 1)
                nc.vector.tensor_tensor(blocks(E[:, u % 2, :], s, 1), blocks(b, s, 1), ref,
                                        ALU.subtract).then_inc(e_in, 1)

            def decayed(h, li):
                s, u = LEVELS[li], h * NL + li
                dve.wait_ge(e_exp, u + 1)
                if h >= 1:
                    need_level_free(dve, h, li)
                for src, dst, side, done in ((gk, KT, 0, kt_out), (gq, QT, 1, qt_out)):
                    for half in range(2):
                        rows = slice(DH * half, DH * (half + 1))
                        sd = side ^ half
                        nc.vector.tensor_tensor(
                            blocks(dst[rows, li, :], s, sd), blocks(src[rows, h, 0:T], s, sd),
                            blocks(E[rows, u % 2, :], s, sd), ALU.mult).then_inc(done, 1)

            def need_level_free(eng, h, li):
                if li <= NS:
                    eng.wait_ge(lev_done, (h - 1) * (NS + 2) + li + 2)
                else:
                    eng.wait_ge(wide_done, h)

            for h in range(HEADS):
                def level_out(li):
                    u = h * (NS + 2) + li + 1
                    dve.wait_ge(lev_done, u + 1)
                    if li < 0 and h >= 1:
                        dve.wait_ge(gav_done, h)
                    if u >= 1:
                        dve.wait_ge(lev_out, u)
                    src = v3(bank(4 + u % 3), TT)
                    if li < NS:
                        mk = masks[:, li + 1:li + 2, :].to_broadcast([P, TT, P])
                        nc.vector.copy_predicated(Adiag, mk, src).then_inc(lev_out, 1)
                    else:
                        for j in range(TT):
                            i = j ^ 1
                            a = nc.vector.tensor_copy(A[:, j, i * P:(i + 1) * P], src[:, j, :])
                        a.then_inc(lev_out, 1)

                if h == 0:
                    exponents(0, 0)
                for li in range(NL):
                    if li + 1 < NL:
                        exponents(h, li + 1)
                    elif h + 1 < HEADS:
                        exponents(h + 1, 0)
                    decayed(h, li)
                    if li >= 1:
                        level_out(li - 2)
                nc.vector.tensor_tensor(Em[0:DH, T:TM],
                                        B[0:DH, h, TM - 1:TM].to_broadcast([DH, M]), B[0:DH, h, T:TM],
                                        ALU.subtract).then_inc(em_in, 1)
                dve.wait_ge(em_exp, h + 1)
                nc.vector.tensor_tensor(KTm[0:DH, :], gk[0:DH, h, T:TM], Em[0:DH, T:TM],
                                        ALU.mult).then_inc(ktm_out, 1)
                nc.vector.tensor_tensor(QTm[0:DH, :], gq[0:DH, h, 0:T], Em[0:DH, 0:T],
                                        ALU.mult).then_inc(ktm_out, 1)
                level_out(NS)
            dve.wait_ge(silu_out, HEADS)
            head_norms(HEADS, KT[:, 0:4, :], vec[:, VEC["glan"]:VEC["glan"] + 1], times=sgr)

            for n in range(N_WO, N_PQ):
                cuts.upto(n + 3)
                dve.wait_ge(slab_done, n + 1)
                c = n - N_WO
                nc.vector.scalar_tensor_tensor(out=X[:, c, 0:T], in0=bank(n % 4), scalar=ISW,
                                               in1=X[:, c, 0:T], op0=ALU.mult,
                                               op1=ALU.add).then_inc(res_out, 1)

            dve.wait_ge(res_out, KC)
            Norm("ln2").dve(dve)

            def tiles(ap):
                return v3(ap, TT)

            def each(fn):
                for side in range(2):
                    for t in range(TT):
                        last = fn(side, t)
                return last

            def settled(ins):
                nc.vector.drain()

            def choose(head, sc):
                k8 = lambda side, t, lo: ts[:, side, t * TOP + lo:t * TOP + lo + 8]
                i8 = lambda side, t, lo: ti[:, side, t * TOP + lo:t * TOP + lo + 8]
                sk = lambda side, t: sc[:, side, t * P:(t + 1) * P]
                s2k = lambda side, t: s2[:, side, t * P:(t + 1) * P]
                settled(each(lambda a, t: nc.vector.max(k8(a, t, 0), sk(a, t))))
                settled(each(lambda a, t: nc.vector.match_replace(s2k(a, t), k8(a, t, 0), sk(a, t), LOWEST)))
                settled(each(lambda a, t: nc.vector.max(k8(a, t, 8), s2k(a, t))))
                each(lambda a, t: nc.vector.max_index(i8(a, t, 0), k8(a, t, 0), sk(a, t)))
                settled(each(lambda a, t: nc.vector.max_index(i8(a, t, 8), k8(a, t, 8), s2k(a, t))))
                nc.vector.tensor_copy(tif, ti)
                full = [P, TT, TOP, TOP]
                c4 = cand.rearrange("p t (a b) -> p t a b", a=TOP)
                settled(nc.vector.tensor_tensor(c4, tiles(ts[:, 0, :]).unsqueeze(3).to_broadcast(full),
                                                    tiles(ts[:, 1, :]).unsqueeze(2).to_broadcast(full), ALU.add))
                rng = range(TT)
                settled([nc.vector.max(best[:, t, 0:8], cand[:, t, :]) for t in rng][-1])
                settled([nc.vector.match_replace(cand2[:, t, :], best[:, t, 0:8], cand[:, t, :], LOWEST)
                             for t in rng][-1])
                settled([nc.vector.max(best[:, t, 8:16], cand2[:, t, :]) for t in rng][-1])
                g3 = v3(gsm, TT)
                nc.vector.tensor_tensor(g3, best, best[:, :, 0:1].to_broadcast([P, TT, TOP]),
                                        ALU.subtract).then_inc(gsub_out, 1)
                [nc.vector.max_index(pos[:, t, 0:8], best[:, t, 0:8], cand[:, t, :]) for t in rng]
                settled([nc.vector.max_index(pos[:, t, 8:16], best[:, t, 8:16], cand2[:, t, :])
                             for t in rng][-1])
                pf = pos.rearrange("p a b -> p (a b)")
                nc.vector.tensor_scalar(posab[:, 0, :], pf, 4, None, ALU.logical_shift_right)
                settled(nc.vector.tensor_scalar(posab[:, 1, :], pf, 15, None, ALU.bitwise_and))
                settled(nc.vector.tensor_copy(posf, posab))
                sel4 = sel.rearrange("p (t k a) -> p t k a", t=TT, k=TOP)
                cols = bass.ds(head * TOP, TOP)
                for side in range(2):
                    settled(nc.vector.tensor_tensor(
                        sel4, tiles(posf[:, side, :]).unsqueeze(3).to_broadcast(full),
                        io16.unsqueeze(1).unsqueeze(1).to_broadcast(full), ALU.is_equal))
                    settled(nc.vector.tensor_tensor(
                        sel4, sel4, tiles(tif[:, side, :]).unsqueeze(2).to_broadcast(full), ALU.mult))
                    nc.vector.tensor_reduce(tiles(idx_tok[:, side, :])[:, :, cols], sel4, AX.X, ALU.add)
                    if side == 0:
                        dve.wait_ge(gexp_out, head + 1)
                        settled(nc.vector.tensor_reduce(gsum[:, 0:TT], g3, AX.X, ALU.add))
                settled(nc.vector.reciprocal(gsum[:, 8:8 + TT], gsum[:, 0:TT]))
                nc.vector.tensor_tensor(tiles(idx_tok[:, 2, :])[:, :, cols], g3,
                                        gsum[:, 8:8 + TT].unsqueeze(2).to_broadcast([P, TT, TOP]),
                                        ALU.mult).then_inc(head_done, 1)

            def query_turn(i):
                for kk in range(SLOTS):
                    if kk % 2:
                        dve.wait_ge(s_out, i * SLOTS + (kk + 1))
                    cuts.ahead(i + N_PQ // SLOTS, kk)
                    if kk % 2:
                        choose(i * 2 + kk // 2, s_[kk // 2])

            LOWEST = -3.0e38
            query_turn(0)
            with dve.Fori(1, PH // 2) as i:
                query_turn(i)
            cuts.n += 2 * PH

            def gate_octet(e, tok):
                for tk in range(8):
                    col = bass.ds(tok + tk, 1)
                    wait(dve, g_done, e * 8 + (tk - 7))
                    nc.vector.tensor_scalar(hot[:, 2 * tk, :], iota, idxT[:, 1, col], None, ALU.is_equal)
                    nc.vector.tensor_scalar(hot[:, 2 * tk + 1, :], iota, idxT[:, 0, col], idxT[:, 2, col],
                                            ALU.is_equal, ALU.mult).then_inc(hot_out, 1)

            dve.wait_ge(idxT_out, 3)
            gate_octet(0, 0)
            with dve.Fori(1, T // 8) as e:
                gate_octet(e, e * 8)

            def gated(g, par, s):
                if s == 0:
                    dve.wait_ge(g_in[par], (g // 2) * 16 + 16 if isinstance(g, int) else g * 8 + (16 - 8 * par))
                dve.wait_ge(gelu_out, g * GRP + (s + 1))
                tl = lambda ap: v3(ap, GT)
                wait(dve, a_cut, g * GRP + (s - 1))
                nc.vector.tensor_tensor(tl(at_s[:, s % 2, :]), tl(act_s[:, s % 2, :]),
                                        GB[par][:, :, s * NT:(s + 1) * NT], ALU.mult).then_inc(gated_out, 1)
                dve.wait_ge(gated_out, g * GRP + (s + 1))
                wait(dve, b_done, (g - 1) * KC)
                x = par * GRP + s
                dchain.link(nc.vector.tensor_copy(Ah[:, x, :], at_s[:, s % 2, :]))
                nc.vector.tensor_tensor(Al[:, x, :], at_s[:, s % 2, :], Ah[:, x, :],
                                        ALU.subtract).then_inc(a_cut, 1)

            def expert_group(g, par, inputs=True, outputs=True):
                gp = g - 1
                for s in range(GRP):
                    if inputs:
                        cuts.ahead(g + N_U // SLOTS, s)
                        dve.wait_ge(vhigh_cut, g * GRP + (s + 1))
                        nc.vector.scalar_tensor_tensor(
                            out=vl[:, par * GRP + s, :], in0=vraw[:, s, :], scalar=WS,
                            in1=vh[:, par * GRP + s, :], op0=ALU.mult, op1=ALU.subtract).then_inc(vlow_cut, 1)
                    if outputs:
                        if s == 0:
                            wait(dve, acc_out, gp * KC)
                        for c in (2 * s, 2 * s + 1):
                            dve.wait_ge(b_done, gp * KC + (c + 1))
                            nc.vector.scalar_tensor_tensor(
                                out=X[:, c, 0:T], in0=bank(2 + c % 4), scalar=ISW, in1=X[:, c, 0:T],
                                op0=ALU.mult, op1=ALU.add).then_inc(acc_out, 1)
                    if inputs:
                        gated(g, par, s)

            expert_group(0, 0, outputs=False)
            expert_group(1, 1)
            expert_group(2, 0)
            with dve.Fori(1, GROUPS // 2 - 1) as o:
                dchain.enter((o - 1) * (2 * GRP))
                expert_group(o * 2 + 1, 1)
                expert_group(o * 2 + 2, 0)
                dchain.leave(2 * GRP, GROUPS // 2 - 2)
            expert_group(GROUPS - 1, 1)
            expert_group(GROUPS, 0, inputs=False)
            cuts.n += NK
            dve.wait_ge(acc_out, GROUPS * KC)
            Norm("final1").dve(dve, dst=X, done=final1_out)

            dve.wait_ge(final1_out, KC)
            Norm("mixn").dve(dve)

            def cut_onto(src, h_, l_, done):
                dchain.link(nc.vector.tensor_copy(h_, src))
                nc.vector.tensor_tensor(l_, src, h_, ALU.subtract).then_inc(done, 1)

            for n in range(N_POOL, N_WP):
                c = n - N_POOL
                cuts.upto(n + 3)
                dve.wait_ge(zpool_out, c + 1)
                src, z = zp[c % 2], zp[c % 2][:, 16:16 + T]
                for kk in range(c // 2 + 1):
                    w = 2 ** kk
                    lo, dst = 2 * w - 1, win[kk % 2]
                    dchain.link(nc.vector.tensor_tensor(dst[:, lo:16 + T], src[:, lo:16 + T],
                                                        src[:, lo - w:16 + T - w], ALU.add))
                    src = dst
                w = WINDOWS[c // 2]
                tmp = win[(c // 2 + 1) % 2][:, 0:T]
                nc.vector.scalar_tensor_tensor(out=tmp[:, w:T], in0=src[:, 16 + w:16 + T], scalar=1.0 / w,
                                               in1=z[:, w:T], op0=ALU.mult, op1=ALU.subtract)
                dchain.link(nc.vector.tensor_tensor(tmp[:, 0:w], src[:, 16:16 + w], icnt[:, 0:w], ALU.mult))
                dchain.link(nc.vector.tensor_tensor(tmp[:, 0:w], tmp[:, 0:w], z[:, 0:w], ALU.subtract))
                cut_onto(tmp, ph_[:, c, :], pl_[:, c, :], pool_cut)
                dve.wait_ge(pool_cut, c + 1)
            for n in range(N_WP, N_SV):
                cuts.upto(n + 3)
                dve.wait_ge(slab_done, n + 1)
                for c in (2 * (n - N_WP), 2 * (n - N_WP) + 1):
                    col = vec[:, VEC["pscale"] + c:VEC["pscale"] + c + 1]
                    dchain.link(nc.vector.tensor_scalar(V2[:, c, :], bank(c % 4), ISW, col, ALU.mult, ALU.mult))
                    cut_onto(V2[:, c, :], yh[:, c, :], yl[:, c, :], y_cut)
            cuts.upto(N_SV + 11)
            dve.wait_ge(vstd_out, 1)
            dchain.link(nc.vector.reciprocal(vrs[:, 4:8], vrs[:, 0:4]))
            for t in range(TT):
                nc.vector.tensor_scalar(V2[:, 2 * t:2 * t + 2, :], V2[:, 2 * t:2 * t + 2, :], vrs[:, 4 + t:5 + t],
                                        None, ALU.mult).then_inc(v_normed, 1)
            dve.wait_ge(small_in, 32)
            for n in range(N_SU, N_GA):
                h = n - N_SU
                cuts.upto(n + 3)
                dve.wait_ge(mix_done, h + 1)
                m = mtmp[:, h % 2, :]
                col = vec[:, VEC["sgun"] + h:VEC["sgun"] + h + 1]
                nc.vector.scalar_tensor_tensor(
                    out=v3(m, TT), in0=v3(bank(4 + h % 2), TT), scalar=col,
                    in1=bsp[:, h * P:(h + 1) * P].unsqueeze(1).to_broadcast([P, TT, P]), op0=ALU.mult,
                    op1=ALU.add).then_inc(mix_read, 1)
                dve.wait_ge(mix_read, h + 1)
                dve.wait_ge(u_out, h + 1)
                dchain.link(nc.vector.tensor_tensor(m, m, U2[:, h, :], ALU.mult))
                cut_onto(m, ph_[:, h, :], pl_[:, h, :], sgu_cut)
            for n in range(N_GA, N_WO2):
                i = n - N_GA
                b, c = i // 2, i // 2 % KC
                cuts.upto(n + 3)
                if i % 2:
                    dve.wait_ge(slab_done, n + 1)
                    dve.wait_ge(gsig_out, b + 1)
                    dst = V2[:, c, :] if b < KC else mtmp[:, b % 2, :]
                    nc.vector.scalar_tensor_tensor(out=dst, in0=bank(n % 4), scalar=ISW, in1=gat[:, b % 2, :],
                                                   op0=ALU.mult, op1=ALU.mult).then_inc(branch_out, 1)
                    if b >= KC:
                        dve.wait_ge(branch_out, b + 1)
                        dchain.link(nc.vector.tensor_tensor(V2[:, c, :], V2[:, c, :], mtmp[:, b % 2, :], ALU.add))
                        cut_onto(V2[:, c, :], yh[:, c, :], yl[:, c, :], m_cut)
            for n in range(N_WO2, N_UP):
                cuts.upto(n + 3)
                dve.wait_ge(slab_done, n + 1)
                c = n - N_WO2
                nc.vector.scalar_tensor_tensor(out=X[:, c, 0:T], in0=bank(n % 4), scalar=ISW,
                                               in1=X[:, c, 0:T], op0=ALU.mult,
                                               op1=ALU.add).then_inc(res2_out, 1)

            dve.wait_ge(res2_out, KC)
            Norm("ffnn").dve(dve)

            def conv(i, f, pair, side):
                s = 2 * pair + side
                dst = cv[:, 3 * pair + side, :]
                cw = lambda tap: vec[:, bass.ds(f + (VEC["convw"] + tap * 2 * FC + side * FC), 1)]
                cb = vec[:, bass.ds(f + (VEC["convb"] + side * FC), 1)]
                dve.wait_ge(up_out, i * SLOTS + (s + 1))
                dchain.link(nc.vector.tensor_scalar(dst, upb[s][:, 2:2 + T], cw(2), cb, ALU.mult, ALU.add))
                dchain.link(nc.vector.scalar_tensor_tensor(out=dst, in0=upb[s][:, 1:1 + T], scalar=cw(1), in1=dst,
                                                           op0=ALU.mult, op1=ALU.add))
                return nc.vector.scalar_tensor_tensor(out=dst, in0=upb[s][:, 0:T], scalar=cw(0), in1=dst,
                                                      op0=ALU.mult, op1=ALU.add)

            def up_turn(i):
                for pair in range(2):
                    f = i * 2 + pair
                    cuts.ahead(i + N_UP // SLOTS, 2 * pair)
                    a = conv(i, f, pair, 0)
                    a.then_inc(conv_out, 1)
                    cuts.ahead(i + N_UP // SLOTS, 2 * pair + 1)
                    conv(i, f, pair, 1).then_inc(conv_out, 1)
                    dve.wait_ge(conv_out, i * SLOTS + (2 * pair + 2))
                    dve.wait_ge(cgelu_out, i * 2 + (pair + 1))
                    p_ = cv[:, 3 * pair + 2, :]
                    dchain.link(nc.vector.tensor_tensor(p_, p_, cv[:, 3 * pair + 1, :], ALU.mult))
                    fi = bass.ds(f, 1)
                    flat = lambda x: x[:, fi, :].rearrange("p a n -> p (a n)")
                    cut_onto(p_, flat(ggh), flat(ggl), ffn_cut)

            first = dchain.n
            up_turn(0)
            per = dchain.n - first
            with dve.Fori(1, FC // 2) as i:
                dchain.enter((i - 1) * per)
                up_turn(i)
                dchain.leave(per, FC // 2 - 1)
            cuts.n += 2 * FC
            cuts.upto(N_DN + 6)
            with dve.Fori(1, FC // SLOTS) as i:
                for s in range(SLOTS):
                    cuts.ahead(i + N_DN // SLOTS, s)
            cuts.n += (FC // SLOTS - 1) * SLOTS
            dve.wait_ge(p_high, 1)
            nc.vector.tensor_tensor(ptl, prw, pth, ALU.subtract).then_inc(p_low, 1)
            cuts.upto(N_PG + 2)
            dve.wait_ge(slab_done, N_PG)
            for c in range(KC):
                nc.vector.scalar_tensor_tensor(out=X[:, c, 0:T], in0=bank(c), scalar=ISW,
                                               in1=X[:, c, 0:T], op0=ALU.mult,
                                               op1=ALU.add).then_inc(down_out, 1)
            dve.wait_ge(down_out, KC)
            Norm("plen").dve(dve)
            for n in range(N_PG, N_PP):
                cuts.upto(n + 3)
            for c in range(KC):
                dve.wait_ge(psig_out, c + 1)
                dve.wait_ge(ple_done, c + 1)
                dchain.link(nc.vector.scalar_tensor_tensor(out=ptmp[:, c % 2, :], in0=bank(4 + c % 4), scalar=ISW,
                                                           in1=pgs[:, c, :], op0=ALU.mult, op1=ALU.mult))
                nc.vector.tensor_tensor(X[:, c, 0:T], X[:, c, 0:T], ptmp[:, c % 2, :],
                                        ALU.add).then_inc(ple_out, 1)
            dve.wait_ge(ple_out, KC)
            Norm("final2").dve(dve, dst=yout, done=y_out)

        @block.gpsimd
        def _(pool):
            nc.gpsimd.memset(EPSC, EPS).then_inc(pool_step, 1)
            pool.wait_ge(final1_out, KC)
            for z in zp:
                nc.gpsimd.memset(z[:, 0:16], 0.0).then_inc(pads, 1)
            pool.wait_ge(small_in, 32)
            w3 = v3(wsT, 8)
            nc.gpsimd.affine_select(out=w3, in_=w3, compare_op=ALU.is_ge, fill=0.0, base=0,
                                    pattern=[[0, 8], [1, P]], channel_multiplier=-1).then_inc(masked, 1)
            pool.wait_ge(res2_out, KC)
            for z in upb:
                nc.gpsimd.memset(z[:, 0:2], 0.0).then_inc(pads, 1)


def tables():
    inv = np.power(np.float32(500000.0), -np.arange(0, 2 * ROPE, 2, dtype=np.float32) / np.float32(2 * ROPE))
    pos = np.concatenate([np.arange(M, TM), np.arange(M)]).astype(np.float32)
    ang = (pos[:, None] * inv[None, :].astype(np.float32)).astype(np.float32)
    ropec, ropes = np.ones((P, TM), np.float32), np.zeros((P, TM), np.float32)
    perm = np.zeros((P, P), np.float32)
    for c in range(2):
        for i in range(ROPE):
            a, b = DH * c + i, DH * c + ROPE + i
            ropec[a] = ropec[b] = np.cos(ang[:, i])
            ropes[a], ropes[b] = -np.sin(ang[:, i]), np.sin(ang[:, i])
            perm[a, b] = perm[b, a] = 1.0
    i = np.arange(P)
    masks = np.zeros((P, len(SMALL) + 1, P), np.uint32)
    masks[:, 0] = np.eye(P, dtype=np.uint32)
    for n, s in enumerate(SMALL):
        masks[:, n + 1] = (i[:, None] // (2 * s) == i[None] // (2 * s)) & (i[:, None] // s != i[None] // s)
    return {
        "ident": np.eye(P, dtype=np.float32), "ones": np.ones((P, P), np.float32),
        "iota": np.tile(i.astype(np.float32), (P, 1)), "perm": perm, "masks": masks, "ropec": ropec,
        "ropes": ropes, "icnt": np.tile(1.0 / np.arange(1, 17, dtype=np.float32), (P, 1)).astype(np.float32),
        "io16": np.tile(np.arange(16, dtype=np.float32), (P, 1)),
    }


def layout(a):
    f = {n: np.asarray(v) for n, v in a.items()}

    def chunks(w):
        kk, n = w.shape
        return w.reshape(kk // P, P, n // P, P).transpose(2, 1, 0, 3).reshape(n // P, P, -1)

    def rows(w):
        return w.reshape(4, 2, P, 512).transpose(0, 2, 1, 3).reshape(4, P, 1024)

    def wide(s):
        return np.concatenate([s, np.zeros((*s.shape[:2], D - s.shape[2]), np.float32)], 2) if s.shape[2] < D else s

    wi = f["w_in"][0]
    cut = np.split(wi, np.cumsum([512, 512, 512, 256, 256, 512, 512, 16])[:].tolist(), axis=1)
    dq, dk, dvw, gqw, gkw, gvw, grw, zf, zb = cut
    w2i = f["w_in_2"][0]
    pool, zu, zv, ga, gb = (w2i[:, i * D:(i + 1) * D] for i in range(5))
    up = chunks(f["w_up_2"][0])
    woven = lambda x, y: np.stack([x, y], 1).reshape(-1, P, x.shape[2])
    wp = f["w_pool_2"][0].reshape(4, 2, P, 2, P).transpose(0, 2, 3, 1, 4).reshape(4, P, 512)
    u = f["peer_u"][0].reshape(NK, NK, KC, P).transpose(0, 3, 2, 1).reshape(NK, P, D)
    parts = [chunks(dq), chunks(dk), rows(dvw), rows(gvw), chunks(gqw), chunks(gkw), chunks(grw),
             chunks(f["w_out"][0]), chunks(f["peer_w_q"][0]), u, chunks(pool), wide(wp),
             rows(zv[:, :512]), rows(zv[:, 512:]), chunks(zu), woven(chunks(ga), chunks(f["w_branch_a_2"][0])),
             woven(chunks(gb), chunks(f["w_branch_b_2"][0])), chunks(f["w_out_2"][0]), woven(up[:FC], up[FC:]),
             f["w_down_2"][0].reshape(FC, P, D), chunks(f["w_ple_gate_2"][0]),
             chunks(f["w_ple_2"][0]).reshape(2, 4, P, 256).transpose(0, 2, 1, 3).reshape(2, P, D)]
    w = np.concatenate(parts, 0)
    assert w.shape[0] == N_END, (w.shape, N_END)

    col = lambda v: v.reshape(-1, P).T
    pad = lambda v: np.concatenate([v, np.zeros(P - v.size, np.float32)])
    vecs = [col(f[n].reshape(-1)) for n in ("ln1_w", "ln2_w", "final_norm_w", "mix_norm_2", "pool_scale_2",
                                            "sgu_norm_2", "ffn_norm_2", "ple_norm_2", "final_norm_2")]
    vecs += [col(f["conv_w_2"][0].reshape(-1)), col(f["conv_b_2"][0]), f["da_subln_w"].T, f["gla_norm_w"].T]
    gf, gbk = f["gla_gate_b_f"][0].reshape(HEADS, DH), f["gla_gate_b_b"][0].reshape(HEADS, DH)
    vecs += [np.concatenate([gf, gbk], 1).T]
    vecs += [np.stack([pad(f[n][0]) for n in ("da_lambda_q1", "da_lambda_k1", "da_lambda_q2", "da_lambda_k2")], 1)]
    w2 = np.zeros((32, HEADS, P), np.float32)
    w2[:16, :, :DH] = f["gla_gate_w2_f"][0].reshape(16, HEADS, DH)
    w2[16:, :, DH:] = f["gla_gate_w2_b"][0].reshape(16, HEADS, DH)
    fm = lambda x: x.T.reshape(-1, P, x.shape[0]).transpose(1, 0, 2)
    out = {
        "xT": fm(f["x"][0]), "metaT": fm(f["meta_tokens"]), "vec": np.concatenate(vecs, 1), "w": w,
        "w2": w2, "wz": np.concatenate([zf, zb], 1).reshape(KC, P, 32).transpose(1, 0, 2).reshape(P, KC * 32),
        "keysT": f["peer_sub_keys"][0].reshape(2 * PH, NK, P).transpose(2, 0, 1),
        "v": f["peer_v"][0].reshape(NK, P, D),
        "wsT": f["w_spatial_2"][0].transpose(2, 0, 1).reshape(P, 8 * P), "bsp": f["b_spatial_2"][0].reshape(1, D),
        "pT": fm(f["p_2"][0, 0]), **tables(),
    }
    return {n: np.ascontiguousarray(v) for n, v in out.items()}


def kernel(**inputs):
    import concourse.bacc as bacc
    from concourse.bass_utils import run_bass_kernel_spmd

    nc = bacc.Bacc("TRN2", target_bir_lowering=False, num_devices=1)
    arrays = layout(inputs)
    io = {n: nc.dram_tensor(f"in_{n}", v.shape, mybir.dt.from_np(v.dtype), kind="ExternalInput").ap()
          for n, v in arrays.items()}
    out = nc.dram_tensor("out", (P, KC, T), mybir.dt.float32, kind="ExternalOutput").ap()
    build(nc, io, out)
    r = run_bass_kernel_spmd(nc, [{f"in_{n}": v for n, v in arrays.items()}], core_ids=[0])
    y = r.results[0]["out"]
    return np.ascontiguousarray(y.transpose(2, 1, 0)).reshape(1, T, D)
```

```python
from contextlib import ExitStack

import concourse.bass as bass
import numpy as np
from concourse import mybir

P = 128
D = 1024
KC = D // P
T = 512
TT = T // P
M = 16
TM = T + M
HEADS = 4
DH = 64
ROPE = 8
LEVELS = (1, 2, 4, 8, 16, 32, 64, 128, 256)
SMALL = [s for s in LEVELS if s < P]
PH = 8
TOP = 16
NK = 128
FF = 2816
FC = FF // P
WINDOWS = (2, 4, 8, 16)
EPS = 1e-6
LAM_INIT = 0.8 - 0.6 * float(np.exp(0.0))
WS = 64.0
ISW = 1.0 / WS

SLOTS = 4
N_Q, N_K, N_V, N_GV, N_GQ, N_GK, N_GR = 0, 4, 8, 12, 16, 18, 20
N_WO = 24
N_PQ = 32
N_U = 48
N_POOL = N_U + NK
N_WP = N_POOL + 8
N_SV = N_WP + 4
N_SU = N_SV + 8
N_GA = N_SU + 8
N_GB = N_GA + 16
N_WO2 = N_GB + 16
N_UP = N_WO2 + 8
N_DN = N_UP + 2 * FC
N_PG = N_DN + FC
N_PP = N_PG + 8
N_END = N_PP + 2

VEC = {}
_at = 0
for _name, _n in (("ln1", 8), ("ln2", 8), ("final1", 8), ("mixn", 8), ("pscale", 8), ("sgun", 8), ("ffnn", 8),
                  ("plen", 8), ("final2", 8), ("convw", 6 * FC), ("convb", 2 * FC), ("subln", 1), ("glan", 1),
                  ("gateb", 4), ("lam", 4)):
    VEC[_name] = _at
    _at += _n
NVEC = _at

GRP = 4
GROUPS = NK // GRP
NT = 64
GT = T // NT
OCT = 8
WOVEN = 2 * PH
BEHIND = WOVEN + 2 * SLOTS
EARLY = BEHIND + SLOTS * (GT + 1)
EG = EARLY // GRP
LOW_POOL = N_PQ + SLOTS - 1
TURN_BANKS = (2, 3, 6)


def build(nc, io, out):
    f32, f16, u32, i32 = mybir.dt.float32, mybir.dt.float16, mybir.dt.uint32, mybir.dt.int32
    ALU, ACT, AX = mybir.AluOpType, mybir.ActivationFunctionType, mybir.AxisListType
    ctx = ExitStack()
    with ctx:
        sem_names = {}

        def sem(name):
            sem_names[name] = 1
            return ctx.enter_context(nc.semaphore(name))

        WORDS = 48000
        arena = ctx.enter_context(nc.sbuf_tensor("arena", [P, WORDS], f32))
        psum = ctx.enter_context(nc.psum_tensor("psum", [P, 8 * 512], f32))

        class Region:
            def __init__(self, start):
                self.at = self.top = start

            def take(self, n, dt=f32):
                words = n if dt in (f32, u32, i32) else (n + 1) // 2
                v = arena[:, self.at:self.at + words]
                self.at += words
                assert self.at <= WORDS, self.at
                return v if dt is f32 else v.bitcast(dt)

        def v3(ap, a):
            return ap.rearrange("p (a b) -> p a b", a=a)

        def bank(b, n=512, off=0):
            return psum[:, b * 512 + off:b * 512 + off + n]

        base = Region(0)
        ident = base.take(P)
        ones = base.take(P)
        iota = base.take(P)
        perm = base.take(P)
        masks = v3(base.take((len(SMALL) + 1) * P, u32), len(SMALL) + 1)
        ropec = base.take(TM)
        ropes = base.take(TM)
        vec = base.take(NVEC)
        icnt = base.take(16)
        io16 = base.take(16)
        w2 = v3(base.take(HEADS * P), HEADS)
        wz = base.take(KC * 32)
        wzh = v3(base.take(KC * 32, f16), KC)
        wzl = v3(base.take(KC * 32, f16), KC)
        small = base.take(64)
        wraw = v3(base.take(SLOTS * D), SLOTS)
        wh = v3(base.take(SLOTS * D, f16), SLOTS)
        wl = v3(base.take(SLOTS * D, f16), SLOTS)
        xsq = v3(arena[:, base.at:base.at + KC * T], KC)
        xh = v3(base.take(KC * TM, f16), KC)
        xl = v3(base.take(KC * TM, f16), KC)
        X = v3(base.take(KC * TM), KC)
        FREE = base.at

        r = Region(FREE)
        q = v3(r.take(HEADS * T), HEADS)
        k = v3(r.take(HEADS * TM), HEADS)
        dv = v3(r.take(5 * T), 5)
        pr = v3(r.take(4 * TM), 4)
        pa = v3(r.take(2 * TM), 2)
        aT = v3(r.take(5 * T), 5)
        rtmp = v3(r.take(2 * T), 2)
        gla_top = r.at
        rz = Region(FREE + HEADS * (T + TM) + 5 * T)
        z32 = rz.take(TM)
        gtmp = v3(rz.take(4 * TM), 4)
        gv = v3(r.take(5 * T), 5)
        gq = v3(r.take(HEADS * T), HEADS)
        gk = v3(r.take(HEADS * TM), HEADS)
        sgr = v3(r.take(HEADS * T), HEADS)
        B = v3(r.take(HEADS * TM), HEADS)
        otmp = v3(r.take(4 * T), 4)
        first_end = r.at
        r = Region(FREE)
        KT = v3(r.take(len(LEVELS) * T), len(LEVELS))
        QT = v3(r.take(len(LEVELS) * T), len(LEVELS))
        Aflat = r.take(TT * (T + P))
        A = v3(Aflat[:, 0:TT * T], TT)
        Adiag = v3(Aflat, TT)[:, :, 0:P]
        Am = r.take(T)
        E = v3(r.take(2 * T), 2)
        KTm = r.take(M)
        assert r.at <= gla_top, (r.at, gla_top)
        Em = Region(first_end).take(TM)
        QTm = Em[:, 0:T]
        r = Region(FREE)
        NB = WORDS - 5400
        r = Region(FREE)
        nsq1 = v3(r.take(KC * TM), KC)
        nstd1 = r.take(TM)
        ninv1 = r.take(TM)
        r = Region(WORDS - 5300)
        nsq = v3(r.take(KC * TM), KC)
        nstd = r.take(TM)
        ninv = r.take(TM)

        r = Region(FREE)
        idx_tok = v3(r.take(3 * T), 3)
        idxT = v3(r.take(3 * T), 3)
        gTh, gTl = r.take(T, f16), r.take(T, f16)
        region_v = r.at
        vraw = v3(r.take(SLOTS * D), SLOTS)
        region_g = r.at
        r = Region(region_v)
        hot_row, hot_slab, hot_high, hot_low = ([v3(r.take(OCT * P, f16), OCT) for _ in range(2)] for _ in range(4))
        assert r.at <= region_g
        r = Region(region_g)
        G = [v3(r.take(P * NT), P) for _ in range(2)]
        act_p = v3(r.take(4 * T), 4)
        r = Region(region_g)
        pq = v3(r.take(2 * T), 2)
        keysT = v3(r.take(2 * PH * P), 2 * PH)
        s_ = [v3(r.take(2 * T), 2) for _ in range(2)]
        s2 = v3(r.take(2 * T), 2)
        ts = v3(r.take(2 * TT * TOP), 2)
        ti = v3(r.take(2 * TT * TOP, u32), 2)
        tif = v3(r.take(2 * TT * TOP), 2)
        cand = v3(r.take(TT * 256), TT)
        cand2 = v3(r.take(TT * 256), TT)
        best = v3(r.take(TT * TOP), TT)
        pos = v3(r.take(TT * TOP, u32), TT)
        posab = v3(r.take(2 * TT * TOP, u32), 2)
        posf = v3(r.take(2 * TT * TOP), 2)
        sel = r.take(TT * 256)
        gsm = r.take(TT * TOP)
        gsum = r.take(16)
        assert r.at <= WORDS
        r = Region(region_g)
        vh = v3(r.take(2 * GRP * D, f16), 2 * GRP)
        vl = v3(r.take(2 * GRP * D, f16), 2 * GRP)
        Ah = v3(r.take(2 * GRP * T, f16), 2 * GRP)
        Al = v3(r.take(2 * GRP * T, f16), 2 * GRP)
        GB = [v3(r.take(GT * GRP * NT), GT) for _ in range(2)]
        act_s = v3(r.take(GRP * T), GRP)
        at_s = v3(r.take(2 * T), 2)

        r = Region(FREE)
        ph_, pl_ = v3(r.take(KC * T, f16), KC), v3(r.take(KC * T, f16), KC)
        yh, yl = v3(r.take(KC * T, f16), KC), v3(r.take(KC * T, f16), KC)
        V2 = v3(r.take(KC * T), KC)
        U2 = v3(r.take(KC * T), KC)
        t2 = r.at
        zp = [r.take(T + 16) for _ in range(2)]
        win = [r.take(T + 16) for _ in range(2)]
        gat = v3(Region(t2).take(2 * T), 2)
        wsT = r.take(D)
        bsp = r.take(D)
        mtmp = v3(r.take(2 * T), 2)
        assert r.at <= WORDS - 5300
        r = Region(FREE)
        ggh, ggl = v3(r.take(FC * T, f16), FC), v3(r.take(FC * T, f16), FC)
        upb = [r.take(T + 2) for _ in range(4)]
        cv = v3(r.take(6 * T), 6)
        prw = v3(r.take(2 * T), 2)
        pth, ptl = v3(r.take(2 * T, f16), 2), v3(r.take(2 * T, f16), 2)
        assert r.at <= WORDS - 5300
        r = Region(FREE)
        pgs = v3(r.take(KC * T), KC)
        yout = v3(r.take(KC * T), KC)
        ptmp = v3(r.take(2 * T), 2)

        consts_in, vecs_in, x_in = sem("consts_in"), sem("vecs_in"), sem("x_in")
        slab_in = [sem(f"slab_in{i}") for i in range(SLOTS)]
        high_cut, low_cut, slab_done = sem("high_cut"), sem("low_cut"), sem("slab_done")
        vslab_in = [sem(f"vslab_in{i}") for i in range(SLOTS)]
        vhigh_cut, vlow_cut, vslab_done = sem("vhigh_cut"), sem("vlow_cut"), sem("vslab_done")
        slab_read = sem("slab_read")
        wz_high, wz_low = sem("wz_high"), sem("wz_low")
        dve_step, act_step, pool_step = sem("dve_step"), sem("act_step"), sem("pool_step")

        def slot(n):
            return n % SLOTS

        gmat = nc.dram_tensor("gate_matrix", [GT, P, NK * NT], f32, kind="Internal").ap()
        early = nc.dram_tensor("early_activations", [EARLY, P, T], f32, kind="Internal").ap()

        class Chain:

            def __init__(self, eng, s):
                self.eng, self.s, self.n, self.off = eng, s, 0, 0

            def link(self, ins):
                ins.then_inc(self.s, 1)
                self.n += 1
                self.eng.wait_ge(self.s, self.off + self.n)

            def enter(self, off):
                self.off, self.first = off, self.n

            def leave(self, per, times):
                assert self.n - self.first == per, (self.n - self.first, per)
                self.n, self.off = self.first + per * times, 0

        dchain = Chain(None, dve_step)

        sq_act, ss_done, std_done = sem("sq_act"), sem("ss_done"), sem("std_done")
        xn_done, xh_done, xl_done = sem("xn_done"), sem("xh_done"), sem("xl_done")
        NORMS = ("ln1", "ln2", "final1", "mixn", "ffnn", "plen", "final2")

        class Norm:

            def __init__(self, name, b):
                self.i = NORMS.index(name)
                self.b = b
                self.w, self.meta = VEC[name], name == "ln1"
                self.cut = name not in ("final1", "final2")
                self.nth = sum(n not in ("final1", "final2") for n in NORMS[:self.i])
                self.cols = TM if self.meta else T
                self.sq = nsq1 if self.meta else xsq if name == "final1" else nsq
                self.std = nstd1 if self.meta else nstd
                self.inv = ninv1 if self.meta else ninv

            def square(self, c):
                nc.scalar.activation(self.sq[:, c, 0:self.cols], X[:, c, 0:self.cols],
                                     ACT.Square).then_inc(sq_act, 1)

            def act(self, act):
                act.wait_ge(ss_done, self.i + 1)
                nc.scalar.activation(self.std[:, 0:self.cols], bank(self.b, self.cols), ACT.Sqrt, bias=EPSC,
                                     scale=1.0 / D).then_inc(std_done, 1)
                if self.cut:
                    for c in range(KC):
                        act.wait_ge(xn_done, self.nth * KC + c + 1)
                        nc.scalar.activation(xh[:, c, 0:self.cols], self.sq[:, c, 0:self.cols],
                                             ACT.Copy).then_inc(xh_done, 1)

            def sum(self, pe, c):
                pe.wait_ge(sq_act, self.i * KC + c + 1)
                last = nc.tensor.matmul(bank(self.b), ones, self.sq[:, c, 0:T], start=c == 0, stop=c == KC - 1)
                if self.meta:
                    last = nc.tensor.matmul(bank(self.b + 1, M), ones, self.sq[:, c, T:TM], start=c == 0,
                                            stop=c == KC - 1)
                if c == KC - 1:
                    last.then_inc(ss_done, 1)

            def dve(self, dve, dst=None, done=None):
                dve.wait_ge(std_done, self.i + 1)
                dchain.link(nc.vector.reciprocal(self.inv[:, 0:self.cols], self.std[:, 0:self.cols]))
                for c in range(KC + 1):
                    if c < KC:
                        o = dst[:, c, 0:T] if dst is not None else self.sq[:, c, 0:self.cols]
                        nc.vector.scalar_tensor_tensor(
                            out=o, in0=X[:, c, 0:self.cols], scalar=vec[:, self.w + c:self.w + c + 1],
                            in1=self.inv[:, 0:self.cols], op0=ALU.mult,
                            op1=ALU.mult).then_inc(xn_done if self.cut else done, 1)
                    if c and self.cut:
                        dve.wait_ge(xh_done, self.nth * KC + c)
                        nc.vector.tensor_tensor(xl[:, c - 1, 0:self.cols], self.sq[:, c - 1, 0:self.cols],
                                                xh[:, c - 1, 0:self.cols], ALU.subtract).then_inc(xl_done, 1)

            def wait_cut(self, pe, c=KC - 1):
                pe.wait_ge(xl_done, self.nth * KC + c + 1)

        EPSC = small[:, 0:1]
        NLAM = small[:, 1:2]
        SUBW = small[:, 2:3]
        LAMP = small[:, 4:6]
        LAME = small[:, 6:8]
        nmx = small[:, 8:12]
        zs = small[:, 12:16]
        rzs = small[:, 16:24]
        vss = small[:, 24:32]
        vrs = small[:, 32:40]
        one = ones[:, 0:1]

        def wait(eng, s, v):
            if not isinstance(v, int) or v > 0:
                eng.wait_ge(s, v)

        def cut_high(act, g, s):
            act.wait_ge(slab_in[s], g * 16 + 16)
            wait(act, slab_done, g * SLOTS + (s + 1 - SLOTS))
            nc.scalar.activation(wh[:, s, :], wraw[:, s, :], ACT.Copy, scale=WS).then_inc(high_cut, 1)

        def cut_high_scaled(act, g, s):
            act.wait_ge(slab_in[s], g * 16 + 16)
            wait(act, slab_done, g * SLOTS + (s + 1 - SLOTS))
            nc.scalar.activation(wh[:, s, :], wraw[:, s, :], ACT.Copy, scale=WS).then_inc(slab_read, 1)
            act.wait_ge(slab_read, g * SLOTS + (s + 1 - LOW_POOL))
            nc.scalar.activation(wraw[:, s, :], wraw[:, s, :], ACT.Copy, scale=WS).then_inc(high_cut, 1)

        def cut_low(dve, g, s):
            dve.wait_ge(high_cut, g * SLOTS + (s + 1))
            nc.vector.scalar_tensor_tensor(out=wl[:, s, :], in0=wraw[:, s, :], scalar=WS, in1=wh[:, s, :],
                                           op0=ALU.mult, op1=ALU.subtract).then_inc(low_cut, 1)

        def cut_low_scaled(pool, g, s):
            pool.wait_ge(high_cut, g * SLOTS + (s + 1))
            nc.gpsimd.tensor_tensor(wl[:, s, :], wraw[:, s, :], wh[:, s, :], ALU.subtract).then_inc(low_cut, 1)

        class Cuts:

            def __init__(self, eng, cut):
                self.eng, self.cut, self.n = eng, cut, 0

            def upto(self, n):
                while self.n <= min(n, N_END - 1):
                    self.cut(self.eng, self.n // SLOTS, slot(self.n))
                    self.n += 1

            def ahead(self, g, s):
                s += SLOTS - 1
                self.cut(self.eng, g + s // SLOTS, s % SLOTS)

        def parts(ps, a_h, a_l, b_h, b_l, first, last):
            nc.tensor.matmul(ps, a_h, b_h, start=first, stop=False)
            nc.tensor.matmul(ps, a_h, b_l, start=False, stop=False)
            return nc.tensor.matmul(ps, a_l, b_h, start=False, stop=last)

        def wslab(sl, c, n=P):
            return wh[:, sl, c * n:(c + 1) * n], wl[:, sl, c * n:(c + 1) * n]

        def chunk(pe, n, sl, ps, sh=None, slo=None, kc=KC, meta=None, norm=None, half=None):
            sh = xh if sh is None else sh
            slo = xl if slo is None else slo
            pe.wait_ge(low_cut, n + 1)
            for c in range(kc) if half is None else range(half * kc // 2, (half + 1) * kc // 2):
                if norm is not None:
                    norm.wait_cut(pe, c)
                a = wslab(sl, c)
                last = parts(ps, *a, sh[:, c, 0:T], slo[:, c, 0:T], c == 0, c == kc - 1)
                if meta is not None:
                    last = parts(meta, *a, sh[:, c, T:TM], slo[:, c, T:TM], c == 0, c == kc - 1)
            if half != 0:
                last.then_inc(slab_done, 1)

        proj_out, proj_meta_out = sem("proj_out"), sem("proj_meta_out")
        rope_in, rope_mul, rope_out = sem("rope_in"), sem("rope_mul"), sem("rope_out")
        values_out = sem("values_out")
        z_done, z_out, gate_mm, gate_abs, gate_pre, gate_ln, gate_out = (
            sem("z_done"), sem("z_out"), sem("gate_mm"), sem("gate_abs"), sem("gate_pre"), sem("gate_ln"),
            sem("gate_out"))
        sig_out, silu_out = sem("sig_out"), sem("silu_out")
        lam_prod, lam_sum, lam_exp, lam_out = sem("lam_prod"), sem("lam_sum"), sem("lam_exp"), sem("lam_out")
        score_done, max_done, exp_done, diff_done = (sem("score_done"), sem("max_done"), sem("exp_done"),
                                                     sem("diff_done"))
        turn_done, turn_out, av_done, av_out = sem("turn_done"), sem("turn_out"), sem("av_done"), sem("av_out")
        osq_out, oss_done, ostd_out, mixh_out, mixl_out = (sem("osq_out"), sem("oss_done"), sem("ostd_out"),
                                                           sem("mixh_out"), sem("mixl_out"))
        zeroed, e_in, e_exp, kt_out, qt_out, lev_done, lev_out = (
            sem("zeroed"), sem("e_in"), sem("e_exp"), sem("kt_out"), sem("qt_out"), sem("lev_done"),
            sem("lev_out"))
        em_in, em_exp, ktm_out, wide_done, wide_out, gav_done, gav_out = (
            sem("em_in"), sem("em_exp"), sem("ktm_out"), sem("wide_done"), sem("wide_out"), sem("gav_done"),
            sem("gav_out"))
        res_out = sem("res_out")
        NL = len(LEVELS)
        NS = len(SMALL)
        keys_in, pq_out, s_done, s_out, head_done, gsub_out, gexp_out = (
            sem("keys_in"), sem("pq_out"), sem("s_done"), sem("s_out"), sem("head_done"), sem("gsub_out"),
            sem("gexp_out"))
        idx_turned, idxT_out = sem("idx_turned"), sem("idxT_out")
        hot_row_out, hot_slab_out, hot_gated, g_done, g_out = (sem("hot_row_out"), sem("hot_slab_out"),
                                                               sem("hot_gated"), sem("g_done"), sem("g_out"))
        gates_cut = sem("gates_cut")
        act_stored = [sem(f"act_stored{i}") for i in range(4)]
        act_in = [sem(f"act_in{i}") for i in range(GRP)]
        g_stored, g_in = [sem(f"g_stored{i}") for i in range(2)], [sem(f"g_in{i}") for i in range(2)]
        gelu_out, gated_out, a_cut, b_done, acc_out = (sem("gelu_out"), sem("gated_out"), sem("a_cut"),
                                                       sem("b_done"), sem("acc_out"))
        final1_out = sem("final1_out")
        pads, small_in, masked = sem("pads"), sem("small_in"), sem("masked")
        zpool_out, pool_cut, y_cut = sem("zpool_out"), sem("pool_cut"), sem("y_cut")
        v_out, vsq_out, vsum_out, vstd_out, v_normed = (sem("v_out"), sem("vsq_out"), sem("vsum_out"),
                                                        sem("vstd_out"), sem("v_normed"))
        u_out, mix_done, mix_read, sgu_cut = sem("u_out"), sem("mix_done"), sem("mix_read"), sem("sgu_cut")
        gsig_out, branch_out, m_cut, res2_out = (sem("gsig_out"), sem("branch_out"), sem("m_cut"),
                                                 sem("res2_out"))
        up_out, conv_out, cgelu_out, ffn_cut = (sem("up_out"), sem("conv_out"),
                                                           sem("cgelu_out"), sem("ffn_cut"))
        down_out, p_in, p_high, p_low = (sem("down_out"), sem("p_in"),
                                                    sem("p_high"), sem("p_low"))
        psig_out, ple_done, ple_out, y_out, stored = (sem("psig_out"), sem("ple_done"), sem("ple_out"),
                                                      sem("y_out"), sem("stored"))

        block = ctx.enter_context(nc.Block())

        @block.sync
        def _(sp):
            sp.dma_start(X[:, :, 0:T], io["xT"]).then_inc(x_in, 16)
            sp.dma_start(X[:, :, T:TM], io["metaT"]).then_inc(x_in, 16)
            sp.dma_start(ones, io["ones"]).then_inc(x_in, 16)
            sp.dma_start(vec, io["vec"]).then_inc(vecs_in, 16)
            for s in range(SLOTS):
                sp.dma_start(wraw[:, s, :], io["w"][s]).then_inc(slab_in[s], 16)
            for dst, name in ((ident, "ident"), (iota, "iota"), (perm, "perm"), (masks, "masks"), (ropec, "ropec"),
                              (ropes, "ropes"), (icnt, "icnt"), (io16, "io16"), (w2[0:32], "w2"), (wz, "wz")):
                sp.dma_start(dst, io[name]).then_inc(consts_in, 16)

            def slabs(lo, hi):
                with sp.Fori(lo // SLOTS, hi // SLOTS) as g:
                    for s in range(SLOTS):
                        sp.wait_ge(low_cut, g * SLOTS + (s + 1 - SLOTS))
                        sp.dma_start(wraw[:, s, :], io["w"][bass.ds(g * SLOTS + s, 1)].rearrange(
                            "a p n -> p (a n)")).then_inc(slab_in[s], 16)

            slabs(SLOTS, N_PQ + SLOTS)
            sp.wait_ge(res_out, KC)
            sp.dma_start(keysT, io["keysT"]).then_inc(keys_in, 16)
            slabs(N_PQ + SLOTS, N_U + EARLY + SLOTS)
            for s in g_stored:
                sp.wait_ge(s, GT // 2 * 16)
            for s in act_stored:
                sp.wait_ge(s, EARLY // 4 * 16)

            def load_group(g, par, inputs=True):
                wait(sp, gated_out, (g - 1) * GRP)
                sp.dma_start(GB[par], gmat[:, :, bass.ds(g * (GRP * NT), GRP * NT)].rearrange(
                    "t p n -> p t n")).then_inc(g_in[par], 16)
                for s in range(GRP):
                    wait(sp, vlow_cut, g * GRP + (s + 1 - GRP))
                    sp.dma_start(vraw[:, s, :], io["v"][bass.ds(g * GRP + s, 1)].rearrange(
                        "a p n -> p (a n)")).then_inc(vslab_in[s], 16)
                    if inputs:
                        n = g * GRP + (N_U + GRP + s)
                        sp.wait_ge(low_cut, n - (SLOTS - 1))
                        sp.dma_start(wraw[:, s, :], io["w"][bass.ds(n, 1)].rearrange(
                            "a p n -> p (a n)")).then_inc(slab_in[s], 16)
                    else:
                        wait(sp, gated_out, g * GRP + (s - 3))
                        sp.dma_start(act_s[:, s, :], early[bass.ds(g * GRP + s, 1)].rearrange(
                            "a p n -> p (a n)")).then_inc(act_in[s], 16)

            load_group(0, 0, inputs=False)
            load_group(1, 1, inputs=False)
            with sp.Fori(1, EG // 2) as o:
                load_group(o * 2, 0, inputs=False)
                load_group(o * 2 + 1, 1, inputs=False)
            load_group(EG - 1, 0, inputs=False)
            load_group(EG, 1)
            with sp.Fori(EG // 2 + 1, GROUPS // 2) as o:
                load_group(o * 2, 0)
                load_group(o * 2 + 1, 1)
            sp.wait_ge(acc_out, GROUPS * KC)
            sp.wait_ge(final1_out, KC)
            sp.dma_start(wsT, io["wsT"]).then_inc(small_in, 16)
            sp.dma_start(bsp, io["bsp"].partition_broadcast(P)).then_inc(small_in, 16)
            slabs(N_POOL + SLOTS, N_UP + SLOTS)
            sp.wait_ge(res2_out, KC)
            sp.dma_start(prw, io["pT"]).then_inc(p_in, 16)
            slabs(N_UP + SLOTS, N_END)
            for c in range(KC):
                sp.wait_ge(y_out, c + 1)
                sp.dma_start(out[:, c, :], yout[:, c, :]).then_inc(stored, 16)
            sp.wait_ge(stored, 16 * KC)

        @block.tensor
        def _(pe):
            pe.wait_ge(x_in, 48)
            n1 = Norm("ln1", 0)
            for c in range(KC):
                n1.sum(pe, c)
            pe.wait_ge(lam_prod, 1)
            nc.tensor.matmul(bank(2, 2), ones[0:DH, :], LAMP[0:DH, :], start=True, stop=True).then_inc(lam_sum, 1)
            pe.wait_ge(consts_in, 160)
            pe.wait_ge(std_done, 1)
            pe.wait_ge(lam_exp, 1)
            def rope_swap(n):
                pe.wait_ge(rope_in, n + 1)
                src = q[:, n, :] if n < HEADS else k[:, n - HEADS, 0:T]
                if n >= 1:
                    pe.wait_ge(rope_mul, n)
                last = nc.tensor.matmul(bank(6), perm, src, start=True, stop=True)
                if n >= HEADS:
                    last = nc.tensor.matmul(bank(7, M), perm, k[:, n - HEADS, T:TM], start=True, stop=True)
                last.then_inc(rope_out, 1)

            for n in range(N_Q, N_V):
                if n >= 4:
                    pe.wait_ge(rope_in, n - 3 if n < 6 else n - 1)
                chunk(pe, n, slot(n), bank(n % 4), meta=bank(4 + n % 2, M) if n >= N_K else None,
                      norm=n1 if n == N_Q else None)
                if n >= 1:
                    rope_swap(n - 1)
            rope_swap(N_V - 1)
            for part in range(2):
                if part == 0:
                    pe.wait_ge(rope_in, 8)
                else:
                    pe.wait_ge(values_out, 5)
                for g in range(4):
                    n = N_V + 4 * part + g
                    pe.wait_ge(low_cut, n + 1)
                    for c in range(2):
                        w_h, w_l = wslab(slot(n), c, 512)
                        for t in range(5):
                            cols = slice(t * P, (t + 1) * P) if t < TT else slice(T, TM)
                            last = parts(psum[0:P if t < TT else M, t * 512:(t + 1) * 512],
                                         xh[:, 2 * g + c, cols], xl[:, 2 * g + c, cols], w_h, w_l,
                                         g == 0 and c == 0, g == 3 and c == 1)
                    last.then_inc(slab_done, 1)
            pe.wait_ge(values_out, 10)
            for n in range(N_GQ, N_GR):
                chunk(pe, n, slot(n), bank(n % 4), meta=bank(4 + n % 2, M) if n >= N_GK else None)
            pe.wait_ge(wz_low, 1)
            for c in range(KC):
                a = wzh[:, c, :], wzl[:, c, :]
                parts(psum[0:32, 6 * 512:7 * 512], *a, xh[:, c, 0:T], xl[:, c, 0:T], c == 0, c == KC - 1)
                last = parts(psum[0:32, 7 * 512:7 * 512 + M], *a, xh[:, c, T:TM], xl[:, c, T:TM], c == 0,
                             c == KC - 1)
            last.then_inc(z_done, 1)
            pe.wait_ge(proj_out, 4)
            for n in range(N_GR, N_WO):
                chunk(pe, n, slot(n), bank(n % 4))
            pe.wait_ge(z_out, 1)
            for h in range(HEADS):
                if h == 0:
                    pe.wait_ge(z_out, 2)
                if h >= 1:
                    pe.wait_ge(gate_mm, h)
                nc.tensor.matmul(bank(4), w2[0:32, h, :], z32[0:32, 0:T], start=True, stop=True)
                nc.tensor.matmul(bank(5, M), w2[0:32, h, :], z32[0:32, T:TM], start=True,
                                 stop=True).then_inc(gate_abs, 1)

            def scores(turn):
                h, t = divmod(turn, TT)
                for c in range(2):
                    u = 2 * turn + c
                    if u >= 2:
                        pe.wait_ge(exp_done, u - 1)
                    rows = slice(DH * c, DH * (c + 1))
                    a = q[rows, h, t * P:(t + 1) * P]
                    nc.tensor.matmul(bank(2 * c), a, k[rows, h, 0:T], start=True, stop=True)
                    nc.tensor.matmul(bank(2 * c + 1, M), a, k[rows, h, T:TM], start=True,
                                     stop=True).then_inc(score_done, 1)

            def turn_over(turn):
                par = turn % 2
                pe.wait_ge(diff_done, turn + 1)
                if turn >= 2:
                    pe.wait_ge(turn_out, turn - 1)
                for j in range(TT):
                    nc.tensor.transpose(bank(4 + par, P, j * P), pa[:, par, j * P:(j + 1) * P], ident)
                if turn >= 1:
                    pe.wait_ge(turn_out, turn)
                nc.tensor.transpose(psum[0:M, 6 * 512 + par * P:6 * 512 + (par + 1) * P],
                                    pa[:, par, T:TM], ident).then_inc(turn_done, 1)

            def mix_values(h):
                pe.wait_ge(turn_out, TT * (h + 1))
                if h >= 1:
                    pe.wait_ge(av_out, h)
                cols = slice(h * P, (h + 1) * P)
                for j in range(TT):
                    nc.tensor.matmul(bank(7), dv[:, j, cols], aT[:, j, :], start=j == 0, stop=False)
                nc.tensor.matmul(bank(7), dv[0:M, TT, cols], aT[0:M, TT, :], start=False,
                                 stop=True).then_inc(av_done, 1)

            pe.wait_ge(silu_out, HEADS)
            pe.wait_ge(gate_out, HEADS)
            for turn in range(HEADS * TT):
                scores(turn)
                if turn >= 1:
                    turn_over(turn - 1)
                    if turn % TT == 0:
                        mix_values(turn // TT - 1)
            turn_over(HEADS * TT - 1)
            mix_values(HEADS - 1)
            for h in range(HEADS):
                pe.wait_ge(osq_out, h + 1)
                nc.tensor.matmul(bank(h), ones, aT[:, h, :], start=True, stop=True).then_inc(oss_done, 1)

            units = [(h, li) for h in range(HEADS) for li in range(-1, NS + 1)]
            for u, (h, li) in enumerate(units):
                b = 4 + u % 3
                if u >= 3:
                    pe.wait_ge(lev_out, u - 2)
                if u == 0:
                    pe.wait_ge(av_out, HEADS)
                    pe.wait_ge(turn_out, HEADS * TT)
                if li >= 0:
                    pe.wait_ge(kt_out, 2 * (h * NL + li + 1))
                    pe.wait_ge(qt_out, 2 * (h * NL + li + 1))
                for j in range(TT):
                    jt = slice(j * P, (j + 1) * P)
                    i = j if li < NS else j ^ 1
                    it = slice(i * P, (i + 1) * P)
                    if li < 0:
                        last = nc.tensor.matmul(bank(b, P, j * P), gk[:, h, jt], gq[:, h, it], start=True,
                                                stop=True)
                    else:
                        last = nc.tensor.matmul(bank(b, P, j * P), KT[:, li, jt], QT[:, li, it], start=True,
                                                stop=True)
                last.then_inc(lev_done, 1)
                if li == NS:
                    pe.wait_ge(kt_out, 2 * (h * NL + NL))
                    pe.wait_ge(qt_out, 2 * (h * NL + NL))
                    if h == 0:
                        pe.wait_ge(ostd_out, HEADS)
                    else:
                        pe.wait_ge(wide_out, 3 * h)
                    for j in range(TT):
                        off = T // 2 if j < 2 else 0
                        last = nc.tensor.matmul(bank(j // 2, 256, 256 * (j % 2)),
                                                KT[:, NL - 1, j * P:(j + 1) * P],
                                                QT[:, NL - 1, off:off + 256], start=True, stop=True)
                    pe.wait_ge(ktm_out, 2 * (h + 1))
                    nc.tensor.matmul(psum[0:M, 2 * 512:3 * 512], KTm[0:DH, :], QTm[0:DH, :], start=True,
                                     stop=True).then_inc(wide_done, 1)
                    pe.wait_ge(lev_out, u + 1)
                    pe.wait_ge(wide_out, 3 * (h + 1))
                    if h >= 1:
                        pe.wait_ge(gav_out, h)
                    cols = slice(h * P, (h + 1) * P)
                    for j in range(TT):
                        nc.tensor.matmul(bank(3), gv[:, j, cols], A[:, j, :], start=j == 0, stop=False)
                    nc.tensor.matmul(bank(3), gv[0:M, TT, cols], Am[0:M, :], start=False,
                                     stop=True).then_inc(gav_done, 1)
            for h in range(HEADS):
                pe.wait_ge(osq_out, HEADS + h + 1)
                if h == 3:
                    pe.wait_ge(gav_out, HEADS)
                nc.tensor.matmul(bank(h), ones, A[:, h, :], start=True, stop=True).then_inc(oss_done, 1)

            pe.wait_ge(mixl_out, 2)
            pe.wait_ge(ostd_out, 2 * HEADS)
            n2 = Norm("ln2", 4)
            for n in range(N_WO, N_PQ):
                i = n - N_WO
                if i >= 4:
                    pe.wait_ge(res_out, i - 3)
                chunk(pe, n, slot(n), bank(n % 4))
                if i:
                    n2.sum(pe, i - 1)
            n2.sum(pe, KC - 1)

            pe.wait_ge(std_done, 2)
            pe.wait_ge(keys_in, 16)

            def key_scores(m, side):
                pe.wait_ge(pq_out, m + 1)
                wait(pe, s_out, m - 1)
                for t in range(TT):
                    last = nc.tensor.matmul(bank(2 + side, P, t * P), pq[:, side, t * P:(t + 1) * P],
                                            keysT[:, bass.ds(m, 1), :].rearrange("p a n -> p (a n)"),
                                            start=True, stop=True)
                last.then_inc(s_done, 1)

            def expert_input(e, n, s, b, half=None):
                wait(pe, gelu_out, e - 1)
                chunk(pe, n, s, bank(b), half=half)

            def query_turn(i):
                for hp in range(2):
                    m, n = i * 4 + 2 * hp, i * (2 * SLOTS) + (N_PQ + SLOTS * hp)
                    for side in range(2):
                        wait(pe, pq_out, m + (side - 1))
                        chunk(pe, n + side, side, bank(side),
                              norm=n2 if isinstance(i, int) and hp + side == 0 else None)
                    key_scores(m, 0)
                    expert_input(m, n + 2, 2, 4)
                    key_scores(m + 1, 1)
                    expert_input(m + 1, n + 3, 3, 5)

            query_turn(0)
            with pe.Fori(1, PH // 2) as i:
                query_turn(i)

            for e in range(WOVEN, BEHIND):
                expert_input(e, N_U + e, e % 4, 4 + e % 2)

            pe.wait_ge(head_done, PH)
            pe.wait_ge(s_out, 2 * PH)
            for v, b in enumerate(TURN_BANKS):
                for t in range(TT):
                    last = nc.tensor.transpose(bank(b, P, t * P), idx_tok[:, v, t * P:(t + 1) * P], ident)
                last.then_inc(idx_turned, 1)
            pe.wait_ge(pq_out, 2 * PH)

            def gate_octet(e, b):
                pe.wait_ge(hot_row_out, e + 1)
                pe.wait_ge(hot_gated, e + 1)
                for half in range(2):
                    wait(pe, g_out, e * 2 + (half - 3))
                    for tk in range(4 * half, 4 * half + 4):
                        ps = bank(2 * b + half, P, tk % 4 * P)
                        nc.tensor.matmul(ps, hot_row[b][:, tk, :], hot_high[b][:, tk, :], start=True, stop=False)
                        last = nc.tensor.matmul(ps, hot_row[b][:, tk, :], hot_low[b][:, tk, :], start=False,
                                                stop=True)
                    last.then_inc(g_done, 1)

            def tile_turn(t, octets=True):
                for s in range(SLOTS):
                    for half in range(2):
                        expert_input(t * SLOTS + (BEHIND + s), t * SLOTS + (N_U + BEHIND + s), s, 4 + s % 2,
                                     half)
                        if octets:
                            gate_octet(t * OCT + (2 * s + half), half)

            tile_turn(0)
            with pe.Fori(1, GT) as t:
                tile_turn(t)
            tile_turn(GT, octets=False)

            pe.wait_ge(g_out, T // 4)

            def expert_group(g, par, inputs=True, outputs=True):
                gp, pp = g - 1, 1 - par
                for s in range(GRP):
                    if inputs:
                        expert_input(g * GRP + s, g * GRP + (N_U + s), s, s % 2)
                    if outputs:
                        if s == 0:
                            pe.wait_ge(a_cut, gp * GRP + GRP)
                            pe.wait_ge(vlow_cut, gp * GRP + GRP)
                        for c in (2 * s, 2 * s + 1):
                            wait(pe, acc_out, gp * KC + (c - 3))
                            for t in range(GRP):
                                x = pp * GRP + t
                                cols = slice(c * P, (c + 1) * P)
                                last = parts(bank(2 + c % 4), vh[:, x, cols], vl[:, x, cols], Ah[:, x, :],
                                             Al[:, x, :], t == 0, t == GRP - 1)
                            last.then_inc(b_done, 1)

            pe.wait_ge(gelu_out, EARLY)
            pe.wait_ge(idxT_out, 3)
            expert_group(1, 1, inputs=False)
            expert_group(2, 0, inputs=False)
            with pe.Fori(1, EG // 2) as o:
                expert_group(o * 2 + 1, 1, inputs=False)
                expert_group(o * 2 + 2, 0, inputs=False)
            with pe.Fori(EG // 2, GROUPS // 2 - 1) as o:
                expert_group(o * 2 + 1, 1)
                expert_group(o * 2 + 2, 0)
            expert_group(GROUPS - 1, 1)
            expert_group(GROUPS, 0, inputs=False)
            n3 = Norm("final1", 6)
            for c in range(KC):
                n3.sum(pe, c)

            n4 = Norm("mixn", 7)
            for c in range(KC):
                n4.sum(pe, c)
            pe.wait_ge(std_done, n4.i + 1)
            for n in range(N_POOL, N_WP):
                wait(pe, zpool_out, n - N_POOL - 3)
                chunk(pe, n, slot(n), bank(n % 4), norm=n4 if n == N_POOL else None)
            pe.wait_ge(zpool_out, KC)
            for n in range(N_WP, N_SV):
                g = n - N_WP
                pe.wait_ge(low_cut, n + 1)
                pe.wait_ge(pool_cut, 2 * g + 2)
                for o in range(2):
                    c = 2 * g + o
                    wait(pe, y_cut, c - 3)
                    for kk in range(2):
                        last = parts(bank(c % 4), *wslab(slot(n), 2 * o + kk), ph_[:, 2 * g + kk, :],
                                     pl_[:, 2 * g + kk, :], kk == 0, kk == 1)
                last.then_inc(slab_done, 1)
            for half in range(2):
                if half == 0:
                    pe.wait_ge(y_cut, KC)
                for g in range(4):
                    n = N_SV + 4 * half + g
                    pe.wait_ge(low_cut, n + 1)
                    for c in range(2):
                        w_h, w_l = wslab(slot(n), c, 512)
                        for t in range(TT):
                            cols = slice(t * P, (t + 1) * P)
                            last = parts(bank(4 * half + t), xh[:, 2 * g + c, cols], xl[:, 2 * g + c, cols],
                                         w_h, w_l, g == 0 and c == 0, g == 3 and c == 1)
                    last.then_inc(slab_done, 1)
            pe.wait_ge(v_out, 2 * TT)
            for n in range(N_SU, N_GA):
                h = n - N_SU
                wait(pe, u_out, h - 3)
                chunk(pe, n, slot(n), bank(n % 4))
                if h == 0:
                    pe.wait_ge(masked, 1)
                    pe.wait_ge(v_normed, TT)
                wait(pe, mix_read, h - 1)
                for t in range(TT):
                    last = nc.tensor.matmul(bank(4 + h % 2, P, t * P),
                                            V2[:, 2 * t + h // 4, h % 4 * P:(h % 4 + 1) * P],
                                            wsT[:, h * P:(h + 1) * P], start=True, stop=True)
                last.then_inc(mix_done, 1)
            pe.wait_ge(u_out, KC)
            for n in range(N_GA, N_WO2):
                i = n - N_GA
                b = i // 2
                if i % 2 == 0:
                    wait(pe, gsig_out, b - 1)
                    chunk(pe, n, slot(n), bank(n % 4))
                else:
                    if b == KC:
                        pe.wait_ge(sgu_cut, KC)
                    wait(pe, branch_out, b - 1)
                    a = (yh, yl) if b < KC else (ph_, pl_)
                    chunk(pe, n, slot(n), bank(n % 4), *a)
            pe.wait_ge(branch_out, 2 * KC)
            pe.wait_ge(m_cut, KC)
            n5 = Norm("ffnn", 7)
            for n in range(N_WO2, N_UP):
                c = n - N_WO2
                wait(pe, res2_out, c - 3)
                chunk(pe, n, slot(n), bank(n % 4), yh, yl)
                if c:
                    n5.sum(pe, c - 1)
            n5.sum(pe, KC - 1)

            pe.wait_ge(std_done, n5.i + 1)

            def up_turn(i):
                for s in range(SLOTS):
                    wait(pe, up_out, i * SLOTS + (s - 3))
                    chunk(pe, i * SLOTS + (N_UP + s), s, bank(s),
                          norm=n5 if isinstance(i, int) and s == 0 else None)

            up_turn(0)
            with pe.Fori(1, FC // 2) as i:
                up_turn(i)

            def down(f, s, first=False, last=False):
                pe.wait_ge(low_cut, f + (N_DN + 1))
                fi = bass.ds(f, 1)
                b_h, b_l = (x[:, fi, :].rearrange("p a n -> p (a n)") for x in (ggh, ggl))
                for c in range(KC):
                    ins = parts(bank(c), *wslab(s, c), b_h, b_l, first, last)
                ins.then_inc(slab_done, 1)

            pe.wait_ge(up_out, 2 * FC)
            pe.wait_ge(ffn_cut, FC)
            for f in range(SLOTS):
                down(f, f, first=f == 0)
            with pe.Fori(1, FC // SLOTS) as i:
                for s in range(SLOTS):
                    down(i * SLOTS + s, s)
            for f in range(FC // SLOTS * SLOTS, FC):
                down(f, f % SLOTS, last=f == FC - 1)

            n6 = Norm("plen", 0)
            for c in range(KC):
                n6.sum(pe, c)
            pe.wait_ge(std_done, n6.i + 1)
            pe.wait_ge(p_low, 1)
            for n in range(N_PG, N_PP):
                wait(pe, psig_out, n - N_PG - 3)
                chunk(pe, n, slot(n), bank(n % 4), norm=n6 if n == N_PG else None)
            n7 = Norm("final2", 0)
            pe.wait_ge(psig_out, KC)
            for n in range(N_PP, N_END):
                pe.wait_ge(low_cut, n + 1)
                for o in range(4):
                    c = 4 * (n - N_PP) + o
                    wait(pe, ple_out, c - 3)
                    for kk in range(2):
                        last = parts(bank(4 + c % 4), *wslab(slot(n), 2 * o + kk), pth[:, kk, :],
                                     ptl[:, kk, :], kk == 0, kk == 1)
                    last.then_inc(ple_done, 1)
                    if c >= 2:
                        n7.sum(pe, c - 2)
            n7.sum(pe, KC - 2)
            n7.sum(pe, KC - 1)

        @block.scalar
        def _(act):
            chain = Chain(act, act_step)
            cuts = Cuts(act, cut_high)
            act.wait_ge(pool_step, 1)
            n1 = Norm("ln1", 0)
            act.wait_ge(x_in, 48)
            for c in range(KC):
                n1.square(c)
            n1.act(act)
            act.wait_ge(lam_sum, 1)
            nc.scalar.activation(LAME, bank(2, 2), ACT.Exp).then_inc(lam_exp, 1)
            cuts.upto(2)
            for n in range(N_Q, N_V):
                cuts.upto(n + 3)
                act.wait_ge(slab_done, n + 1)
                if n < N_K:
                    nc.scalar.activation(q[:, n, :], bank(n % 4), ACT.Copy, scale=ISW / 8).then_inc(rope_in, 1)
                else:
                    nc.scalar.activation(k[:, n - N_K, T:TM], bank(4 + n % 2, M), ACT.Copy, scale=ISW)
                    nc.scalar.activation(k[:, n - N_K, 0:T], bank(n % 4), ACT.Copy, scale=ISW).then_inc(rope_in, 1)
            act.wait_ge(consts_in, 160)
            nc.scalar.activation(wzh.rearrange("p a b -> p (a b)"), wz, ACT.Copy, scale=WS).then_inc(wz_high, 1)
            for part in range(2):
                cuts.upto(N_V + 4 * part + 7)
                act.wait_ge(slab_done, N_V + 4 * part + 4)
                dst = (dv, gv)[part]
                for t in range(5):
                    rows = P if t < TT else M
                    nc.scalar.activation(dst[0:rows, t, :], psum[0:rows, t * 512:(t + 1) * 512], ACT.Copy,
                                         scale=ISW).then_inc(values_out, 1)
            for n in range(N_GQ, N_GR):
                cuts.upto(n + 3)
                act.wait_ge(slab_done, n + 1)
                for c in range(2):
                    rows = slice(DH * c, DH * (c + 1))
                    for half in range(2):
                        d = slice(DH * half, DH * (half + 1))
                        if n < N_GK:
                            last = nc.scalar.activation(gq[d, 2 * (n - N_GQ) + c, :],
                                                        psum[rows, (n % 4) * 512:(n % 4 + 1) * 512], ACT.Copy,
                                                        scale=ISW / 8)
                        else:
                            h = 2 * (n - N_GK) + c
                            nc.scalar.activation(gk[d, h, T:TM],
                                                 bank(4 + n % 2, M)[rows],
                                                 ACT.Copy, scale=ISW)
                            last = nc.scalar.activation(gk[d, h, 0:T],
                                                        psum[rows, (n % 4) * 512:(n % 4 + 1) * 512], ACT.Copy,
                                                        scale=ISW)
                last.then_inc(proj_out, 1)
            act.wait_ge(z_done, 1)
            nc.scalar.activation(z32[0:32, 0:T], psum[0:32, 6 * 512:7 * 512], ACT.Copy, scale=ISW).then_inc(z_out, 1)
            nc.scalar.activation(z32[0:32, T:TM], psum[0:32, 7 * 512:7 * 512 + M], ACT.Copy,
                                 scale=ISW).then_inc(z_out, 1)
            for n in range(N_GR, N_WO):
                cuts.upto(n + 3)
                act.wait_ge(slab_done, n + 1)
                nc.scalar.activation(sgr[:, n - N_GR, :], bank(n % 4), ACT.Sigmoid, scale=ISW).then_inc(sig_out, 1)
            for h in range(HEADS):
                act.wait_ge(gate_abs, h + 1)
                bcol = vec[:, VEC["gateb"] + h:VEC["gateb"] + h + 1]
                nc.scalar.activation(B[:, h, 0:T], bank(4), ACT.Identity, bias=bcol)
                nc.scalar.activation(B[:, h, T:TM], bank(5, M), ACT.Identity, bias=bcol).then_inc(gate_mm, 1)
            act.wait_ge(gate_mm, HEADS)
            chain.link(nc.scalar.activation(gtmp, B, ACT.Abs))
            chain.link(nc.scalar.activation(gtmp, gtmp, ACT.Exp, scale=-1.0))
            nc.scalar.activation(gtmp, gtmp, ACT.Ln, bias=one).then_inc(gate_ln, 1)

            def turn_copy(turn):
                par, (h, t) = turn % 2, divmod(turn, TT)
                act.wait_ge(turn_done, turn + 1)
                if h >= 1 and t == 0:
                    act.wait_ge(av_done, h)
                nc.scalar.activation(aT[:, 0:TT, t * P:(t + 1) * P], v3(bank(4 + par), TT), ACT.Copy)
                nc.scalar.activation(aT[0:M, TT, t * P:(t + 1) * P],
                                     psum[0:M, 6 * 512 + par * P:6 * 512 + (par + 1) * P],
                                     ACT.Copy).then_inc(turn_out, 1)

            def head_out(h):
                act.wait_ge(av_done, h + 1)
                nc.scalar.activation(otmp[:, h, :], bank(7), ACT.Copy).then_inc(av_out, 1)

            for turn in range(HEADS * TT):
                for c in range(2):
                    u = 2 * turn + c
                    act.wait_ge(max_done, u + 1)
                    if turn >= 2:
                        act.wait_ge(diff_done, turn - 1)
                    nc.scalar.activation(pr[:, u % 4, :], psum[:, 2 * c * 512:2 * c * 512 + TM], ACT.Exp,
                                         bias=nmx[:, u % 4:u % 4 + 1],
                                         accum_out=zs[:, u % 4:u % 4 + 1]).then_inc(exp_done, 1)
                if turn >= 1:
                    turn_copy(turn - 1)
                    if turn % TT == 0:
                        head_out(turn // TT - 1)
            turn_copy(HEADS * TT - 1)
            head_out(HEADS - 1)

            def head_norms(lo, sqs, stds):
                for h in range(HEADS):
                    nc.scalar.activation(sqs[:, h, :], otmp[:, h, :], ACT.Square).then_inc(osq_out, 1)
                for h in range(HEADS):
                    act.wait_ge(oss_done, lo + h + 1)
                    nc.scalar.activation(stds[:, h, :], bank(h), ACT.Sqrt, bias=EPSC,
                                         scale=1.0 / P).then_inc(ostd_out, 1)

            act.wait_ge(av_out, HEADS)
            act.wait_ge(exp_done, 2 * HEADS * TT)
            head_norms(0, aT, v3(pr.rearrange("p a b -> p (a b)")[:, 0:4 * T], 4))

            for h in range(HEADS):
                for li in range(NL):
                    u = h * NL + li
                    act.wait_ge(e_in, 2 * (u + 1))
                    nc.scalar.activation(E[:, u % 2, :], E[:, u % 2, :], ACT.Exp,
                                         scale=1.0 / 16).then_inc(e_exp, 1)
                act.wait_ge(em_in, h + 1)
                nc.scalar.activation(Em[0:DH, T:TM], Em[0:DH, T:TM], ACT.Exp, scale=1.0 / 16)
                nc.scalar.activation(Em[0:DH, 0:T], B[0:DH, h, 0:T], ACT.Exp,
                                     scale=1.0 / 16).then_inc(em_exp, 1)
                act.wait_ge(wide_done, h + 1)
                if h >= 1:
                    act.wait_ge(gav_done, h)
                for half in range(2):
                    off = T // 2 if half == 0 else 0
                    nc.scalar.activation(A[:, 2 * half:2 * half + 2, off:off + 256], v3(bank(half), 2),
                                         ACT.Copy).then_inc(wide_out, 1)
                nc.scalar.activation(Am[0:M, :], psum[0:M, 2 * 512:3 * 512], ACT.Copy).then_inc(wide_out, 1)
                act.wait_ge(gav_done, h + 1)
                if h == 0:
                    act.wait_ge(mixl_out, 1)
                nc.scalar.activation(otmp[:, h, :], bank(3), ACT.Copy).then_inc(gav_out, 1)
            act.wait_ge(gav_out, HEADS)
            head_norms(HEADS, A, KT[:, 0:4, :])
            n2 = Norm("ln2", 4)
            for n in range(N_WO, N_PQ):
                cuts.upto(n + 3)
                act.wait_ge(res_out, n - N_WO + 1)
                n2.square(n - N_WO)

            n2.act(act)

            def query_out(m, n, side):
                act.wait_ge(slab_done, n + 1)
                wait(act, s_done, m - 1)
                nc.scalar.activation(pq[:, side, :], bank(side), ACT.Copy, scale=ISW).then_inc(pq_out, 1)

            def scores_out(m, head, hp, side):
                act.wait_ge(s_done, m + 1)
                wait(act, head_done, head - 1)
                nc.scalar.activation(s_[hp][:, side, :], bank(2 + side), ACT.Copy).then_inc(s_out, 1)

            def gate_exp(head):
                act.wait_ge(gsub_out, head + 1)
                nc.scalar.activation(gsm, gsm, ACT.Exp).then_inc(gexp_out, 1)

            def store_early(e, x):
                act.wait_ge(gelu_out, e + 1)
                act.dma_start(early[bass.ds(e, 1)].rearrange("a p n -> p (a n)"),
                              act_p[:, x, :]).then_inc(act_stored[x], 16)

            def early_gelu(e, n, x, b, k):
                if not isinstance(e, int) or e > 0:
                    store_early(e - 1, (x - 1) % 4)
                act.wait_ge(slab_done, n + 1)
                wait(act, act_stored[x], k * 16)
                nc.scalar.activation(act_p[:, x, :], bank(b), ACT.Gelu, scale=ISW).then_inc(gelu_out, 1)

            def query_turn(i):
                for hp in range(2):
                    m, n, g = i * 4 + 2 * hp, i * (2 * SLOTS) + (N_PQ + SLOTS * hp), i * 2 + (N_PQ // SLOTS + hp)
                    h = i * 2 + hp
                    for side in range(2):
                        cuts.ahead(g, side)
                        query_out(m + side, n + side, side)
                    for side in range(2):
                        cuts.ahead(g, 2 + side)
                        scores_out(m + side, h, hp, side)
                        if side == 1 and (not isinstance(h, int) or h > 0):
                            gate_exp(h - 1)
                        early_gelu(m + side, n + 2 + side, 2 * hp + side, 4 + side, i)

            cuts.cut = cut_high_scaled
            query_turn(0)
            with act.Fori(1, PH // 2) as i:
                query_turn(i)
            cuts.n += 4 * PH
            for e in range(WOVEN, BEHIND):
                if e == WOVEN + SLOTS:
                    gate_exp(PH - 1)
                cuts.upto(N_U + e + 3)
                early_gelu(e, N_U + e, e % 4, 4 + e % 2, e // 4)
            cuts.cut = cut_high

            for v, b in enumerate(TURN_BANKS):
                act.wait_ge(idx_turned, v + 1)
                nc.scalar.activation(idxT[:, v, :], bank(b), ACT.Copy).then_inc(idxT_out, 1)

            def tile_turn(t, par, octets=True):
                if octets:
                    wait(act, g_stored[par], t * 8 - 8 * par)
                for s in range(SLOTS):
                    if octets:
                        cuts.ahead(t + (N_U + BEHIND) // SLOTS, s)
                        for j in range(2 * s, 2 * s + 2):
                            for half in range(2):
                                act.wait_ge(g_done, t * (2 * OCT) + (2 * j + half + 1))
                                lo = j * OCT + 4 * half
                                nc.scalar.activation(G[par][:, :, lo:lo + 4].rearrange("p i n -> p n i"),
                                                     v3(bank(2 * (j % 2) + half), 4),
                                                     ACT.Copy).then_inc(g_out, 1)
                    if not octets:
                        cuts.ahead(t + (N_U + BEHIND) // SLOTS, s)
                    early_gelu(t * SLOTS + (BEHIND + s), t * SLOTS + (N_U + BEHIND + s), s, 4 + s % 2,
                               t + BEHIND // SLOTS)
                if octets:
                    act.wait_ge(g_out, t * (2 * OCT) + 2 * OCT)
                    act.dma_start(gmat[bass.ds(t, 1)].rearrange("a p n -> p (a n)"),
                                  G[par].rearrange("p i n -> p (i n)")).then_inc(g_stored[par], 16)

            act.wait_ge(head_done, PH)
            for t in range(2):
                tile_turn(t, t)
            with act.Fori(1, GT // 2) as o:
                for par in range(2):
                    tile_turn(o * 2 + par, par)
            tile_turn(GT, 0, octets=False)
            store_early(EARLY - 1, 3)
            cuts.n += EARLY - BEHIND

            def expert_group(g, par, inputs=True):
                for s in range(GRP):
                    if inputs:
                        cuts.ahead(g + N_U // SLOTS, s)
                    act.wait_ge(vslab_in[s], g * 16 + 16)
                    wait(act, b_done, (g - 1) * KC)
                    nc.scalar.activation(vh[:, par * GRP + s, :], vraw[:, s, :], ACT.Copy,
                                         scale=WS).then_inc(vhigh_cut, 1)
                    if inputs:
                        act.wait_ge(slab_done, g * GRP + (N_U + s + 1))
                        wait(act, gated_out, g * GRP + (s - 3))
                        nc.scalar.activation(act_s[:, s, :], bank(s % 2), ACT.Gelu,
                                             scale=ISW).then_inc(gelu_out, 1)

            act.wait_ge(g_stored[0], GT // 2 * 16)
            act.wait_ge(g_stored[1], GT // 2 * 16)
            for g in range(3):
                expert_group(g, g % 2, inputs=False)
            with act.Fori(1, EG // 2) as o:
                expert_group(o * 2 + 1, 1, inputs=False)
                expert_group(o * 2 + 2, 0, inputs=False)
            with act.Fori(EG // 2, GROUPS // 2 - 1) as o:
                expert_group(o * 2 + 1, 1)
                expert_group(o * 2 + 2, 0)
            expert_group(GROUPS - 1, 1)
            cuts.n += NK - EARLY
            n3, n4 = Norm("final1", 6), Norm("mixn", 7)
            for c in range(KC):
                act.wait_ge(acc_out, (GROUPS - 1) * KC + c + 1)
                n3.square(c)
            n3.act(act)

            for c in range(KC):
                act.wait_ge(final1_out, c + 1)
                n4.square(c)
            n4.act(act)
            act.wait_ge(pads, 2)
            for n in range(N_POOL, N_WP):
                c = n - N_POOL
                cuts.upto(n + 3)
                act.wait_ge(slab_done, n + 1)
                wait(act, pool_cut, c - 1)
                nc.scalar.activation(zp[c % 2][:, 16:16 + T], bank(n % 4), ACT.Copy,
                                     scale=ISW).then_inc(zpool_out, 1)
            for n in range(N_WP, N_SV):
                cuts.upto(n + 3)
            act.wait_ge(y_cut, KC)
            for half in range(2):
                cuts.upto(N_SV + 4 * half + 7)
                act.wait_ge(slab_done, N_SV + 4 * half + 4)
                for t in range(TT):
                    nc.scalar.activation(V2[:, 2 * t + half, :], bank(4 * half + t), ACT.Gelu,
                                         scale=ISW).then_inc(v_out, 1)
            act.wait_ge(v_out, 2 * TT)
            for t in range(TT):
                nc.scalar.activation(U2[:, 2 * (t % 2):2 * (t % 2) + 2, :], V2[:, 2 * t:2 * t + 2, :], ACT.Square,
                                     accum_out=vss[:, t:t + 1]).then_inc(vsq_out, 1)
                act.wait_ge(vsq_out, t + 1)
            nc.scalar.activation(vrs[:, 0:TT], vss[:, 0:TT], ACT.Sqrt, bias=EPSC,
                                 scale=1.0 / D).then_inc(vstd_out, 1)
            for n in range(N_SU, N_GA):
                cuts.upto(n + 3)
                act.wait_ge(slab_done, n + 1)
                nc.scalar.activation(U2[:, n - N_SU, :], bank(n % 4), ACT.Gelu, scale=ISW).then_inc(u_out, 1)
            act.wait_ge(sgu_cut, KC)
            for n in range(N_GA, N_WO2):
                i = n - N_GA
                b = i // 2
                cuts.upto(n + 3)
                if i % 2 == 0:
                    act.wait_ge(slab_done, n + 1)
                    wait(act, branch_out, b - 1)
                    nc.scalar.activation(gat[:, b % 2, :], bank(n % 4), ACT.Sigmoid,
                                         scale=ISW).then_inc(gsig_out, 1)
            n5 = Norm("ffnn", 7)
            for n in range(N_WO2, N_UP):
                cuts.upto(n + 3)
                act.wait_ge(res2_out, n - N_WO2 + 1)
                n5.square(n - N_WO2)

            n5.act(act)
            act.wait_ge(pads, 6)

            def up_turn(i):
                for pair in range(2):
                    for side in range(2):
                        s = 2 * pair + side
                        cuts.ahead(i + N_UP // SLOTS, s)
                        act.wait_ge(slab_done, i * SLOTS + (N_UP + s + 1))
                        wait(act, conv_out, i * SLOTS + (s - 3))
                        nc.scalar.activation(upb[s][:, 2:2 + T], bank(s), ACT.Copy,
                                             scale=ISW).then_inc(up_out, 1)
                    act.wait_ge(conv_out, i * SLOTS + (2 * pair + 1))
                    nc.scalar.activation(cv[:, 3 * pair + 2, :], cv[:, 3 * pair, :],
                                         ACT.Gelu).then_inc(cgelu_out, 1)

            up_turn(0)
            with act.Fori(1, FC // 2) as i:
                up_turn(i)
            cuts.n += 2 * FC
            cuts.upto(N_DN + 6)
            with act.Fori(1, FC // SLOTS) as i:
                for s in range(SLOTS):
                    cuts.ahead(i + N_DN // SLOTS, s)
            cuts.n += (FC // SLOTS - 1) * SLOTS
            act.wait_ge(p_in, 16)
            nc.scalar.activation(pth, prw, ACT.Copy).then_inc(p_high, 1)
            cuts.upto(N_PG + 2)
            n6 = Norm("plen", 0)
            for c in range(KC):
                act.wait_ge(down_out, c + 1)
                n6.square(c)
            n6.act(act)
            for n in range(N_PG, N_PP):
                cuts.upto(n + 3)
                act.wait_ge(slab_done, n + 1)
                nc.scalar.activation(pgs[:, n - N_PG, :], bank(n % 4), ACT.Sigmoid,
                                     scale=ISW).then_inc(psig_out, 1)
            n7 = Norm("final2", 0)
            for c in range(KC):
                act.wait_ge(ple_out, c + 1)
                n7.square(c)
            n7.act(act)

        @block.vector
        def _(dve):
            dchain.eng = dve
            cuts = Cuts(dve, cut_low)
            dve.wait_ge(vecs_in, 16)
            L = VEC["lam"]
            nc.vector.tensor_tensor(LAMP[0:DH, :], vec[0:DH, L:L + 4:2], vec[0:DH, L + 1:L + 4:2],
                                    ALU.mult).then_inc(lam_prod, 1)
            dve.wait_ge(x_in, 48)
            n1 = Norm("ln1", 0)
            n1.dve(dve)
            dve.wait_ge(lam_exp, 1)
            dchain.link(nc.vector.tensor_tensor(NLAM, LAME[:, 1:2], LAME[:, 0:1], ALU.subtract))
            dchain.link(nc.vector.tensor_scalar(NLAM, NLAM, LAM_INIT, None, ALU.subtract))
            nc.vector.tensor_scalar(SUBW, vec[:, VEC["subln"]:VEC["subln"] + 1], 1.0 - LAM_INIT, None, ALU.mult)
            cuts.upto(2)
            dve.wait_ge(consts_in, 160)

            def rope(n):
                dve.wait_ge(rope_out, n + 1)
                if n < HEADS:
                    dst, m = q[:, n, :], None
                else:
                    dst, m = k[:, n - HEADS, 0:T], k[:, n - HEADS, T:TM]
                a = nc.vector.tensor_tensor(rtmp[:, 0, :], bank(6), ropes[:, 0:T], ALU.mult)
                if m is not None:
                    a = nc.vector.tensor_tensor(rtmp[:, 1, 0:M], bank(7, M), ropes[:, T:TM], ALU.mult)
                a.then_inc(rope_mul, 1)
                a = nc.vector.tensor_tensor(dst, dst, ropec[:, 0:T], ALU.mult)
                if m is not None:
                    a = nc.vector.tensor_tensor(m, m, ropec[:, T:TM], ALU.mult)
                dchain.link(a)
                dve.wait_ge(rope_mul, n + 1)
                a = nc.vector.tensor_tensor(dst, dst, rtmp[:, 0, :], ALU.add)
                if m is not None:
                    a = nc.vector.tensor_tensor(m, m, rtmp[:, 1, 0:M], ALU.add)
                dchain.link(a)

            for n in range(N_Q, N_V):
                cuts.upto(n + 3)
                if n >= 1:
                    rope(n - 1)
            rope(N_V - 1)
            dve.wait_ge(wz_high, 1)
            nc.vector.scalar_tensor_tensor(out=wzl.rearrange("p a b -> p (a b)"), in0=wz, scalar=WS,
                                           in1=wzh.rearrange("p a b -> p (a b)"), op0=ALU.mult,
                                           op1=ALU.subtract).then_inc(wz_low, 1)
            cuts.upto(N_V + 11)
            for n in range(N_GQ, N_GR):
                cuts.upto(n + 3)
            for n in range(N_GR, N_WO):
                cuts.upto(n + 3)
                dve.wait_ge(sig_out, n - N_GR + 1)
                nc.vector.scalar_tensor_tensor(out=sgr[:, n - N_GR, :], in0=bank(n % 4), scalar=ISW,
                                               in1=sgr[:, n - N_GR, :], op0=ALU.mult,
                                               op1=ALU.mult).then_inc(silu_out, 1)
            dve.wait_ge(gate_ln, 1)
            dchain.link(nc.vector.scalar_tensor_tensor(
                out=gtmp.rearrange("p a b -> p (a b)"), in0=B.rearrange("p a b -> p (a b)"), scalar=0.0,
                in1=gtmp.rearrange("p a b -> p (a b)"), op0=ALU.min, op1=ALU.subtract))
            for h in range(HEADS):
                nc.vector.tensor_tensor_scan(B[:, h, 0:T], one.to_broadcast([P, T]), gtmp[:, h, 0:T], 0.0,
                                             ALU.mult, ALU.add)
                a = nc.vector.tensor_tensor_scan(B[:, h, T:TM], one.to_broadcast([P, M]), gtmp[:, h, T:TM], 0.0,
                                                 ALU.mult, ALU.add)
            dchain.link(a)
            for h in range(HEADS):
                nc.vector.tensor_tensor(B[DH:P, h, 0:T], B[DH:P, h, 0:T], gtmp[DH:P, h, 0:T],
                                        ALU.subtract).then_inc(gate_out, 1)

            def scores_max(turn):
                for c in range(2):
                    u = 2 * turn + c
                    dve.wait_ge(score_done, u + 1)
                    nc.vector.tensor_reduce(nmx[:, u % 4:u % 4 + 1], psum[:, 2 * c * 512:2 * c * 512 + TM],
                                            AX.X, ALU.max, negate=True).then_inc(max_done, 1)

            def difference(turn):
                par = turn % 2
                dve.wait_ge(exp_done, 2 * turn + 2)
                rz_ = rzs[:, 4 * par:4 * par + 2]
                dchain.link(nc.vector.reciprocal(rz_, zs[:, 2 * par:2 * par + 2]))
                dchain.link(nc.vector.tensor_tensor(rz_[:, 1:2], rz_[:, 1:2], NLAM, ALU.mult))
                dchain.link(nc.vector.tensor_scalar(pr[:, 2 * par + 1, :], pr[:, 2 * par + 1, :],
                                                    rz_[:, 1:2], None, ALU.mult))
                if turn >= 2:
                    dve.wait_ge(turn_done, turn - 1)
                nc.vector.scalar_tensor_tensor(out=pa[:, par, :], in0=pr[:, 2 * par, :],
                                               scalar=rz_[:, 0:1], in1=pr[:, 2 * par + 1, :],
                                               op0=ALU.mult, op1=ALU.add).then_inc(diff_done, 1)

            for turn in range(HEADS * TT):
                scores_max(turn)
                if turn >= 1:
                    difference(turn - 1)
            difference(HEADS * TT - 1)

            def head_norms(lo, stds, w, times=None):
                dve.wait_ge(ostd_out, lo + HEADS)
                dchain.link(nc.vector.reciprocal(stds, stds))
                for h in range(HEADS):
                    a = nc.vector.scalar_tensor_tensor(out=otmp[:, h, :], in0=otmp[:, h, :], scalar=w,
                                                       in1=stds[:, h, :], op0=ALU.mult, op1=ALU.mult)
                dchain.link(a)
                if times is not None:
                    dchain.link(nc.vector.tensor_tensor(otmp, otmp, times, ALU.mult))
                dchain.link(nc.vector.tensor_copy(xh[:, lo:lo + HEADS, 0:T], otmp))
                nc.vector.tensor_tensor(xl[:, lo:lo + HEADS, 0:T], otmp, xh[:, lo:lo + HEADS, 0:T],
                                        ALU.subtract).then_inc(mixl_out, 1)

            head_norms(0, v3(pr.rearrange("p a b -> p (a b)")[:, 0:4 * T], 4), SUBW)

            dve.wait_ge(mixl_out, 1)
            dve.wait_ge(gate_out, HEADS)
            nc.vector.memset(KT, 0.0)
            nc.vector.memset(QT, 0.0).then_inc(zeroed, 1)
            dve.wait_ge(zeroed, 1)

            def blocks(ap, s, side):
                return ap.rearrange("p (n two s) -> p n two s", two=2, s=s)[:, :, side, :]

            def exponents(h, li):
                s, u = LEVELS[li], h * NL + li
                b = B[:, h, 0:T]
                ref = blocks(b, s, 0)[:, :, s - 1:s].to_broadcast([P, T // (2 * s), s])
                if u >= 2:
                    dve.wait_ge(kt_out, 2 * (u - 1))
                    dve.wait_ge(qt_out, 2 * (u - 1))
                nc.vector.tensor_tensor(blocks(E[:, u % 2, :], s, 0), ref, blocks(b, s, 0),
                                        ALU.subtract).then_inc(e_in, 1)
                nc.vector.tensor_tensor(blocks(E[:, u % 2, :], s, 1), blocks(b, s, 1), ref,
                                        ALU.subtract).then_inc(e_in, 1)

            def decayed(h, li):
                s, u = LEVELS[li], h * NL + li
                dve.wait_ge(e_exp, u + 1)
                if h >= 1:
                    need_level_free(dve, h, li)
                for src, dst, side, done in ((gk, KT, 0, kt_out), (gq, QT, 1, qt_out)):
                    for half in range(2):
                        rows = slice(DH * half, DH * (half + 1))
                        sd = side ^ half
                        nc.vector.tensor_tensor(
                            blocks(dst[rows, li, :], s, sd), blocks(src[rows, h, 0:T], s, sd),
                            blocks(E[rows, u % 2, :], s, sd), ALU.mult).then_inc(done, 1)

            def need_level_free(eng, h, li):
                if li <= NS:
                    eng.wait_ge(lev_done, (h - 1) * (NS + 2) + li + 2)
                else:
                    eng.wait_ge(wide_done, h)

            for h in range(HEADS):
                def level_out(li):
                    u = h * (NS + 2) + li + 1
                    dve.wait_ge(lev_done, u + 1)
                    if li < 0 and h >= 1:
                        dve.wait_ge(gav_done, h)
                    if u >= 1:
                        dve.wait_ge(lev_out, u)
                    src = v3(bank(4 + u % 3), TT)
                    if li < NS:
                        mk = masks[:, li + 1:li + 2, :].to_broadcast([P, TT, P])
                        nc.vector.copy_predicated(Adiag, mk, src).then_inc(lev_out, 1)
                    else:
                        for j in range(TT):
                            i = j ^ 1
                            a = nc.vector.tensor_copy(A[:, j, i * P:(i + 1) * P], src[:, j, :])
                        a.then_inc(lev_out, 1)

                if h == 0:
                    exponents(0, 0)
                for li in range(NL):
                    if li + 1 < NL:
                        exponents(h, li + 1)
                    elif h + 1 < HEADS:
                        exponents(h + 1, 0)
                    decayed(h, li)
                    if li >= 1:
                        level_out(li - 2)
                nc.vector.tensor_tensor(Em[0:DH, T:TM],
                                        B[0:DH, h, TM - 1:TM].to_broadcast([DH, M]), B[0:DH, h, T:TM],
                                        ALU.subtract).then_inc(em_in, 1)
                dve.wait_ge(em_exp, h + 1)
                nc.vector.tensor_tensor(KTm[0:DH, :], gk[0:DH, h, T:TM], Em[0:DH, T:TM],
                                        ALU.mult).then_inc(ktm_out, 1)
                nc.vector.tensor_tensor(QTm[0:DH, :], gq[0:DH, h, 0:T], Em[0:DH, 0:T],
                                        ALU.mult).then_inc(ktm_out, 1)
                level_out(NS)
            dve.wait_ge(silu_out, HEADS)
            head_norms(HEADS, KT[:, 0:4, :], vec[:, VEC["glan"]:VEC["glan"] + 1], times=sgr)

            for n in range(N_WO, N_PQ):
                cuts.upto(n + 3)
                dve.wait_ge(slab_done, n + 1)
                c = n - N_WO
                nc.vector.scalar_tensor_tensor(out=X[:, c, 0:T], in0=bank(n % 4), scalar=ISW,
                                               in1=X[:, c, 0:T], op0=ALU.mult,
                                               op1=ALU.add).then_inc(res_out, 1)

            Norm("ln2", 4).dve(dve)

            def tiles(ap):
                return v3(ap, TT)

            def each(fn):
                for side in range(2):
                    for t in range(TT):
                        last = fn(side, t)
                return last

            def settled(ins):
                nc.vector.drain()

            def choose(head, sc):
                k8 = lambda side, t, lo: ts[:, side, t * TOP + lo:t * TOP + lo + 8]
                i8 = lambda side, t, lo: ti[:, side, t * TOP + lo:t * TOP + lo + 8]
                sk = lambda side, t: sc[:, side, t * P:(t + 1) * P]
                s2k = lambda side, t: s2[:, side, t * P:(t + 1) * P]
                settled(each(lambda a, t: nc.vector.max(k8(a, t, 0), sk(a, t))))
                settled(each(lambda a, t: nc.vector.match_replace(s2k(a, t), k8(a, t, 0), sk(a, t), LOWEST)))
                settled(each(lambda a, t: nc.vector.max(k8(a, t, 8), s2k(a, t))))
                each(lambda a, t: nc.vector.max_index(i8(a, t, 0), k8(a, t, 0), sk(a, t)))
                settled(each(lambda a, t: nc.vector.max_index(i8(a, t, 8), k8(a, t, 8), s2k(a, t))))
                nc.vector.tensor_copy(tif, ti)
                full = [P, TT, TOP, TOP]
                c4 = cand.rearrange("p t (a b) -> p t a b", a=TOP)
                settled(nc.vector.tensor_tensor(c4, tiles(ts[:, 0, :]).unsqueeze(3).to_broadcast(full),
                                                    tiles(ts[:, 1, :]).unsqueeze(2).to_broadcast(full), ALU.add))
                rng = range(TT)
                settled([nc.vector.max(best[:, t, 0:8], cand[:, t, :]) for t in rng][-1])
                settled([nc.vector.match_replace(cand2[:, t, :], best[:, t, 0:8], cand[:, t, :], LOWEST)
                             for t in rng][-1])
                settled([nc.vector.max(best[:, t, 8:16], cand2[:, t, :]) for t in rng][-1])
                g3 = v3(gsm, TT)
                nc.vector.tensor_tensor(g3, best, best[:, :, 0:1].to_broadcast([P, TT, TOP]),
                                        ALU.subtract).then_inc(gsub_out, 1)
                [nc.vector.max_index(pos[:, t, 0:8], best[:, t, 0:8], cand[:, t, :]) for t in rng]
                settled([nc.vector.max_index(pos[:, t, 8:16], best[:, t, 8:16], cand2[:, t, :])
                             for t in rng][-1])
                pf = pos.rearrange("p a b -> p (a b)")
                nc.vector.tensor_scalar(posab[:, 0, :], pf, 4, None, ALU.logical_shift_right)
                settled(nc.vector.tensor_scalar(posab[:, 1, :], pf, 15, None, ALU.bitwise_and))
                settled(nc.vector.tensor_copy(posf, posab))
                sel4 = sel.rearrange("p (t k a) -> p t k a", t=TT, k=TOP)
                cols = bass.ds(head * TOP, TOP)
                for side in range(2):
                    settled(nc.vector.tensor_tensor(
                        sel4, tiles(posf[:, side, :]).unsqueeze(3).to_broadcast(full),
                        io16.unsqueeze(1).unsqueeze(1).to_broadcast(full), ALU.is_equal))
                    settled(nc.vector.tensor_tensor(
                        sel4, sel4, tiles(tif[:, side, :]).unsqueeze(2).to_broadcast(full), ALU.mult))
                    nc.vector.tensor_reduce(tiles(idx_tok[:, side, :])[:, :, cols], sel4, AX.X, ALU.add)
                    if side == 0:
                        dve.wait_ge(gexp_out, head + 1)
                        settled(nc.vector.tensor_reduce(gsum[:, 0:TT], g3, AX.X, ALU.add))
                settled(nc.vector.reciprocal(gsum[:, 8:8 + TT], gsum[:, 0:TT]))
                nc.vector.tensor_tensor(tiles(idx_tok[:, 2, :])[:, :, cols], g3,
                                        gsum[:, 8:8 + TT].unsqueeze(2).to_broadcast([P, TT, TOP]),
                                        ALU.mult).then_inc(head_done, 1)

            def query_turn(i):
                for hp in range(2):
                    dve.wait_ge(s_out, i * 4 + (2 * hp + 2))
                    nc.vector.tensor_copy(gsum[:, 12 + hp:13 + hp], s_[hp][:, 0, 0:1])
                    choose(i * 2 + hp, s_[hp])

            LOWEST = -3.0e38
            query_turn(0)
            with dve.Fori(1, PH // 2) as i:
                query_turn(i)
            cuts.n += 4 * PH + BEHIND - WOVEN

            dve.wait_ge(idxT_out, 3)
            dchain.link(nc.vector.tensor_copy(gTh, idxT[:, 2, :]))
            nc.vector.tensor_tensor(gTl, idxT[:, 2, :], gTh, ALU.subtract).then_inc(gates_cut, 1)
            dve.wait_ge(low_cut, cuts.n)

            def one_hots(e, b, tok, slab):
                full = [P, OCT, P]
                col = lambda v: idxT[:, v, bass.ds(tok, OCT)].unsqueeze(2).to_broadcast(full)
                numbers = iota.unsqueeze(1).to_broadcast(full)
                if slab:
                    wait(dve, hot_gated, e - 1)
                    nc.vector.tensor_tensor(hot_slab[b], numbers, col(0), ALU.is_equal).then_inc(hot_slab_out, 1)
                else:
                    wait(dve, g_done, e * 2 - 2)
                    nc.vector.tensor_tensor(hot_row[b], numbers, col(1), ALU.is_equal).then_inc(hot_row_out, 1)

            def tile_turn(t, octets=True):
                for s in range(SLOTS):
                    if octets:
                        for slab, b in ((1, 0), (1, 1), (0, 0), (0, 1)):
                            one_hots(t * OCT + (2 * s + b), b, t * NT + (2 * s + b) * OCT, slab)
                    cuts.ahead(t + (N_U + BEHIND) // SLOTS, s)

            tile_turn(0)
            with dve.Fori(1, GT) as t:
                tile_turn(t)
            tile_turn(GT, octets=False)
            cuts.n += EARLY - BEHIND

            def gated(g, par, s, inputs):
                if s == 0:
                    dve.wait_ge(g_in[par], (g // 2) * 16 + 16 if isinstance(g, int) else g * 8 + (16 - 8 * par))
                if inputs:
                    dve.wait_ge(gelu_out, g * GRP + (s + 1))
                else:
                    dve.wait_ge(act_in[s], g * 16 + 16)
                tl = lambda ap: v3(ap, GT)
                wait(dve, a_cut, g * GRP + (s - 1))
                nc.vector.tensor_tensor(tl(at_s[:, s % 2, :]), tl(act_s[:, s, :]),
                                        GB[par][:, :, s * NT:(s + 1) * NT], ALU.mult).then_inc(gated_out, 1)
                dve.wait_ge(gated_out, g * GRP + (s + 1))
                wait(dve, b_done, (g - 1) * KC)
                x = par * GRP + s
                dchain.link(nc.vector.tensor_copy(Ah[:, x, :], at_s[:, s % 2, :]))
                nc.vector.tensor_tensor(Al[:, x, :], at_s[:, s % 2, :], Ah[:, x, :],
                                        ALU.subtract).then_inc(a_cut, 1)

            def expert_group(g, par, inputs=True, outputs=True, last=False):
                gp = g - 1
                for s in range(GRP):
                    if inputs:
                        cuts.ahead(g + N_U // SLOTS, s)
                    if not last:
                        dve.wait_ge(vhigh_cut, g * GRP + (s + 1))
                        nc.vector.scalar_tensor_tensor(
                            out=vl[:, par * GRP + s, :], in0=vraw[:, s, :], scalar=WS,
                            in1=vh[:, par * GRP + s, :], op0=ALU.mult, op1=ALU.subtract).then_inc(vlow_cut, 1)
                        gated(g, par, s, inputs)
                    if outputs:
                        if s == 0:
                            wait(dve, acc_out, gp * KC)
                        for c in (2 * s, 2 * s + 1):
                            dve.wait_ge(b_done, gp * KC + (c + 1))
                            nc.vector.scalar_tensor_tensor(
                                out=X[:, c, 0:T], in0=bank(2 + c % 4), scalar=ISW, in1=X[:, c, 0:T],
                                op0=ALU.mult, op1=ALU.add).then_inc(acc_out, 1)

            expert_group(0, 0, inputs=False, outputs=False)
            expert_group(1, 1, inputs=False)
            expert_group(2, 0, inputs=False)
            with dve.Fori(1, EG // 2) as o:
                dchain.enter((o - 1) * (2 * GRP))
                expert_group(o * 2 + 1, 1, inputs=False)
                expert_group(o * 2 + 2, 0, inputs=False)
                dchain.leave(2 * GRP, EG // 2 - 1)
            with dve.Fori(EG // 2, GROUPS // 2 - 1) as o:
                dchain.enter((o - EG // 2) * (2 * GRP))
                expert_group(o * 2 + 1, 1)
                expert_group(o * 2 + 2, 0)
                dchain.leave(2 * GRP, GROUPS // 2 - 1 - EG // 2)
            expert_group(GROUPS - 1, 1)
            expert_group(GROUPS, 0, inputs=False, last=True)
            cuts.n += NK - EARLY
            Norm("final1", 6).dve(dve, dst=X, done=final1_out)

            Norm("mixn", 7).dve(dve)

            def cut_onto(src, h_, l_, done):
                dchain.link(nc.vector.tensor_copy(h_, src))
                nc.vector.tensor_tensor(l_, src, h_, ALU.subtract).then_inc(done, 1)

            for n in range(N_POOL, N_WP):
                c = n - N_POOL
                cuts.upto(n + 3)
                dve.wait_ge(zpool_out, c + 1)
                src, z = zp[c % 2], zp[c % 2][:, 16:16 + T]
                for kk in range(c // 2 + 1):
                    w = 2 ** kk
                    lo, dst = 2 * w - 1, win[kk % 2]
                    dchain.link(nc.vector.tensor_tensor(dst[:, lo:16 + T], src[:, lo:16 + T],
                                                        src[:, lo - w:16 + T - w], ALU.add))
                    src = dst
                w = WINDOWS[c // 2]
                tmp = win[(c // 2 + 1) % 2][:, 0:T]
                nc.vector.scalar_tensor_tensor(out=tmp[:, w:T], in0=src[:, 16 + w:16 + T], scalar=1.0 / w,
                                               in1=z[:, w:T], op0=ALU.mult, op1=ALU.subtract)
                dchain.link(nc.vector.tensor_tensor(tmp[:, 0:w], src[:, 16:16 + w], icnt[:, 0:w], ALU.mult))
                dchain.link(nc.vector.tensor_tensor(tmp[:, 0:w], tmp[:, 0:w], z[:, 0:w], ALU.subtract))
                cut_onto(tmp, ph_[:, c, :], pl_[:, c, :], pool_cut)
                dve.wait_ge(pool_cut, c + 1)
            for n in range(N_WP, N_SV):
                cuts.upto(n + 3)
                dve.wait_ge(slab_done, n + 1)
                for c in (2 * (n - N_WP), 2 * (n - N_WP) + 1):
                    col = vec[:, VEC["pscale"] + c:VEC["pscale"] + c + 1]
                    dchain.link(nc.vector.tensor_scalar(V2[:, c, :], bank(c % 4), ISW, col, ALU.mult, ALU.mult))
                    cut_onto(V2[:, c, :], yh[:, c, :], yl[:, c, :], y_cut)
            cuts.upto(N_SV + 11)
            dve.wait_ge(vstd_out, 1)
            dchain.link(nc.vector.reciprocal(vrs[:, 4:8], vrs[:, 0:4]))
            for t in range(TT):
                nc.vector.tensor_scalar(V2[:, 2 * t:2 * t + 2, :], V2[:, 2 * t:2 * t + 2, :], vrs[:, 4 + t:5 + t],
                                        None, ALU.mult).then_inc(v_normed, 1)
            dve.wait_ge(small_in, 32)
            for n in range(N_SU, N_GA):
                h = n - N_SU
                cuts.upto(n + 3)
                dve.wait_ge(mix_done, h + 1)
                m = mtmp[:, h % 2, :]
                col = vec[:, VEC["sgun"] + h:VEC["sgun"] + h + 1]
                nc.vector.scalar_tensor_tensor(
                    out=v3(m, TT), in0=v3(bank(4 + h % 2), TT), scalar=col,
                    in1=bsp[:, h * P:(h + 1) * P].unsqueeze(1).to_broadcast([P, TT, P]), op0=ALU.mult,
                    op1=ALU.add).then_inc(mix_read, 1)
                dve.wait_ge(mix_read, h + 1)
                dve.wait_ge(u_out, h + 1)
                dchain.link(nc.vector.tensor_tensor(m, m, U2[:, h, :], ALU.mult))
                cut_onto(m, ph_[:, h, :], pl_[:, h, :], sgu_cut)
            for n in range(N_GA, N_WO2):
                i = n - N_GA
                b, c = i // 2, i // 2 % KC
                cuts.upto(n + 3)
                if i % 2:
                    dve.wait_ge(slab_done, n + 1)
                    dve.wait_ge(gsig_out, b + 1)
                    dst = V2[:, c, :] if b < KC else mtmp[:, b % 2, :]
                    nc.vector.scalar_tensor_tensor(out=dst, in0=bank(n % 4), scalar=ISW, in1=gat[:, b % 2, :],
                                                   op0=ALU.mult, op1=ALU.mult).then_inc(branch_out, 1)
                    if b >= KC:
                        dve.wait_ge(branch_out, b + 1)
                        dchain.link(nc.vector.tensor_tensor(V2[:, c, :], V2[:, c, :], mtmp[:, b % 2, :], ALU.add))
                        cut_onto(V2[:, c, :], yh[:, c, :], yl[:, c, :], m_cut)
            for n in range(N_WO2, N_UP):
                cuts.upto(n + 3)
                dve.wait_ge(slab_done, n + 1)
                c = n - N_WO2
                nc.vector.scalar_tensor_tensor(out=X[:, c, 0:T], in0=bank(n % 4), scalar=ISW,
                                               in1=X[:, c, 0:T], op0=ALU.mult,
                                               op1=ALU.add).then_inc(res2_out, 1)

            Norm("ffnn", 7).dve(dve)

            def conv(i, f, pair, side):
                s = 2 * pair + side
                dst = cv[:, 3 * pair + side, :]
                cw = lambda tap: vec[:, bass.ds(f + (VEC["convw"] + tap * 2 * FC + side * FC), 1)]
                cb = vec[:, bass.ds(f + (VEC["convb"] + side * FC), 1)]
                dve.wait_ge(up_out, i * SLOTS + (s + 1))
                dchain.link(nc.vector.tensor_scalar(dst, upb[s][:, 2:2 + T], cw(2), cb, ALU.mult, ALU.add))
                dchain.link(nc.vector.scalar_tensor_tensor(out=dst, in0=upb[s][:, 1:1 + T], scalar=cw(1), in1=dst,
                                                           op0=ALU.mult, op1=ALU.add))
                return nc.vector.scalar_tensor_tensor(out=dst, in0=upb[s][:, 0:T], scalar=cw(0), in1=dst,
                                                      op0=ALU.mult, op1=ALU.add)

            def up_turn(i):
                for pair in range(2):
                    f = i * 2 + pair
                    cuts.ahead(i + N_UP // SLOTS, 2 * pair)
                    a = conv(i, f, pair, 0)
                    a.then_inc(conv_out, 1)
                    cuts.ahead(i + N_UP // SLOTS, 2 * pair + 1)
                    conv(i, f, pair, 1).then_inc(conv_out, 1)
                    dve.wait_ge(conv_out, i * SLOTS + (2 * pair + 2))
                    dve.wait_ge(cgelu_out, i * 2 + (pair + 1))
                    p_ = cv[:, 3 * pair + 2, :]
                    dchain.link(nc.vector.tensor_tensor(p_, p_, cv[:, 3 * pair + 1, :], ALU.mult))
                    fi = bass.ds(f, 1)
                    flat = lambda x: x[:, fi, :].rearrange("p a n -> p (a n)")
                    cut_onto(p_, flat(ggh), flat(ggl), ffn_cut)

            first = dchain.n
            up_turn(0)
            per = dchain.n - first
            with dve.Fori(1, FC // 2) as i:
                dchain.enter((i - 1) * per)
                up_turn(i)
                dchain.leave(per, FC // 2 - 1)
            cuts.n += 2 * FC
            cuts.upto(N_DN + 6)
            with dve.Fori(1, FC // SLOTS) as i:
                for s in range(SLOTS):
                    cuts.ahead(i + N_DN // SLOTS, s)
            cuts.n += (FC // SLOTS - 1) * SLOTS
            dve.wait_ge(p_high, 1)
            nc.vector.tensor_tensor(ptl, prw, pth, ALU.subtract).then_inc(p_low, 1)
            cuts.upto(N_PG + 2)
            dve.wait_ge(slab_done, N_PG)
            for c in range(KC):
                nc.vector.scalar_tensor_tensor(out=X[:, c, 0:T], in0=bank(c), scalar=ISW,
                                               in1=X[:, c, 0:T], op0=ALU.mult,
                                               op1=ALU.add).then_inc(down_out, 1)
            Norm("plen", 0).dve(dve)
            for n in range(N_PG, N_PP):
                cuts.upto(n + 3)
            for c in range(KC):
                dve.wait_ge(psig_out, c + 1)
                dve.wait_ge(ple_done, c + 1)
                dchain.link(nc.vector.scalar_tensor_tensor(out=ptmp[:, c % 2, :], in0=bank(4 + c % 4), scalar=ISW,
                                                           in1=pgs[:, c, :], op0=ALU.mult, op1=ALU.mult))
                nc.vector.tensor_tensor(X[:, c, 0:T], X[:, c, 0:T], ptmp[:, c % 2, :],
                                        ALU.add).then_inc(ple_out, 1)
            Norm("final2", 0).dve(dve, dst=yout, done=y_out)

        @block.gpsimd
        def _(pool):
            nc.gpsimd.memset(EPSC, EPS).then_inc(pool_step, 1)
            pool.wait_ge(low_cut, LOW_POOL)
            with pool.Fori(N_PQ // SLOTS, (N_U + BEHIND) // SLOTS) as g:
                for s in range(SLOTS):
                    n = s + SLOTS - 1
                    cut_low_scaled(pool, g + n // SLOTS, n % SLOTS)
            pool.wait_ge(gates_cut, 1)

            def gate_octet(e, b, tok):
                pool.wait_ge(hot_slab_out, e + 1)
                wait(pool, g_done, e * 2 - 2)
                for src, dst in ((gTh, hot_high), (gTl, hot_low)):
                    last = nc.gpsimd.tensor_tensor(
                        dst[b], hot_slab[b], src[:, bass.ds(tok, OCT)].unsqueeze(2).to_broadcast([P, OCT, P]),
                        ALU.mult)
                last.then_inc(hot_gated, 1)

            gate_octet(0, 0, 0)
            gate_octet(1, 1, OCT)
            with pool.Fori(1, T // OCT // 2) as o:
                for b in range(2):
                    gate_octet(o * 2 + b, b, o * (2 * OCT) + b * OCT)
            pool.wait_ge(final1_out, KC)
            for z in zp:
                nc.gpsimd.memset(z[:, 0:16], 0.0).then_inc(pads, 1)
            pool.wait_ge(small_in, 32)
            w3 = v3(wsT, 8)
            nc.gpsimd.affine_select(out=w3, in_=w3, compare_op=ALU.is_ge, fill=0.0, base=0,
                                    pattern=[[0, 8], [1, P]], channel_multiplier=-1).then_inc(masked, 1)
            pool.wait_ge(res2_out, KC)
            for z in upb:
                nc.gpsimd.memset(z[:, 0:2], 0.0).then_inc(pads, 1)


def tables():
    inv = np.power(np.float32(500000.0), -np.arange(0, 2 * ROPE, 2, dtype=np.float32) / np.float32(2 * ROPE))
    pos = np.concatenate([np.arange(M, TM), np.arange(M)]).astype(np.float32)
    ang = (pos[:, None] * inv[None, :].astype(np.float32)).astype(np.float32)
    ropec, ropes = np.ones((P, TM), np.float32), np.zeros((P, TM), np.float32)
    perm = np.zeros((P, P), np.float32)
    for c in range(2):
        for i in range(ROPE):
            a, b = DH * c + i, DH * c + ROPE + i
            ropec[a] = ropec[b] = np.cos(ang[:, i])
            ropes[a], ropes[b] = -np.sin(ang[:, i]), np.sin(ang[:, i])
            perm[a, b] = perm[b, a] = 1.0
    i = np.arange(P)
    masks = np.zeros((P, len(SMALL) + 1, P), np.uint32)
    masks[:, 0] = np.eye(P, dtype=np.uint32)
    for n, s in enumerate(SMALL):
        masks[:, n + 1] = (i[:, None] // (2 * s) == i[None] // (2 * s)) & (i[:, None] // s != i[None] // s)
    return {
        "ident": np.eye(P, dtype=np.float32), "ones": np.ones((P, P), np.float32),
        "iota": np.tile(i.astype(np.float32), (P, 1)), "perm": perm, "masks": masks, "ropec": ropec,
        "ropes": ropes, "icnt": np.tile(1.0 / np.arange(1, 17, dtype=np.float32), (P, 1)).astype(np.float32),
        "io16": np.tile(np.arange(16, dtype=np.float32), (P, 1)),
    }


def layout(a):
    f = {n: np.asarray(v) for n, v in a.items()}

    def chunks(w):
        kk, n = w.shape
        return w.reshape(kk // P, P, n // P, P).transpose(2, 1, 0, 3).reshape(n // P, P, -1)

    def rows(w):
        return w.reshape(4, 2, P, 512).transpose(0, 2, 1, 3).reshape(4, P, 1024)

    def wide(s):
        return np.concatenate([s, np.zeros((*s.shape[:2], D - s.shape[2]), np.float32)], 2) if s.shape[2] < D else s

    wi = f["w_in"][0]
    cut = np.split(wi, np.cumsum([512, 512, 512, 256, 256, 512, 512, 16])[:].tolist(), axis=1)
    dq, dk, dvw, gqw, gkw, gvw, grw, zf, zb = cut
    w2i = f["w_in_2"][0]
    pool, zu, zv, ga, gb = (w2i[:, i * D:(i + 1) * D] for i in range(5))
    up = chunks(f["w_up_2"][0])
    woven = lambda x, y: np.stack([x, y], 1).reshape(-1, P, x.shape[2])
    wp = f["w_pool_2"][0].reshape(4, 2, P, 2, P).transpose(0, 2, 3, 1, 4).reshape(4, P, 512)
    u = f["peer_u"][0].reshape(NK, NK, KC, P).transpose(0, 3, 2, 1).reshape(NK, P, D)
    two = lambda x: x.reshape(-1, 2, P, D)
    queries = np.concatenate([two(chunks(f["peer_w_q"][0])), two(u[:WOVEN])], 1).reshape(-1, P, D)
    parts = [chunks(dq), chunks(dk), rows(dvw), rows(gvw), chunks(gqw), chunks(gkw), chunks(grw),
             chunks(f["w_out"][0]), queries, u[WOVEN:], chunks(pool), wide(wp),
             rows(zv[:, :512]), rows(zv[:, 512:]), chunks(zu), woven(chunks(ga), chunks(f["w_branch_a_2"][0])),
             woven(chunks(gb), chunks(f["w_branch_b_2"][0])), chunks(f["w_out_2"][0]), woven(up[:FC], up[FC:]),
             f["w_down_2"][0].reshape(FC, P, D), chunks(f["w_ple_gate_2"][0]),
             chunks(f["w_ple_2"][0]).reshape(2, 4, P, 256).transpose(0, 2, 1, 3).reshape(2, P, D)]
    w = np.concatenate(parts, 0)
    assert w.shape[0] == N_END, (w.shape, N_END)

    col = lambda v: v.reshape(-1, P).T
    pad = lambda v: np.concatenate([v, np.zeros(P - v.size, np.float32)])
    vecs = [col(f[n].reshape(-1)) for n in ("ln1_w", "ln2_w", "final_norm_w", "mix_norm_2", "pool_scale_2",
                                            "sgu_norm_2", "ffn_norm_2", "ple_norm_2", "final_norm_2")]
    vecs += [col(f["conv_w_2"][0].reshape(-1)), col(f["conv_b_2"][0]), f["da_subln_w"].T, f["gla_norm_w"].T]
    gf, gbk = f["gla_gate_b_f"][0].reshape(HEADS, DH), f["gla_gate_b_b"][0].reshape(HEADS, DH)
    vecs += [np.concatenate([gf, gbk], 1).T]
    vecs += [np.stack([pad(f[n][0]) for n in ("da_lambda_q1", "da_lambda_k1", "da_lambda_q2", "da_lambda_k2")], 1)]
    w2 = np.zeros((32, HEADS, P), np.float32)
    w2[:16, :, :DH] = f["gla_gate_w2_f"][0].reshape(16, HEADS, DH)
    w2[16:, :, DH:] = f["gla_gate_w2_b"][0].reshape(16, HEADS, DH)
    fm = lambda x: x.T.reshape(-1, P, x.shape[0]).transpose(1, 0, 2)
    out = {
        "xT": fm(f["x"][0]), "metaT": fm(f["meta_tokens"]), "vec": np.concatenate(vecs, 1), "w": w,
        "w2": w2, "wz": np.concatenate([zf, zb], 1).reshape(KC, P, 32).transpose(1, 0, 2).reshape(P, KC * 32),
        "keysT": f["peer_sub_keys"][0].reshape(2 * PH, NK, P).transpose(2, 0, 1),
        "v": f["peer_v"][0].reshape(NK, P, D),
        "wsT": f["w_spatial_2"][0].transpose(2, 0, 1).reshape(P, 8 * P), "bsp": f["b_spatial_2"][0].reshape(1, D),
        "pT": fm(f["p_2"][0, 0]), **tables(),
    }
    return {n: np.ascontiguousarray(v) for n, v in out.items()}


def kernel(**inputs):
    import concourse.bacc as bacc
    from concourse.bass_utils import run_bass_kernel_spmd

    nc = bacc.Bacc("TRN2", target_bir_lowering=False, num_devices=1)
    arrays = layout(inputs)
    io = {n: nc.dram_tensor(f"in_{n}", v.shape, mybir.dt.from_np(v.dtype), kind="ExternalInput").ap()
          for n, v in arrays.items()}
    out = nc.dram_tensor("out", (P, KC, T), mybir.dt.float32, kind="ExternalOutput").ap()
    build(nc, io, out)
    r = run_bass_kernel_spmd(nc, [{f"in_{n}": v for n, v in arrays.items()}], core_ids=[0])
    y = r.results[0]["out"]
    return np.ascontiguousarray(y.transpose(2, 1, 0)).reshape(1, T, D)
```

```python
from contextlib import ExitStack

import concourse.bass as bass
import numpy as np
from concourse import mybir

P = 128
D = 1024
KC = D // P
T = 512
TT = T // P
M = 16
TM = T + M
HEADS = 4
DH = 64
ROPE = 8
LEVELS = (1, 2, 4, 8, 16, 32, 64, 128, 256)
NLEV = len(LEVELS)
SMALL = [s for s in LEVELS if s < P]
PH = 8
TOP = 16
NK = 128
FF = 2816
FC = FF // P
WINDOWS = (2, 4, 8, 16)
EPS = 1e-6
LAM_INIT = 0.8 - 0.6 * float(np.exp(0.0))
WS = 64.0
ISW = 1.0 / WS

SLOTS = 4
N_Q, N_K, N_V, N_GV, N_GQ, N_GK, N_GR = 0, 4, 8, 12, 16, 18, 20
N_WO = 24
N_PQ = 32
N_U = 48
N_POOL = N_U + NK
N_WP = N_POOL + 8
N_SV = N_WP + 4
N_SU = N_SV + 8
N_GA = N_SU + 8
N_GB = N_GA + 16
N_WO2 = N_GB + 16
N_UP = N_WO2 + 8
N_DN = N_UP + 2 * FC
N_PP = N_DN + FC
N_PG = N_PP + 2
N_END = N_PG + 8

VEC = {}
_at = 0
for _name, _n in (("ln1", 8), ("ln2", 8), ("final1", 8), ("mixn", 8), ("pscale", 8), ("sgun", 8), ("ffnn", 8),
                  ("plen", 8), ("final2", 8), ("convw", 6 * FC), ("convb", 2 * FC), ("subln", 1), ("glan", 1),
                  ("gateb", 4), ("lam", 4)):
    VEC[_name] = _at
    _at += _n
NVEC = _at
XL = 4

GRP = 4
GROUPS = NK // GRP
NT = 64
GT = T // NT
OCT = 8
WOVEN = 2 * PH
BEHIND = WOVEN + 2 * SLOTS
TURNS = GT + 3
EARLY = BEHIND + SLOTS * TURNS
EG = EARLY // GRP
LOW_POOL = N_PQ + SLOTS - 1
TURN_BANKS = (2, 3, 6)


def build(nc, io, out):
    f32, f16, u32, i32 = mybir.dt.float32, mybir.dt.float16, mybir.dt.uint32, mybir.dt.int32
    ALU, ACT, AX = mybir.AluOpType, mybir.ActivationFunctionType, mybir.AxisListType
    ctx = ExitStack()
    with ctx:

        def sem(name):
            return ctx.enter_context(nc.semaphore(name))

        WORDS = 48000
        arena = ctx.enter_context(nc.sbuf_tensor("arena", [P, WORDS], f32))
        psum = ctx.enter_context(nc.psum_tensor("psum", [P, 8 * 512], f32))

        class Region:
            def __init__(self, start):
                self.at = self.top = start

            def take(self, n, dt=f32):
                words = n if dt in (f32, u32, i32) else (n + 1) // 2
                v = arena[:, self.at:self.at + words]
                self.at += words
                assert self.at <= WORDS, self.at
                return v if dt is f32 else v.bitcast(dt)

        def v3(ap, a):
            return ap.rearrange("p (a b) -> p a b", a=a)

        def bank(b, n=512, off=0):
            return psum[:, b * 512 + off:b * 512 + off + n]

        base = Region(0)
        ident = base.take(P)
        ones = base.take(P)
        iota = base.take(P)
        perm = base.take(P)
        strip = base.take(P + 96)
        masks = v3(base.take((len(SMALL) + 1) * P, u32), len(SMALL) + 1)
        ropec = base.take(TM)
        ropes = base.take(TM)
        vec = base.take(NVEC)
        icnt = base.take(16)
        io16 = base.take(16)
        w2 = v3(base.take(HEADS * P), HEADS)
        wz = base.take(KC * 32)
        wzh = v3(base.take(KC * 32, f16), KC)
        wzl = v3(base.take(KC * 32, f16), KC)
        small = base.take(64)
        ring = base.at
        wraw = v3(base.take(SLOTS * D), SLOTS)
        wh = v3(base.take(SLOTS * D, f16), SLOTS)
        wl = v3(base.take(SLOTS * D, f16), SLOTS)
        ring_end, x_parts = base.at, base.at
        xsq = v3(arena[:, base.at:base.at + KC * T], KC)
        xh = v3(base.take(KC * TM, f16), KC)
        xl = v3(base.take(KC * TM, f16), KC)
        X = v3(base.take(KC * TM), KC)
        FREE = base.at

        r = Region(FREE)
        q = v3(r.take(HEADS * T), HEADS)
        k = v3(r.take(HEADS * TM), HEADS)
        dv = v3(r.take(5 * T), 5)
        pr = v3(r.take(4 * TM), 4)
        pa = v3(r.take(2 * TM), 2)
        aT = v3(r.take(5 * T), 5)
        rtmp = v3(r.take(2 * T), 2)
        gtmp = v3(Region(ring).take(4 * TM), 4)
        gv = v3(r.take(5 * T), 5)
        gq = v3(r.take(HEADS * T), HEADS)
        gk = v3(r.take(HEADS * TM), HEADS)
        sgr = v3(r.take(HEADS * T), HEADS)
        B = v3(r.take(HEADS * TM), HEADS)
        z32 = Region(r.at).take(TM)
        otmp = v3(r.take(4 * T), 4)
        first_end = r.at
        r = Region(FREE)
        Aflat = r.take(TT * (T + P))
        A = v3(Aflat[:, 0:TT * T], TT)
        Adiag = v3(Aflat, TT)[:, :, 0:P]
        Am = r.take(T)
        KTm = r.take(M)
        gstd = v3(r.take(2 * T), 2)
        r = Region(ring)
        kt8, qt8 = (r.take((NLEV - 1) * T) for _ in range(2))
        assert r.at <= ring_end
        KT, QT = ([v[:, i * T:(i + 1) * T] for i in range(NLEV - 1)] + [rtmp[:, j, :]]
                  for j, v in enumerate((kt8, qt8)))
        E = v3(Region(x_parts + HEADS * TM // 2).take(2 * T), 2)
        r = Region(FREE)
        r = Region(first_end)
        Em = r.take(TM)
        QTm = Em[:, 0:T]
        r = Region(FREE)
        nsq1 = v3(r.take(KC * TM), KC)
        nstd1 = r.take(TM)
        ninv1 = r.take(TM)
        r = Region(WORDS - 5300)
        nsq = v3(r.take(KC * TM), KC)
        nstd = r.take(P)
        ninv = r.take(P)

        r = Region(FREE)
        idx_tok = v3(r.take(3 * T), 3)
        idxT = v3(r.take(3 * T), 3)
        act_q = v3(arena[:, FREE:FREE + 4 * T], 4)
        gTh, gTl = r.take(T, f16), r.take(T, f16)
        region_v = r.at
        vraw = v3(r.take(SLOTS * D), SLOTS)
        region_g = r.at
        r = Region(region_v)
        hot_row, hot_slab, hot_high, hot_low = ([v3(r.take(OCT * P, f16), OCT) for _ in range(2)] for _ in range(4))
        assert r.at <= region_g
        r = Region(region_g)
        G = [v3(r.take(P * NT), P) for _ in range(2)]
        act_p = v3(r.take(4 * T), 4)
        r = Region(region_g)
        pq = v3(r.take(2 * T), 2)
        keysT = v3(r.take(2 * PH * P), 2 * PH)
        s_ = [v3(r.take(2 * T), 2) for _ in range(2)]
        s2 = v3(r.take(2 * T), 2)
        ts = v3(r.take(2 * TT * TOP), 2)
        ti = v3(r.take(2 * TT * TOP, u32), 2)
        tif = v3(r.take(2 * TT * TOP), 2)
        cand = v3(r.take(TT * 256), TT)
        cand2 = v3(r.take(TT * 256), TT)
        best = v3(r.take(TT * TOP), TT)
        pos = v3(r.take(TT * TOP, u32), TT)
        posab = v3(r.take(2 * TT * TOP, u32), 2)
        posf = v3(r.take(2 * TT * TOP), 2)
        sel = v3(r.take(2 * TT * 256), 2)
        gsm = r.take(TT * TOP)
        gsum = r.take(16)
        assert r.at <= WORDS
        r = Region(region_g)
        vh = v3(r.take(2 * GRP * D, f16), 2 * GRP)
        vl = v3(r.take(2 * GRP * D, f16), 2 * GRP)
        Ah = v3(r.take(2 * GRP * T, f16), 2 * GRP)
        Al = v3(r.take(2 * GRP * T, f16), 2 * GRP)
        GB = [v3(r.take(GT * GRP * NT), GT) for _ in range(2)]
        act_s = v3(r.take(GRP * T), GRP)
        at_s = v3(r.take(2 * T), 2)

        r = Region(FREE)
        ph_, pl_ = v3(r.take(KC * T, f16), KC), v3(r.take(KC * T, f16), KC)
        yh, yl = v3(r.take(KC * T, f16), KC), v3(r.take(KC * T, f16), KC)
        V2 = v3(r.take(KC * T), KC)
        U2 = v3(r.take(KC * T), KC)
        t2 = r.at
        zp = [r.take(T + 16) for _ in range(2)]
        win = [[r.take(T + 16) for _ in range(2)]]
        gat = v3(Region(t2).take(2 * T), 2)
        wsT = r.take(D)
        bsp = r.take(D)
        mt = r.at
        win.append([r.take(T + 16) for _ in range(2)])
        mtmp = v3(arena[:, mt:mt + 2 * T], 2)
        assert r.at <= WORDS - 5300
        r = Region(FREE)
        ggh, ggl = v3(r.take(FC * T, f16), FC), v3(r.take(FC * T, f16), FC)
        upb = [r.take(T + 2) for _ in range(4)]
        cv = v3(r.take(6 * T), 6)
        prw = v3(r.take(2 * T), 2)
        pth, ptl = v3(r.take(2 * T, f16), 2), v3(r.take(2 * T, f16), 2)
        assert r.at <= WORDS - 5300
        r = Region(FREE)
        pgs = v3(r.take(KC * T), KC)
        yout = v3(r.take(KC * T), KC)
        ptmp = v3(r.take(2 * T), 2)

        consts_in, vecs_in, ones_in, meta_in = sem("consts_in"), sem("vecs_in"), sem("ones_in"), sem("meta_in")
        x_in = [sem(f"x_in{i}") for i in range(XL)]
        slab_in = [sem(f"slab_in{i}") for i in range(SLOTS)]
        high_cut, low_cut, slab_done = sem("high_cut"), sem("low_cut"), sem("slab_done")
        vslab_in = [sem(f"vslab_in{i}") for i in range(SLOTS)]
        vhigh_cut, vlow_cut = sem("vhigh_cut"), sem("vlow_cut")
        slab_read = sem("slab_read")
        wz_high, wz_low = sem("wz_high"), sem("wz_low")
        dve_step, act_step, pool_step = sem("dve_step"), sem("act_step"), sem("pool_step")

        def slot(n):
            return n % SLOTS

        gmat = nc.dram_tensor("gate_matrix", [GT, P, NK * NT], f32, kind="Internal").ap()
        early = nc.dram_tensor("early_activations", [EARLY, P, T], f32, kind="Internal").ap()

        class Chain:

            def __init__(self, eng, s):
                self.eng, self.s, self.n, self.off = eng, s, 0, 0

            def link(self, ins):
                ins.then_inc(self.s, 1)
                self.n += 1
                self.eng.wait_ge(self.s, self.off + self.n)

            def enter(self, off):
                self.off, self.first = off, self.n

            def leave(self, per, times):
                assert self.n - self.first == per, (self.n - self.first, per)
                self.n, self.off = self.first + per * times, 0

        dchain = Chain(None, dve_step)

        sq_act, ss_done, std_done = sem("sq_act"), sem("ss_done"), sem("std_done")
        inv_done, spread_done = sem("inv_done"), sem("spread_done")
        xn_done, xh_done, xl_done = sem("xn_done"), sem("xh_done"), sem("xl_done")
        POOLED, FIRST = ("ln2", "ffnn", "final2"), 6
        squares_added = sem("squares_added")
        NORMS = ("ln1", "ln2", "final1", "mixn", "ffnn", "plen", "final2")

        def roots_table(i):
            nc.scalar.activation(small[:, 48 + i:49 + i], EPSC, ACT.Sqrt)

        class Norm:

            def __init__(self, name, b):
                self.i = NORMS.index(name)
                self.b = b
                self.w, self.meta = VEC[name], name == "ln1"
                self.cut = name not in ("final1", "final2")
                self.nth = sum(n not in ("final1", "final2") for n in NORMS[:self.i])
                self.cols = TM if self.meta else T
                self.pooled = POOLED.index(name) if name in POOLED else None
                self.sq = nsq1 if self.meta else xsq if name == "final1" else nsq
                self.std = nstd1 if self.meta else nstd
                self.inv = ninv1 if self.meta else ninv

            def square(self, c):
                nc.scalar.activation(self.sq[:, c, 0:self.cols], X[:, c, 0:self.cols],
                                     ACT.Square).then_inc(sq_act, 1)
                if c == KC - 2 and self.i < len(NORMS) - 1:
                    roots_table(self.i)

            def act(self, act, meanwhile=lambda: None):
                act.wait_ge(ss_done, self.i + 1)
                nc.scalar.activation(self.std, bank(self.b, TM if self.meta else P), ACT.Sqrt, bias=EPSC,
                                     scale=1.0 / D).then_inc(std_done, 1)
                meanwhile()
                if self.cut:
                    for c in range(KC):
                        act.wait_ge(xn_done, self.nth * KC + c + 1)
                        nc.scalar.activation(xh[:, c, 0:self.cols], self.sq[:, c, 0:self.cols],
                                             ACT.Copy).then_inc(xh_done, 1)

            def sum(self, pe, c):
                first = c == 0
                if self.pooled is not None and c < FIRST:
                    if c < FIRST - 1:
                        return
                    pe.wait_ge(squares_added, (self.pooled + 1) * (FIRST - 1))
                    c, first = 0, True
                else:
                    pe.wait_ge(sq_act, self.i * KC + c + 1)
                if self.meta:
                    nc.tensor.matmul(bank(self.b), ones, self.sq[:, c, 0:T], start=c == 0, stop=c == KC - 1)
                    last = nc.tensor.matmul(bank(self.b + 1, M), ones, self.sq[:, c, T:TM], start=c == 0,
                                            stop=c == KC - 1)
                else:
                    for t in range(TT):
                        last = nc.tensor.matmul(bank(self.b, P), strip[:, 96 - 32 * t:96 - 32 * t + P],
                                                self.sq[:, c, t * P:(t + 1) * P], start=first and t == 0,
                                                stop=c == KC - 1 and t == TT - 1)
                if c == KC - 1:
                    last.then_inc(ss_done, 1)

            def add_squares(self, pool):
                for c in range(1, FIRST):
                    pool.wait_ge(sq_act, self.i * KC + c + 1)
                    if c > 1:
                        pool.wait_ge(squares_added, self.pooled * (FIRST - 1) + c - 1)
                    nc.gpsimd.tensor_tensor(self.sq[:, 0, 0:T], self.sq[:, 0, 0:T], self.sq[:, c, 0:T],
                                            ALU.add).then_inc(squares_added, 1)

            def spread(self, pe):
                pe.wait_ge(inv_done, self.i)
                for t in range(TT):
                    last = nc.tensor.matmul(bank(self.b, P, t * P), ident[:, 32 * t:32 * t + 1].to_broadcast([P, P]),
                                            self.inv, start=True, stop=True)
                last.then_inc(spread_done, 1)

            def dve(self, dve, dst=None, done=None):
                dve.wait_ge(std_done, self.i + 1)
                if self.meta:
                    dchain.link(nc.vector.reciprocal(self.inv, self.std))
                    inv = self.inv
                else:
                    nc.vector.reciprocal(self.inv, self.std).then_inc(inv_done, 1)
                    dve.wait_ge(spread_done, self.i)
                    inv = bank(self.b)
                for c in range(KC + 1):
                    if c < KC:
                        o = dst[:, c, 0:T] if dst is not None else self.sq[:, c, 0:self.cols]
                        nc.vector.scalar_tensor_tensor(
                            out=o, in0=X[:, c, 0:self.cols], scalar=vec[:, self.w + c:self.w + c + 1],
                            in1=inv, op0=ALU.mult,
                            op1=ALU.mult).then_inc(xn_done if self.cut else done, 1)
                    if c and self.cut:
                        dve.wait_ge(xh_done, self.nth * KC + c)
                        nc.vector.tensor_tensor(xl[:, c - 1, 0:self.cols], self.sq[:, c - 1, 0:self.cols],
                                                xh[:, c - 1, 0:self.cols], ALU.subtract).then_inc(xl_done, 1)

            def wait_cut(self, pe, c=KC - 1):
                pe.wait_ge(xl_done, self.nth * KC + c + 1)

        EPSC = small[:, 0:1]
        NLAM = small[:, 1:2]
        SUBW = small[:, 2:3]
        LAMP = small[:, 4:6]
        LAME = small[:, 6:8]
        nmx = small[:, 8:12]
        zs = small[:, 12:16]
        rzs = small[:, 16:24]
        vss = small[:, 24:32]
        vrs = small[:, 32:40]
        PSC = small[:, 56:64]
        one = ones[:, 0:1]

        def wait(eng, s, v):
            if not isinstance(v, int) or v > 0:
                eng.wait_ge(s, v)

        def cut_high(act, g, s):
            act.wait_ge(slab_in[s], g * 16 + 16)
            wait(act, slab_done, g * SLOTS + (s + 1 - SLOTS))
            nc.scalar.activation(wh[:, s, :], wraw[:, s, :], ACT.Copy, scale=WS).then_inc(high_cut, 1)

        def cut_high_scaled(act, g, s):
            act.wait_ge(slab_in[s], g * 16 + 16)
            wait(act, slab_done, g * SLOTS + (s + 1 - SLOTS))
            nc.scalar.activation(wh[:, s, :], wraw[:, s, :], ACT.Copy, scale=WS).then_inc(slab_read, 1)
            act.wait_ge(slab_read, g * SLOTS + (s + 1 - LOW_POOL))
            nc.scalar.activation(wraw[:, s, :], wraw[:, s, :], ACT.Copy, scale=WS).then_inc(high_cut, 1)

        def cut_low(dve, g, s):
            dve.wait_ge(high_cut, g * SLOTS + (s + 1))
            nc.vector.scalar_tensor_tensor(out=wl[:, s, :], in0=wraw[:, s, :], scalar=WS, in1=wh[:, s, :],
                                           op0=ALU.mult, op1=ALU.subtract).then_inc(low_cut, 1)

        def cut_low_scaled(pool, g, s):
            pool.wait_ge(high_cut, g * SLOTS + (s + 1))
            nc.gpsimd.tensor_tensor(wl[:, s, :], wraw[:, s, :], wh[:, s, :], ALU.subtract).then_inc(low_cut, 1)

        class Cuts:

            def __init__(self, eng, cut):
                self.eng, self.cut, self.n = eng, cut, 0

            def upto(self, n):
                while self.n <= min(n, N_END - 1):
                    self.cut(self.eng, self.n // SLOTS, slot(self.n))
                    self.n += 1

            def ahead(self, g, s):
                s += SLOTS - 1
                self.cut(self.eng, g + s // SLOTS, s % SLOTS)

        def parts(ps, a_h, a_l, b_h, b_l, first, last):
            nc.tensor.matmul(ps, a_h, b_h, start=first, stop=False)
            nc.tensor.matmul(ps, a_h, b_l, start=False, stop=False)
            return nc.tensor.matmul(ps, a_l, b_h, start=False, stop=last)

        def chunk_pair(pe, n, banks, norm):
            for i in range(2):
                pe.wait_ge(low_cut, n + i + 1)
            for c in range(KC):
                norm.wait_cut(pe, c)
                for i in range(2):
                    last = parts(banks[i], *wslab(slot(n + i), c), xh[:, c, 0:T], xl[:, c, 0:T], c == 0, c == KC - 1)
                    if c == KC - 1:
                        last.then_inc(slab_done, 1)

        def value_bank(part, t):
            return (5 * part + t) % 8

        G_BANKS = {N_GQ: 2, N_GQ + 1: 3, N_GK: 4, N_GK + 1: 0}
        G_META = {N_GK: 1, N_GK + 1: 5}

        def wslab(sl, c, n=P):
            return wh[:, sl, c * n:(c + 1) * n], wl[:, sl, c * n:(c + 1) * n]

        def chunk(pe, n, sl, ps, sh=None, slo=None, kc=KC, meta=None, norm=None, half=None):
            sh = xh if sh is None else sh
            slo = xl if slo is None else slo
            pe.wait_ge(low_cut, n + 1)
            for c in range(kc) if half is None else range(half * kc // 2, (half + 1) * kc // 2):
                if norm is not None:
                    norm.wait_cut(pe, c)
                a = wslab(sl, c)
                last = parts(ps, *a, sh[:, c, 0:T], slo[:, c, 0:T], c == 0, c == kc - 1)
                if meta is not None:
                    last = parts(meta, *a, sh[:, c, T:TM], slo[:, c, T:TM], c == 0, c == kc - 1)
            if half != 0:
                last.then_inc(slab_done, 1)

        proj_out = sem("proj_out")
        rope_in, rope_mul, rope_out = sem("rope_in"), sem("rope_mul"), sem("rope_out")
        values_out = sem("values_out")
        z_done, z_out, gate_mm, gate_abs, gate_ln, gate_out = (
            sem("z_done"), sem("z_out"), sem("gate_mm"), sem("gate_abs"), sem("gate_ln"), sem("gate_out"))
        sig_out, silu_out = sem("sig_out"), sem("silu_out")
        lam_prod, lam_sum, lam_exp = sem("lam_prod"), sem("lam_sum"), sem("lam_exp")
        score_done, max_done, exp_done, diff_done = (sem("score_done"), sem("max_done"), sem("exp_done"),
                                                     sem("diff_done"))
        turn_done, turn_out, av_done, av_out = sem("turn_done"), sem("turn_out"), sem("av_done"), sem("av_out")
        osq_out, oss_done, ostd_out, oinv_out, oinv_spread, mixl_out = (
            sem("osq_out"), sem("oss_done"), sem("ostd_out"), sem("oinv_out"), sem("oinv_spread"),
            sem("mixl_out"))
        zeroed, e_in, e_exp, kt_out, qt_out, lev_done, lev_out = (
            sem("zeroed"), sem("e_in"), sem("e_exp"), sem("kt_out"), sem("qt_out"), sem("lev_done"),
            sem("lev_out"))
        em_in, em_exp, ktm_out, wide_done, wide_out, gav_done, gav_out = (
            sem("em_in"), sem("em_exp"), sem("ktm_out"), sem("wide_done"), sem("wide_out"), sem("gav_done"),
            sem("gav_out"))
        res_out = sem("res_out")
        NL = len(LEVELS)
        NS = len(SMALL)
        PREWORK = 5
        META_AT = 4
        keys_in, pq_out, s_done, s_out, head_done, gsub_out, gexp_out = (
            sem("keys_in"), sem("pq_out"), sem("s_done"), sem("s_out"), sem("head_done"), sem("gsub_out"),
            sem("gexp_out"))
        idx_turned, idxT_out = sem("idx_turned"), sem("idxT_out")
        hot_row_out, hot_slab_out, hot_gated, g_done, g_out = (sem("hot_row_out"), sem("hot_slab_out"),
                                                               sem("hot_gated"), sem("g_done"), sem("g_out"))
        sel_out, sel_times = sem("sel_out"), sem("sel_times")

        def sel4(side):
            return sel[:, side, :].rearrange("p (t k a) -> p t k a", t=TT, k=TOP)

        gates_cut, hot_low_out = sem("gates_cut"), sem("hot_low_out")
        act_stored = [sem(f"act_stored{i}") for i in range(4)]
        act_in = [sem(f"act_in{i}") for i in range(GRP)]
        g_stored, g_in = [sem(f"g_stored{i}") for i in range(2)], [sem(f"g_in{i}") for i in range(2)]
        gelu_out, gated_out, a_cut, b_done, acc_out = (sem("gelu_out"), sem("gated_out"), sem("a_cut"),
                                                       sem("b_done"), sem("acc_out"))
        final1_out = sem("final1_out")
        pads, small_in, masked = sem("pads"), sem("small_in"), sem("masked")
        psc_out, window_out, y_scaled, y_high = sem("psc_out"), sem("window_out"), sem("y_scaled"), sem("y_high")
        WIN_STEPS = [sum(i // 2 + 1 for i in range(c)) for c in range(KC + 1)]
        zpool_out, pool_cut, y_cut = sem("zpool_out"), sem("pool_cut"), sem("y_cut")
        v_out, vsq_out, vstd_out, v_normed = sem("v_out"), sem("vsq_out"), sem("vstd_out"), sem("v_normed")
        u_out, mix_done, mix_read, sgu_cut = sem("u_out"), sem("mix_done"), sem("mix_read"), sem("sgu_cut")
        gsig_out, branch_out, m_cut, res2_out = (sem("gsig_out"), sem("branch_out"), sem("m_cut"),
                                                 sem("res2_out"))
        up_out, conv_out, cgelu_out, ffn_cut = (sem("up_out"), sem("conv_out"),
                                                           sem("cgelu_out"), sem("ffn_cut"))
        down_out, p_in, p_high, p_low = (sem("down_out"), sem("p_in"),
                                                    sem("p_high"), sem("p_low"))
        pple_out = sem("pple_out")
        psig_out, ple_done, ple_out, y_out, stored = (sem("psig_out"), sem("ple_done"), sem("ple_out"),
                                                      sem("y_out"), sem("stored"))

        def blocks(ap, s, side):
            return ap.rearrange("p (n two s) -> p n two s", two=2, s=s)[:, :, side, :]

        def need_level_free(eng, h, li):
            if li <= NS:
                eng.wait_ge(lev_done, (h - 1) * (NS + 2) + li + 2)
            else:
                eng.wait_ge(wide_done, h)

        def decayed(eng, do, h, li, src, dst, side, done):
            s, u = LEVELS[li], h * NL + li
            eng.wait_ge(e_exp, u + 1)
            if h >= 1:
                need_level_free(eng, h, li)
            for half in range(2):
                rows = slice(DH * half, DH * (half + 1))
                sd = side ^ half
                do.tensor_tensor(blocks(dst[li][rows, :], s, sd), blocks(src[rows, h, 0:T], s, sd),
                                 blocks(E[rows, u % 2, :], s, sd), ALU.mult).then_inc(done, 1)

        block = ctx.enter_context(nc.Block())

        @block.sync
        def _(sp):
            sp.dma_start(X[:, :, T:TM], io["metaT"]).then_inc(meta_in, 16)
            for i in range(XL):
                c = slice(i * KC // XL, (i + 1) * KC // XL)
                sp.dma_start(X[:, c, 0:T], io["xT"][:, c, :]).then_inc(x_in[i], 16)
                if i == 0:
                    sp.dma_start(ones, io["ones"]).then_inc(ones_in, 16)
            sp.dma_start(vec, io["vec"]).then_inc(vecs_in, 16)
            for s in range(SLOTS):
                sp.dma_start(wraw[:, s, :], io["w"][s]).then_inc(slab_in[s], 16)
            for dst, name in ((ident, "ident"), (iota, "iota"), (perm, "perm"), (masks, "masks"), (ropec, "ropec"),
                              (ropes, "ropes"), (icnt, "icnt"), (io16, "io16"), (w2[0:32], "w2"), (wz, "wz"), (strip, "strip")):
                sp.dma_start(dst, io[name]).then_inc(consts_in, 16)

            def slabs(lo, hi):
                with sp.Fori(lo // SLOTS, hi // SLOTS) as g:
                    for s in range(SLOTS):
                        sp.wait_ge(low_cut, g * SLOTS + (s + 1 - SLOTS))
                        sp.dma_start(wraw[:, s, :], io["w"][bass.ds(g * SLOTS + s, 1)].rearrange(
                            "a p n -> p (a n)")).then_inc(slab_in[s], 16)

            slabs(SLOTS, N_WO)
            sp.wait_ge(wide_done, HEADS)
            slabs(N_WO, N_PQ + SLOTS)
            sp.wait_ge(res_out, KC)
            sp.dma_start(keysT, io["keysT"]).then_inc(keys_in, 16)
            slabs(N_PQ + SLOTS, N_U + BEHIND + (GT + 2) * SLOTS)
            for s in g_stored:
                sp.wait_ge(s, GT // 2 * 16)

            def load_group(g, par, inputs=True):
                wait(sp, gated_out, (g - 1) * GRP)
                sp.dma_start(GB[par], gmat[:, :, bass.ds(g * (GRP * NT), GRP * NT)].rearrange(
                    "t p n -> p t n")).then_inc(g_in[par], 16)
                for s in range(GRP):
                    wait(sp, vlow_cut, g * GRP + (s + 1 - GRP))
                    sp.dma_start(vraw[:, s, :], io["v"][bass.ds(g * GRP + s, 1)].rearrange(
                        "a p n -> p (a n)")).then_inc(vslab_in[s], 16)
                    if inputs:
                        n = g * GRP + (N_U + GRP + s)
                        sp.wait_ge(low_cut, n - (SLOTS - 1))
                        sp.dma_start(wraw[:, s, :], io["w"][bass.ds(n, 1)].rearrange(
                            "a p n -> p (a n)")).then_inc(slab_in[s], 16)
                    else:
                        wait(sp, gated_out, g * GRP + (s - 3))
                        if isinstance(g, int) and g == 0:
                            sp.wait_ge(act_stored[s], (BEHIND // 4 + GT) * 16)
                        else:
                            sp.wait_ge(act_stored[s], g * 16 + 16)
                        sp.dma_start(act_s[:, s, :], early[bass.ds(g * GRP + s, 1)].rearrange(
                            "a p n -> p (a n)")).then_inc(act_in[s], 16)

            load_group(0, 0, inputs=False)
            slabs(N_U + BEHIND + (GT + 2) * SLOTS, N_U + EARLY + SLOTS)
            load_group(1, 1, inputs=False)
            with sp.Fori(1, EG // 2) as o:
                load_group(o * 2, 0, inputs=False)
                load_group(o * 2 + 1, 1, inputs=False)
            load_group(EG - 1, 0, inputs=False)
            load_group(EG, 1)
            with sp.Fori(EG // 2 + 1, GROUPS // 2) as o:
                load_group(o * 2, 0)
                load_group(o * 2 + 1, 1)
            sp.wait_ge(acc_out, GROUPS * KC)
            sp.wait_ge(final1_out, KC)
            sp.dma_start(wsT, io["wsT"]).then_inc(small_in, 16)
            sp.dma_start(bsp, io["bsp"].partition_broadcast(P)).then_inc(small_in, 16)
            slabs(N_POOL + SLOTS, N_UP + SLOTS)
            sp.wait_ge(res2_out, KC)
            sp.dma_start(prw, io["pT"]).then_inc(p_in, 16)
            slabs(N_UP + SLOTS, N_END)
            for c in range(KC):
                sp.wait_ge(y_out, c + 1)
                sp.dma_start(out[:, c, :], yout[:, c, :]).then_inc(stored, 16)
            sp.wait_ge(stored, 16 * KC)

        @block.tensor
        def _(pe):
            pe.wait_ge(ones_in, 16)
            n1 = Norm("ln1", 0)
            for c in range(KC):
                n1.sum(pe, c)
            pe.wait_ge(lam_prod, 1)
            nc.tensor.matmul(bank(2, 2), ones[0:DH, :], LAMP[0:DH, :], start=True, stop=True).then_inc(lam_sum, 1)
            pe.wait_ge(consts_in, 176)
            pe.wait_ge(std_done, 1)
            def rope_swap(n):
                pe.wait_ge(rope_in, n + 1)
                src = q[:, n, :] if n < HEADS else k[:, n - HEADS, 0:T]
                if n >= 1:
                    pe.wait_ge(rope_mul, n)
                last = nc.tensor.matmul(bank(6), perm, src, start=True, stop=True)
                if n >= HEADS:
                    last = nc.tensor.matmul(bank(7, M), perm, k[:, n - HEADS, T:TM], start=True, stop=True)
                last.then_inc(rope_out, 1)

            for n in range(N_Q, N_V):
                if n >= 4:
                    pe.wait_ge(rope_in, n - 3 if n < 6 else n - 1)
                if n == N_Q:
                    chunk_pair(pe, n, (bank(0), bank(1)), n1)
                elif n > N_Q + 1:
                    if n == N_Q + 2:
                        pe.wait_ge(lam_exp, 1)
                    chunk(pe, n, slot(n), bank(n % 4), meta=bank(4 + n % 2, M) if n >= N_K else None)
                if n >= 1:
                    rope_swap(n - 1)
            rope_swap(N_V - 1)
            for part in range(2):
                if part == 0:
                    pe.wait_ge(rope_in, 8)
                else:
                    pe.wait_ge(rope_mul, 8)
                for g in range(4):
                    n = N_V + 4 * part + g
                    pe.wait_ge(low_cut, n + 1)
                    for c in range(2):
                        w_h, w_l = wslab(slot(n), c, 512)
                        for t in range(5):
                            cols = slice(t * P, (t + 1) * P) if t < TT else slice(T, TM)
                            b = value_bank(part, t)
                            if part == 1 and g + c == 0 and t >= 3:
                                pe.wait_ge(values_out, t - 2)
                            last = parts(psum[0:P if t < TT else M, b * 512:(b + 1) * 512],
                                         xh[:, 2 * g + c, cols], xl[:, 2 * g + c, cols], w_h, w_l,
                                         g == 0 and c == 0, g == 3 and c == 1)
                    last.then_inc(slab_done, 1)
            pe.wait_ge(values_out, 5)
            for n in range(N_GQ, N_GR):
                if n == N_GK:
                    pe.wait_ge(values_out, 10)
                chunk(pe, n, slot(n), bank(G_BANKS[n]), meta=bank(G_META[n], M) if n >= N_GK else None)
            pe.wait_ge(wz_low, 1)
            for c in range(KC):
                a = wzh[:, c, :], wzl[:, c, :]
                parts(psum[0:32, 6 * 512:7 * 512], *a, xh[:, c, 0:T], xl[:, c, 0:T], c == 0, c == KC - 1)
                last = parts(psum[0:32, 7 * 512:7 * 512 + M], *a, xh[:, c, T:TM], xl[:, c, T:TM], c == 0,
                             c == KC - 1)
            last.then_inc(z_done, 1)
            pe.wait_ge(proj_out, 4)
            for h in range(HEADS):
                n = N_GR + h
                chunk(pe, n, slot(n), bank(n % 4))
                if h == 0:
                    pe.wait_ge(z_out, 2)
                if h >= 1:
                    pe.wait_ge(gate_mm, h)
                nc.tensor.matmul(bank(4), w2[0:32, h, :], z32[0:32, 0:T], start=True, stop=True)
                nc.tensor.matmul(bank(5, M), w2[0:32, h, :], z32[0:32, T:TM], start=True,
                                 stop=True).then_inc(gate_abs, 1)

            def scores(turn):
                h, t = divmod(turn, TT)
                for c in range(2):
                    u = 2 * turn + c
                    if u >= 2:
                        pe.wait_ge(exp_done, u - 1)
                    rows = slice(DH * c, DH * (c + 1))
                    a = q[rows, h, t * P:(t + 1) * P]
                    nc.tensor.matmul(bank(2 * c), a, k[rows, h, 0:T], start=True, stop=True)
                    nc.tensor.matmul(bank(2 * c + 1, M), a, k[rows, h, T:TM], start=True,
                                     stop=True).then_inc(score_done, 1)

            def turn_over(turn):
                par = turn % 2
                pe.wait_ge(diff_done, turn + 1)
                if turn >= 2:
                    pe.wait_ge(turn_out, turn - 1)
                for j in range(TT):
                    nc.tensor.transpose(bank(4 + par, P, j * P), pa[:, par, j * P:(j + 1) * P], ident)
                if turn >= 1:
                    pe.wait_ge(turn_out, turn)
                nc.tensor.transpose(psum[0:M, 6 * 512 + par * P:6 * 512 + (par + 1) * P],
                                    pa[:, par, T:TM], ident).then_inc(turn_done, 1)

            def mix_values(h):
                pe.wait_ge(turn_out, TT * (h + 1))
                if h >= 1:
                    pe.wait_ge(av_out, h)
                cols = slice(h * P, (h + 1) * P)
                for j in range(TT):
                    nc.tensor.matmul(bank(7), dv[:, j, cols], aT[:, j, :], start=j == 0, stop=False)
                nc.tensor.matmul(bank(7), dv[0:M, TT, cols], aT[0:M, TT, :], start=False,
                                 stop=True).then_inc(av_done, 1)

            pe.wait_ge(silu_out, HEADS)
            pe.wait_ge(gate_mm, HEADS)
            for turn in range(HEADS * TT):
                scores(turn)
                if turn >= 1:
                    turn_over(turn - 1)
                    if turn % TT == 0:
                        mix_values(turn // TT - 1)
            turn_over(HEADS * TT - 1)
            mix_values(HEADS - 1)

            def head_sums(k, sqs):
                for h in range(HEADS):
                    pe.wait_ge(osq_out, k * HEADS + h + 1)
                    last = nc.tensor.matmul(bank(0), strip[:, 96 - 32 * h:96 - 32 * h + P], sqs[:, h, :],
                                            start=h == 0, stop=h == HEADS - 1)
                last.then_inc(oss_done, 1)

            def head_spread(k):
                pe.wait_ge(oinv_out, k + 1)
                for h in range(HEADS):
                    nc.tensor.matmul(bank(h), ident[:, 32 * h:32 * h + 1].to_broadcast([P, P]), gstd[:, k, :],
                                     start=True, stop=True).then_inc(oinv_spread, 1)

            head_sums(0, aT)

            def heads_values(h):
                pe.wait_ge(lev_out, (h + 1) * (NS + 2))
                pe.wait_ge(wide_out, 3 * (h + 1))
                if h >= 1:
                    pe.wait_ge(gav_out, h)
                cols = slice(h * P, (h + 1) * P)
                for j in range(TT):
                    nc.tensor.matmul(bank(3), gv[:, j, cols], A[:, j, :], start=j == 0, stop=False)
                nc.tensor.matmul(bank(3), gv[0:M, TT, cols], Am[0:M, :], start=False,
                                 stop=True).then_inc(gav_done, 1)

            units = [(h, li) for h in range(HEADS) for li in range(-1, NS + 1)]
            for u, (h, li) in enumerate(units):
                b = 4 + u % 3
                if u >= 3:
                    pe.wait_ge(lev_out, u - 2)
                if u == 0:
                    pe.wait_ge(av_out, HEADS)
                    pe.wait_ge(turn_out, HEADS * TT)
                if li >= 0:
                    pe.wait_ge(kt_out, 2 * (h * NL + li + 1))
                    pe.wait_ge(qt_out, 2 * (h * NL + li + 1))
                for j in range(TT):
                    jt = slice(j * P, (j + 1) * P)
                    i = j if li < NS else j ^ 1
                    it = slice(i * P, (i + 1) * P)
                    if li < 0:
                        last = nc.tensor.matmul(bank(b, P, j * P), gk[:, h, jt], gq[:, h, it], start=True,
                                                stop=True)
                    else:
                        last = nc.tensor.matmul(bank(b, P, j * P), KT[li][:, jt], QT[li][:, it], start=True,
                                                stop=True)
                last.then_inc(lev_done, 1)
                if li == 0 and h >= 1:
                    heads_values(h - 1)
                if li == 1 and h == 0:
                    head_spread(0)
                if li == NS:
                    pe.wait_ge(kt_out, 2 * (h * NL + NL))
                    pe.wait_ge(qt_out, 2 * (h * NL + NL))
                    if h == 0:
                        pe.wait_ge(mixl_out, 1)
                    else:
                        pe.wait_ge(wide_out, 3 * h)
                    for j in range(TT):
                        off = T // 2 if j < 2 else 0
                        last = nc.tensor.matmul(bank(j // 2, 256, 256 * (j % 2)),
                                                KT[NL - 1][:, j * P:(j + 1) * P],
                                                QT[NL - 1][:, off:off + 256], start=True, stop=True)
                    pe.wait_ge(ktm_out, 2 * (h + 1))
                    nc.tensor.matmul(psum[0:M, 2 * 512:3 * 512], KTm[0:DH, :], QTm[0:DH, :], start=True,
                                     stop=True).then_inc(wide_done, 1)
            heads_values(HEADS - 1)
            pe.wait_ge(gav_out, HEADS)
            head_sums(1, A)
            class Mixed:

                def wait_cut(self, pe, c):
                    pe.wait_ge(mixl_out, max(1, c - HEADS + 2))

            n2 = Norm("ln2", 3)
            pe.wait_ge(mixl_out, 1)
            for i in range(4):
                if i == 2:
                    head_spread(1)
                chunk(pe, N_WO + i, slot(N_WO + i), bank(4 + i), half=0)
            for n in range(N_WO, N_PQ):
                i = n - N_WO
                if i >= 4:
                    pe.wait_ge(res_out, i - 3)
                chunk(pe, n, slot(n), bank(4 + n % 4), norm=Mixed() if i == 0 else None, half=1 if i < 4 else None)
                if i:
                    n2.sum(pe, i - 1)
            n2.sum(pe, KC - 1)
            n2.spread(pe)

            pe.wait_ge(std_done, 2)
            pe.wait_ge(keys_in, 16)

            def key_scores(m, side):
                pe.wait_ge(pq_out, m + 1)
                wait(pe, s_out, m - 1)
                for t in range(TT):
                    last = nc.tensor.matmul(bank(2 + side, P, t * P), pq[:, side, t * P:(t + 1) * P],
                                            keysT[:, bass.ds(m, 1), :].rearrange("p a n -> p (a n)"),
                                            start=True, stop=True)
                last.then_inc(s_done, 1)

            def expert_input(e, n, s, b, half=None):
                wait(pe, gelu_out, e - 1)
                chunk(pe, n, s, bank(b), half=half)

            def query_turn(i):
                for hp in range(2):
                    m, n = i * 4 + 2 * hp, i * (2 * SLOTS) + (N_PQ + SLOTS * hp)
                    if isinstance(i, int) and hp == 0:
                        chunk_pair(pe, n, (bank(0), bank(1)), n2)
                    else:
                        for side in range(2):
                            wait(pe, pq_out, m + (side - 1))
                            chunk(pe, n + side, side, bank(side))
                    key_scores(m, 0)
                    expert_input(m, n + 2, 2, 4)
                    key_scores(m + 1, 1)
                    expert_input(m + 1, n + 3, 3, 5)

            query_turn(0)
            with pe.Fori(1, PH // 2) as i:
                query_turn(i)

            for e in range(WOVEN, BEHIND):
                expert_input(e, N_U + e, e % 4, 4 + e % 2)

            pe.wait_ge(head_done, PH)
            pe.wait_ge(s_out, 2 * PH)
            for v, b in enumerate(TURN_BANKS):
                for t in range(TT):
                    last = nc.tensor.transpose(bank(b, P, t * P), idx_tok[:, v, t * P:(t + 1) * P], ident)
                last.then_inc(idx_turned, 1)
            pe.wait_ge(pq_out, 2 * PH)

            def gate_octet(e, b, odd=None):
                pe.wait_ge(hot_row_out, e + 1)
                pe.wait_ge(hot_gated, e + 1)
                if b:
                    pe.wait_ge(hot_low_out, odd)
                for half in range(2):
                    wait(pe, g_out, e * 2 + (half - 3))
                    for tk in range(4 * half, 4 * half + 4):
                        ps = bank(2 * b + half, P, tk % 4 * P)
                        nc.tensor.matmul(ps, hot_row[b][:, tk, :], hot_high[b][:, tk, :], start=True, stop=False)
                        last = nc.tensor.matmul(ps, hot_row[b][:, tk, :], hot_low[b][:, tk, :], start=False,
                                                stop=True)
                    last.then_inc(g_done, 1)

            def tile_turn(t, octets=True):
                for s in range(SLOTS):
                    for half in range(2):
                        expert_input(t * SLOTS + (BEHIND + s), t * SLOTS + (N_U + BEHIND + s), s, 4 + s % 2,
                                     half)
                        if octets:
                            gate_octet(t * OCT + (2 * s + half), half, t * (OCT // 2) + (s + 1))

            tile_turn(0)
            with pe.Fori(1, GT) as t:
                tile_turn(t)
            for t in range(GT, TURNS):
                tile_turn(t, octets=False)

            pe.wait_ge(g_out, T // 4)

            def expert_group(g, par, inputs=True, outputs=True):
                gp, pp = g - 1, 1 - par
                for s in range(GRP):
                    if inputs:
                        expert_input(g * GRP + s, g * GRP + (N_U + s), s, s % 2)
                    if outputs:
                        if s == 0:
                            pe.wait_ge(a_cut, gp * GRP + GRP)
                            pe.wait_ge(vlow_cut, gp * GRP + GRP)
                        for c in (2 * s, 2 * s + 1):
                            wait(pe, acc_out, gp * KC + (c - 3))
                            for t in range(GRP):
                                x = pp * GRP + t
                                cols = slice(c * P, (c + 1) * P)
                                last = parts(bank(2 + c % 4), vh[:, x, cols], vl[:, x, cols], Ah[:, x, :],
                                             Al[:, x, :], t == 0, t == GRP - 1)
                            last.then_inc(b_done, 1)

            pe.wait_ge(gelu_out, EARLY)
            pe.wait_ge(idxT_out, 3)
            expert_group(1, 1, inputs=False)
            expert_group(2, 0, inputs=False)
            with pe.Fori(1, EG // 2) as o:
                expert_group(o * 2 + 1, 1, inputs=False)
                expert_group(o * 2 + 2, 0, inputs=False)
            with pe.Fori(EG // 2, GROUPS // 2 - 1) as o:
                expert_group(o * 2 + 1, 1)
                expert_group(o * 2 + 2, 0)
            expert_group(GROUPS - 1, 1)
            expert_group(GROUPS, 0, inputs=False)
            n3 = Norm("final1", 6)
            for c in range(KC):
                n3.sum(pe, c)
            n3.spread(pe)

            n4 = Norm("mixn", 7)
            for c in range(KC):
                n4.sum(pe, c)
            n4.spread(pe)
            pe.wait_ge(std_done, n4.i + 1)
            for n in range(N_POOL, N_WP):
                wait(pe, zpool_out, n - N_POOL - 3)
                if n == N_POOL:
                    chunk_pair(pe, n, (bank(0), bank(1)), n4)
                elif n > N_POOL + 1:
                    chunk(pe, n, slot(n), bank(n % 4))
            pe.wait_ge(zpool_out, KC)
            for n in range(N_WP, N_SV):
                g = n - N_WP
                pe.wait_ge(low_cut, n + 1)
                pe.wait_ge(pool_cut, 2 * g + 2)
                for o in range(2):
                    c = 2 * g + o
                    wait(pe, y_cut, c - 3)
                    for kk in range(2):
                        last = parts(bank(c % 4), *wslab(slot(n), 2 * o + kk), ph_[:, 2 * g + kk, :],
                                     pl_[:, 2 * g + kk, :], kk == 0, kk == 1)
                last.then_inc(slab_done, 1)
            for half in range(2):
                if half == 1:
                    pe.wait_ge(y_cut, KC)
                for g in range(4):
                    n = N_SV + 4 * half + g
                    pe.wait_ge(low_cut, n + 1)
                    for c in range(2):
                        w_h, w_l = wslab(slot(n), c, 512)
                        for t in range(TT):
                            cols = slice(t * P, (t + 1) * P)
                            last = parts(bank(4 * (1 - half) + t), xh[:, 2 * g + c, cols], xl[:, 2 * g + c, cols],
                                         w_h, w_l, g == 0 and c == 0, g == 3 and c == 1)
                    last.then_inc(slab_done, 1)
            def mix_tokens(h):
                if h == 0:
                    pe.wait_ge(masked, 1)
                    pe.wait_ge(v_normed, TT)
                wait(pe, mix_read, h - 1)
                for t in range(TT):
                    last = nc.tensor.matmul(bank(6 + h % 2, P, t * P),
                                            V2[:, 2 * t + h // 4, h % 4 * P:(h % 4 + 1) * P],
                                            wsT[:, h * P:(h + 1) * P], start=True, stop=True)
                last.then_inc(mix_done, 1)

            pe.wait_ge(v_out, TT)
            for n in range(N_SU, N_GA):
                h = n - N_SU
                wait(pe, u_out, h - 1)
                chunk(pe, n, slot(n), bank(4 + h % 2))
                if h >= 2:
                    mix_tokens(h - 2)
            for h in (KC - 2, KC - 1):
                mix_tokens(h)
            pe.wait_ge(u_out, KC)
            for n in range(N_GA, N_WO2):
                i = n - N_GA
                b = i // 2
                if i % 2 == 0:
                    wait(pe, gsig_out, b - 1)
                    chunk(pe, n, slot(n), bank(n % 4))
                else:
                    if b == KC:
                        pe.wait_ge(sgu_cut, KC)
                    wait(pe, branch_out, b - 1)
                    a = (yh, yl) if b < KC else (ph_, pl_)
                    chunk(pe, n, slot(n), bank(n % 4), *a)
            pe.wait_ge(branch_out, 2 * KC)
            pe.wait_ge(m_cut, KC)
            n5 = Norm("ffnn", 7)
            for n in range(N_WO2, N_UP):
                c = n - N_WO2
                wait(pe, res2_out, c - 3)
                chunk(pe, n, slot(n), bank(n % 4), yh, yl)
                if c:
                    n5.sum(pe, c - 1)
            n5.sum(pe, KC - 1)
            n5.spread(pe)

            pe.wait_ge(std_done, n5.i + 1)

            def up_turn(i):
                for s in range(SLOTS):
                    if isinstance(i, int) and s < 2:
                        if s == 0:
                            chunk_pair(pe, N_UP, (bank(0), bank(1)), n5)
                    else:
                        wait(pe, up_out, i * SLOTS + (s - 3))
                        chunk(pe, i * SLOTS + (N_UP + s), s, bank(s))

            up_turn(0)
            with pe.Fori(1, FC // 2) as i:
                up_turn(i)

            def down(f, s, first=False, last=False):
                pe.wait_ge(low_cut, f + (N_DN + 1))
                fi = bass.ds(f, 1)
                b_h, b_l = (x[:, fi, :].rearrange("p a n -> p (a n)") for x in (ggh, ggl))
                for c in range(KC):
                    ins = parts(bank(c), *wslab(s, c), b_h, b_l, first, last)
                ins.then_inc(slab_done, 1)

            pe.wait_ge(up_out, 2 * FC)
            pe.wait_ge(ffn_cut, FC)
            for f in range(SLOTS):
                down(f, f, first=f == 0)
            with pe.Fori(1, FC // SLOTS) as i:
                for s in range(SLOTS):
                    down(i * SLOTS + s, s)
            for f in range(FC // SLOTS * SLOTS, FC):
                down(f, f % SLOTS, last=f == FC - 1)

            n6 = Norm("plen", 0)
            for c in range(KC):
                n6.sum(pe, c)
            pe.wait_ge(p_low, 1)
            for c in range(KC):
                n = N_PP + c // 4
                pe.wait_ge(low_cut, n + 1)
                if c == 2:
                    n6.spread(pe)
                if c == KC - 1:
                    pe.wait_ge(pple_out, 1)
                for kk in range(2):
                    last = parts(bank(c + 1 if c < KC - 1 else 1), *wslab(slot(n), 2 * (c % 4) + kk), pth[:, kk, :],
                                 ptl[:, kk, :], kk == 0, kk == 1)
                last.then_inc(slab_done if c % 4 == 3 else ple_done, 1)
            n7 = Norm("final2", 0)
            for n in range(N_PG, N_END):
                i = n - N_PG
                pe.wait_ge(pple_out, min(i + 2, KC))
                wait(pe, psig_out, i - 3)
                if i == 0:
                    pe.wait_ge(pple_out, 3)
                    chunk_pair(pe, n, (bank(2), bank(3)), n6)
                elif i > 1:
                    chunk(pe, n, slot(n), bank(2 + i % 4))
                if i:
                    n7.sum(pe, i - 1)
            n7.sum(pe, KC - 1)
            n7.spread(pe)

        @block.scalar
        def _(act):
            chain = Chain(act, act_step)
            cuts = Cuts(act, cut_high)
            act.wait_ge(pool_step, 1)
            n1 = Norm("ln1", 0)
            act.wait_ge(meta_in, 16)
            for c in range(KC):
                if c % (KC // XL) == 0:
                    act.wait_ge(x_in[c * XL // KC], 16)
                n1.square(c)
            cuts.upto(2)
            n1.act(act)
            act.wait_ge(lam_sum, 1)
            nc.scalar.activation(LAME, bank(2, 2), ACT.Exp).then_inc(lam_exp, 1)
            for n in range(N_Q, N_V):
                cuts.upto(n + 3)
                act.wait_ge(slab_done, n + 1)
                if n < N_K:
                    nc.scalar.activation(q[:, n, :], bank(n % 4), ACT.Copy, scale=ISW / 8).then_inc(rope_in, 1)
                else:
                    nc.scalar.activation(k[:, n - N_K, T:TM], bank(4 + n % 2, M), ACT.Copy, scale=ISW)
                    nc.scalar.activation(k[:, n - N_K, 0:T], bank(n % 4), ACT.Copy, scale=ISW).then_inc(rope_in, 1)
            act.wait_ge(consts_in, 176)
            nc.scalar.activation(wzh.rearrange("p a b -> p (a b)"), wz, ACT.Copy, scale=WS).then_inc(wz_high, 1)
            for part in range(2):
                cuts.upto(N_V + 4 * part + 7)
                act.wait_ge(slab_done, N_V + 4 * part + 4)
                dst = (dv, gv)[part]
                for t in range(5):
                    rows = P if t < TT else M
                    b = value_bank(part, t)
                    nc.scalar.activation(dst[0:rows, t, :], psum[0:rows, b * 512:(b + 1) * 512], ACT.Copy,
                                         scale=ISW).then_inc(values_out, 1)
            for n in range(N_GQ, N_GR):
                cuts.upto(n + 3)
                act.wait_ge(slab_done, n + 1)
                for c in range(2):
                    rows = slice(DH * c, DH * (c + 1))
                    for half in range(2):
                        d = slice(DH * half, DH * (half + 1))
                        if n < N_GK:
                            last = nc.scalar.activation(gq[d, 2 * (n - N_GQ) + c, :],
                                                        bank(G_BANKS[n])[rows], ACT.Copy,
                                                        scale=ISW / 8)
                        else:
                            h = 2 * (n - N_GK) + c
                            nc.scalar.activation(gk[d, h, T:TM],
                                                 bank(G_META[n], M)[rows],
                                                 ACT.Copy, scale=ISW)
                            last = nc.scalar.activation(gk[d, h, 0:T],
                                                        bank(G_BANKS[n])[rows], ACT.Copy,
                                                        scale=ISW)
                last.then_inc(proj_out, 1)
            act.wait_ge(z_done, 1)
            nc.scalar.activation(z32[0:32, 0:T], psum[0:32, 6 * 512:7 * 512], ACT.Copy, scale=ISW).then_inc(z_out, 1)
            nc.scalar.activation(z32[0:32, T:TM], psum[0:32, 7 * 512:7 * 512 + M], ACT.Copy,
                                 scale=ISW).then_inc(z_out, 1)
            for n in range(N_GR, N_WO):
                cuts.upto(min(n + 3, N_WO - 1))
                act.wait_ge(slab_done, n + 1)
                h = n - N_GR
                nc.scalar.activation(sgr[:, h, :], bank(n % 4), ACT.Sigmoid, scale=ISW).then_inc(sig_out, 1)
                act.wait_ge(gate_abs, h + 1)
                bcol = vec[:, VEC["gateb"] + h:VEC["gateb"] + h + 1]
                nc.scalar.activation(B[:, h, 0:T], bank(4), ACT.Identity, bias=bcol)
                nc.scalar.activation(B[:, h, T:TM], bank(5, M), ACT.Identity, bias=bcol).then_inc(gate_mm, 1)

            def gate_log(h):
                act.wait_ge(gate_mm, h + 1)
                chain.link(nc.scalar.activation(gtmp[:, h, :], B[:, h, :], ACT.Abs))
                chain.link(nc.scalar.activation(gtmp[:, h, :], gtmp[:, h, :], ACT.Exp, scale=-1.0))
                nc.scalar.activation(gtmp[:, h, :], gtmp[:, h, :], ACT.Ln, bias=one).then_inc(gate_ln, 1)

            def level_exp(h, li):
                u = h * NL + li
                act.wait_ge(e_in, 2 * (u + 1))
                nc.scalar.activation(E[:, u % 2, :], E[:, u % 2, :], ACT.Exp, scale=1.0 / 16).then_inc(e_exp, 1)

            def turn_copy(turn):
                par, (h, t) = turn % 2, divmod(turn, TT)
                act.wait_ge(turn_done, turn + 1)
                if h >= 1 and t == 0:
                    act.wait_ge(av_done, h)
                nc.scalar.activation(aT[:, 0:TT, t * P:(t + 1) * P], v3(bank(4 + par), TT), ACT.Copy)
                nc.scalar.activation(aT[0:M, TT, t * P:(t + 1) * P],
                                     psum[0:M, 6 * 512 + par * P:6 * 512 + (par + 1) * P],
                                     ACT.Copy).then_inc(turn_out, 1)

            def head_out(h):
                act.wait_ge(av_done, h + 1)
                nc.scalar.activation(otmp[:, h, :], bank(7), ACT.Copy).then_inc(av_out, 1)

            for turn in range(HEADS * TT):
                for c in range(2):
                    u = 2 * turn + c
                    act.wait_ge(max_done, u + 1)
                    if turn >= 2:
                        act.wait_ge(diff_done, turn - 1)
                    nc.scalar.activation(pr[:, u % 4, :], psum[:, 2 * c * 512:2 * c * 512 + TM], ACT.Exp,
                                         bias=nmx[:, u % 4:u % 4 + 1],
                                         accum_out=zs[:, u % 4:u % 4 + 1]).then_inc(exp_done, 1)
                if turn >= 1:
                    turn_copy(turn - 1)
                    if turn % TT == 0:
                        head_out(turn // TT - 1)
                if turn < HEADS:
                    gate_log(turn)
                if PREWORK <= turn < PREWORK + NL:
                    level_exp(0, turn - PREWORK)
            turn_copy(HEADS * TT - 1)
            head_out(HEADS - 1)

            def head_norms(k, sqs):
                for h in range(HEADS):
                    nc.scalar.activation(sqs[:, h, :], otmp[:, h, :], ACT.Square).then_inc(osq_out, 1)
                act.wait_ge(oss_done, k + 1)
                nc.scalar.activation(gstd[:, k, :], bank(0), ACT.Sqrt, bias=EPSC,
                                     scale=1.0 / P).then_inc(ostd_out, 1)

            act.wait_ge(av_out, HEADS)
            act.wait_ge(exp_done, 2 * HEADS * TT)
            head_norms(0, aT)

            def head_values_out(h):
                act.wait_ge(gav_done, h + 1)
                if h == 0:
                    act.wait_ge(mixl_out, 1)
                nc.scalar.activation(otmp[:, h, :], bank(3), ACT.Copy).then_inc(gav_out, 1)

            for h in range(HEADS):
                for li in range(NL):
                    if h + 1 < HEADS:
                        level_exp(h + 1, li)
                    if li == 2 and h >= 1:
                        head_values_out(h - 1)
                    if li == META_AT:
                        act.wait_ge(em_in, h + 1)
                        nc.scalar.activation(Em[0:DH, T:TM], Em[0:DH, T:TM], ACT.Exp, scale=1.0 / 16)
                        nc.scalar.activation(Em[0:DH, 0:T], B[0:DH, h, 0:T], ACT.Exp,
                                             scale=1.0 / 16).then_inc(em_exp, 1)
                act.wait_ge(wide_done, h + 1)
                for half in range(2):
                    off = T // 2 if half == 0 else 0
                    nc.scalar.activation(A[:, 2 * half:2 * half + 2, off:off + 256], v3(bank(half), 2),
                                         ACT.Copy).then_inc(wide_out, 1)
                nc.scalar.activation(Am[0:M, :], psum[0:M, 2 * 512:3 * 512], ACT.Copy).then_inc(wide_out, 1)
            cuts.upto(N_WO + 3)
            head_values_out(HEADS - 1)
            act.wait_ge(gav_out, HEADS)
            head_norms(1, A)
            n2 = Norm("ln2", 3)
            for n in range(N_WO, N_PQ):
                cuts.upto(n + 3)
                act.wait_ge(res_out, n - N_WO + 1)
                n2.square(n - N_WO)

            n2.act(act)

            def query_out(m, n, side):
                act.wait_ge(slab_done, n + 1)
                wait(act, s_done, m - 1)
                nc.scalar.activation(pq[:, side, :], bank(side), ACT.Copy, scale=ISW).then_inc(pq_out, 1)

            def scores_out(m, head, hp, side):
                act.wait_ge(s_done, m + 1)
                wait(act, head_done, head - 1)
                nc.scalar.activation(s_[hp][:, side, :], bank(2 + side), ACT.Copy).then_inc(s_out, 1)

            def gate_exp(head):
                act.wait_ge(gsub_out, head + 1)
                nc.scalar.activation(gsm, gsm, ACT.Exp).then_inc(gexp_out, 1)

            def store_early(e, x, buf=act_p):
                act.wait_ge(gelu_out, e + 1)
                act.dma_start(early[bass.ds(e, 1)].rearrange("a p n -> p (a n)"),
                              buf[:, x, :]).then_inc(act_stored[x], 16)

            def early_gelu(e, n, x, b, k, buf=act_p, before=act_p):
                if not isinstance(e, int) or e > 0:
                    store_early(e - 1, (x - 1) % 4, before)
                act.wait_ge(slab_done, n + 1)
                wait(act, act_stored[x], k * 16)
                nc.scalar.activation(buf[:, x, :], bank(b), ACT.Gelu, scale=ISW).then_inc(gelu_out, 1)

            def query_turn(i):
                for hp in range(2):
                    m, n, g = i * 4 + 2 * hp, i * (2 * SLOTS) + (N_PQ + SLOTS * hp), i * 2 + (N_PQ // SLOTS + hp)
                    h = i * 2 + hp
                    for side in range(2):
                        cuts.ahead(g, side)
                        query_out(m + side, n + side, side)
                    for side in range(2):
                        cuts.ahead(g, 2 + side)
                        scores_out(m + side, h, hp, side)
                        if side == 1 and (not isinstance(h, int) or h > 0):
                            gate_exp(h - 1)
                        early_gelu(m + side, n + 2 + side, 2 * hp + side, 4 + side, i)

            cuts.cut = cut_high_scaled
            query_turn(0)
            with act.Fori(1, PH // 2) as i:
                query_turn(i)
            cuts.n += 4 * PH
            for e in range(WOVEN, BEHIND):
                if e == WOVEN + SLOTS:
                    gate_exp(PH - 1)
                cuts.upto(N_U + e + 3)
                early_gelu(e, N_U + e, e % 4, 4 + e % 2, e // 4)
            cuts.cut = cut_high

            for v, b in enumerate(TURN_BANKS):
                act.wait_ge(idx_turned, v + 1)
                nc.scalar.activation(idxT[:, v, :], bank(b), ACT.Copy).then_inc(idxT_out, 1)

            def tile_turn(t, par, octets=True):
                if octets:
                    wait(act, g_stored[par], t * 8 - 8 * par)
                for s in range(SLOTS):
                    if octets:
                        cuts.ahead(t + (N_U + BEHIND) // SLOTS, s)
                        for j in range(2 * s, 2 * s + 2):
                            for half in range(2):
                                act.wait_ge(g_done, t * (2 * OCT) + (2 * j + half + 1))
                                lo = j * OCT + 4 * half
                                nc.scalar.activation(G[par][:, :, lo:lo + 4].rearrange("p i n -> p n i"),
                                                     v3(bank(2 * (j % 2) + half), 4),
                                                     ACT.Copy).then_inc(g_out, 1)
                    if not octets:
                        cuts.ahead(t + (N_U + BEHIND) // SLOTS, s)
                    early_gelu(t * SLOTS + (BEHIND + s), t * SLOTS + (N_U + BEHIND + s), s, 4 + s % 2,
                               t + BEHIND // SLOTS, act_p if octets else act_q,
                               act_p if octets or (s == 0 and t == GT) else act_q)
                if octets:
                    act.wait_ge(g_out, t * (2 * OCT) + 2 * OCT)
                    act.dma_start(gmat[bass.ds(t, 1)].rearrange("a p n -> p (a n)"),
                                  G[par].rearrange("p i n -> p (i n)")).then_inc(g_stored[par], 16)

            act.wait_ge(head_done, PH)
            for t in range(2):
                tile_turn(t, t)
            with act.Fori(1, GT // 2) as o:
                for par in range(2):
                    tile_turn(o * 2 + par, par)
            def expert_group(g, par, inputs=True):
                for s in range(GRP):
                    if inputs:
                        cuts.ahead(g + N_U // SLOTS, s)
                    act.wait_ge(vslab_in[s], g * 16 + 16)
                    wait(act, b_done, (g - 1) * KC)
                    nc.scalar.activation(vh[:, par * GRP + s, :], vraw[:, s, :], ACT.Copy,
                                         scale=WS).then_inc(vhigh_cut, 1)
                    if inputs:
                        act.wait_ge(slab_done, g * GRP + (N_U + s + 1))
                        wait(act, gated_out, g * GRP + (s - 3))
                        nc.scalar.activation(act_s[:, s, :], bank(s % 2), ACT.Gelu,
                                             scale=ISW).then_inc(gelu_out, 1)

            for t in range(GT, TURNS - 1):
                tile_turn(t, 0, octets=False)
            act.wait_ge(g_stored[0], GT // 2 * 16)
            act.wait_ge(g_stored[1], GT // 2 * 16)
            expert_group(0, 0, inputs=False)
            tile_turn(TURNS - 1, 0, octets=False)
            store_early(EARLY - 1, 3, act_q)
            cuts.n += EARLY - BEHIND
            for g in range(1, 3):
                expert_group(g, g % 2, inputs=False)
            with act.Fori(1, EG // 2) as o:
                expert_group(o * 2 + 1, 1, inputs=False)
                expert_group(o * 2 + 2, 0, inputs=False)
            with act.Fori(EG // 2, GROUPS // 2 - 1) as o:
                expert_group(o * 2 + 1, 1)
                expert_group(o * 2 + 2, 0)
            expert_group(GROUPS - 1, 1)
            cuts.n += NK - EARLY
            n3, n4 = Norm("final1", 6), Norm("mixn", 7)
            for c in range(KC):
                act.wait_ge(acc_out, (GROUPS - 1) * KC + c + 1)
                n3.square(c)
            n3.act(act)

            for c in range(KC):
                act.wait_ge(final1_out, c + 1)
                n4.square(c)
            n4.act(act)
            act.wait_ge(pads, 2)
            act.wait_ge(psc_out, 1)
            for n in range(N_POOL, N_WP):
                c = n - N_POOL
                cuts.upto(n + 3)
                act.wait_ge(slab_done, n + 1)
                wait(act, pool_cut, c - 1)
                nc.scalar.activation(zp[c % 2][:, 16:16 + T], bank(n % 4), ACT.Copy,
                                     scale=ISW).then_inc(zpool_out, 1)
            for n in range(N_WP, N_SV):
                cuts.upto(n + 3)
                for c in (2 * (n - N_WP), 2 * (n - N_WP) + 1):
                    if c % 2 == 0:
                        act.wait_ge(slab_done, n + 1)
                    nc.scalar.activation(V2[:, c, :], bank(c % 4), ACT.Copy, scale=PSC[:, c:c + 1]).then_inc(
                        y_scaled, 1)
                    act.wait_ge(y_scaled, c + 1)
                    nc.scalar.activation(yh[:, c, :], V2[:, c, :], ACT.Copy).then_inc(y_high, 1)
            act.wait_ge(y_cut, KC)
            for half in range(2):
                cuts.upto(N_SV + 4 * half + 7)
                act.wait_ge(slab_done, N_SV + 4 * half + 4)
                for t in range(TT):
                    nc.scalar.activation(V2[:, 2 * t + half, :], bank(4 * (1 - half) + t), ACT.Gelu,
                                         scale=ISW).then_inc(v_out, 1)
            act.wait_ge(v_out, 2 * TT)
            for t in range(TT):
                nc.scalar.activation(U2[:, 2 * (t % 2):2 * (t % 2) + 2, :], V2[:, 2 * t:2 * t + 2, :], ACT.Square,
                                     accum_out=vss[:, t:t + 1]).then_inc(vsq_out, 1)
                act.wait_ge(vsq_out, t + 1)
            nc.scalar.activation(vrs[:, 0:TT], vss[:, 0:TT], ACT.Sqrt, bias=EPSC,
                                 scale=1.0 / D).then_inc(vstd_out, 1)
            for n in range(N_SU, N_GA):
                cuts.upto(n + 3)
                act.wait_ge(slab_done, n + 1)
                nc.scalar.activation(U2[:, n - N_SU, :], bank(4 + n % 2), ACT.Gelu, scale=ISW).then_inc(u_out, 1)
            act.wait_ge(sgu_cut, KC)
            for n in range(N_GA, N_WO2):
                i = n - N_GA
                b = i // 2
                cuts.upto(n + 3)
                if i % 2 == 0:
                    act.wait_ge(slab_done, n + 1)
                    wait(act, branch_out, b - 1)
                    nc.scalar.activation(gat[:, b % 2, :], bank(n % 4), ACT.Sigmoid,
                                         scale=ISW).then_inc(gsig_out, 1)
            n5 = Norm("ffnn", 7)
            for n in range(N_WO2, N_UP):
                cuts.upto(n + 3)
                act.wait_ge(res2_out, n - N_WO2 + 1)
                n5.square(n - N_WO2)

            n5.act(act)
            act.wait_ge(pads, 6)

            def up_turn(i):
                for pair in range(2):
                    for side in range(2):
                        s = 2 * pair + side
                        cuts.ahead(i + N_UP // SLOTS, s)
                        act.wait_ge(slab_done, i * SLOTS + (N_UP + s + 1))
                        wait(act, conv_out, i * SLOTS + (s - 3))
                        nc.scalar.activation(upb[s][:, 2:2 + T], bank(s), ACT.Copy,
                                             scale=ISW).then_inc(up_out, 1)
                    act.wait_ge(conv_out, i * SLOTS + (2 * pair + 1))
                    nc.scalar.activation(cv[:, 3 * pair + 2, :], cv[:, 3 * pair, :],
                                         ACT.Gelu).then_inc(cgelu_out, 1)

            up_turn(0)
            with act.Fori(1, FC // 2) as i:
                up_turn(i)
            cuts.n += 2 * FC
            cuts.upto(N_DN + 6)
            with act.Fori(1, FC // SLOTS) as i:
                for s in range(SLOTS):
                    cuts.ahead(i + N_DN // SLOTS, s)
            cuts.n += (FC // SLOTS - 1) * SLOTS
            act.wait_ge(p_in, 16)
            nc.scalar.activation(pth, prw, ACT.Copy).then_inc(p_high, 1)
            cuts.upto(N_PP + 2)
            n6 = Norm("plen", 0)
            for c in range(KC):
                act.wait_ge(down_out, c + 1)
                n6.square(c)
            def product_out(c):
                if c % 4 == 3:
                    act.wait_ge(slab_done, N_PP + c // 4 + 1)
                else:
                    act.wait_ge(ple_done, c - c // 4 + 1)
                nc.scalar.activation(yout[:, c, :], bank(c + 1 if c < KC - 1 else 1), ACT.Copy, scale=ISW).then_inc(pple_out, 1)

            cuts.upto(N_PG + 1)
            n6.act(act, lambda: [product_out(c) for c in range(3)])
            cuts.upto(N_PG + 2)
            for c in range(3, KC):
                product_out(c)
                if c == 4:
                    cuts.upto(N_PG + 3)
            n7 = Norm("final2", 0)
            for n in range(N_PG, N_END):
                cuts.upto(n + 3)
                c = n - N_PG
                if c:
                    act.wait_ge(ple_out, c)
                    n7.square(c - 1)
                act.wait_ge(slab_done, n + 1)
                nc.scalar.activation(pgs[:, c, :], bank(2 + c % 4), ACT.Sigmoid,
                                     scale=ISW).then_inc(psig_out, 1)
            roots_table(n7.i)
            act.wait_ge(ple_out, KC)
            n7.square(KC - 1)
            n7.act(act)

        @block.vector
        def _(dve):
            dchain.eng = dve
            cuts = Cuts(dve, cut_low)
            dve.wait_ge(vecs_in, 16)
            L = VEC["lam"]
            nc.vector.tensor_tensor(LAMP[0:DH, :], vec[0:DH, L:L + 4:2], vec[0:DH, L + 1:L + 4:2],
                                    ALU.mult).then_inc(lam_prod, 1)
            dve.wait_ge(meta_in, 16)
            for s in x_in:
                dve.wait_ge(s, 16)
            cuts.upto(2)
            n1 = Norm("ln1", 0)
            n1.dve(dve)
            dve.wait_ge(lam_exp, 1)
            dchain.link(nc.vector.tensor_tensor(NLAM, LAME[:, 1:2], LAME[:, 0:1], ALU.subtract))
            dchain.link(nc.vector.tensor_scalar(NLAM, NLAM, LAM_INIT, None, ALU.subtract))
            nc.vector.tensor_scalar(SUBW, vec[:, VEC["subln"]:VEC["subln"] + 1], 1.0 - LAM_INIT, None, ALU.mult)
            dve.wait_ge(consts_in, 176)

            def rope(n):
                dve.wait_ge(rope_out, n + 1)
                if n < HEADS:
                    dst, m = q[:, n, :], None
                else:
                    dst, m = k[:, n - HEADS, 0:T], k[:, n - HEADS, T:TM]
                a = nc.vector.tensor_tensor(rtmp[:, 0, :], bank(6), ropes[:, 0:T], ALU.mult)
                if m is not None:
                    a = nc.vector.tensor_tensor(rtmp[:, 1, 0:M], bank(7, M), ropes[:, T:TM], ALU.mult)
                a.then_inc(rope_mul, 1)
                a = nc.vector.tensor_tensor(dst, dst, ropec[:, 0:T], ALU.mult)
                if m is not None:
                    a = nc.vector.tensor_tensor(m, m, ropec[:, T:TM], ALU.mult)
                dchain.link(a)
                dve.wait_ge(rope_mul, n + 1)
                a = nc.vector.tensor_tensor(dst, dst, rtmp[:, 0, :], ALU.add)
                if m is not None:
                    a = nc.vector.tensor_tensor(m, m, rtmp[:, 1, 0:M], ALU.add)
                dchain.link(a)

            for n in range(N_Q, N_V):
                cuts.upto(n + 3)
                if n >= 1:
                    rope(n - 1)
            rope(N_V - 1)
            dve.wait_ge(wz_high, 1)
            nc.vector.scalar_tensor_tensor(out=wzl.rearrange("p a b -> p (a b)"), in0=wz, scalar=WS,
                                           in1=wzh.rearrange("p a b -> p (a b)"), op0=ALU.mult,
                                           op1=ALU.subtract).then_inc(wz_low, 1)
            cuts.upto(N_V + 11)
            for n in range(N_GQ, N_GR):
                cuts.upto(n + 3)
            for n in range(N_GR, N_WO):
                cuts.upto(min(n + 3, N_WO - 1))
                dve.wait_ge(sig_out, n - N_GR + 1)
                nc.vector.scalar_tensor_tensor(out=sgr[:, n - N_GR, :], in0=bank(n % 4), scalar=ISW,
                                               in1=sgr[:, n - N_GR, :], op0=ALU.mult,
                                               op1=ALU.mult).then_inc(silu_out, 1)

            def gate_sums(h):
                dve.wait_ge(gate_ln, h + 1)
                dchain.link(nc.vector.scalar_tensor_tensor(out=gtmp[:, h, :], in0=B[:, h, :], scalar=0.0,
                                                           in1=gtmp[:, h, :], op0=ALU.min, op1=ALU.subtract))
                nc.vector.tensor_tensor_scan(B[:, h, T:TM], one.to_broadcast([P, M]), gtmp[:, h, T:TM], 0.0,
                                             ALU.mult, ALU.add)
                dchain.link(nc.vector.tensor_tensor_scan(B[:, h, 0:T], one.to_broadcast([P, T]), gtmp[:, h, 0:T],
                                                         0.0, ALU.mult, ALU.add))
                nc.vector.tensor_tensor(B[DH:P, h, 0:T], B[DH:P, h, 0:T], gtmp[DH:P, h, 0:T],
                                        ALU.subtract).then_inc(gate_out, 1)

            def exponents(h, li):
                s, u = LEVELS[li], h * NL + li
                b = B[:, h, 0:T]
                ref = blocks(b, s, 0)[:, :, s - 1:s].to_broadcast([P, T // (2 * s), s])
                if u >= 2:
                    dve.wait_ge(kt_out, 2 * (u - 1))
                    dve.wait_ge(qt_out, 2 * (u - 1))
                nc.vector.tensor_tensor(blocks(E[:, u % 2, :], s, 0), ref, blocks(b, s, 0),
                                        ALU.subtract).then_inc(e_in, 1)
                nc.vector.tensor_tensor(blocks(E[:, u % 2, :], s, 1), blocks(b, s, 1), ref,
                                        ALU.subtract).then_inc(e_in, 1)

            def queries(h, li):
                decayed(dve, nc.vector, h, li, gq, QT, 1, qt_out)

            def scores_max(turn):
                for c in range(2):
                    u = 2 * turn + c
                    dve.wait_ge(score_done, u + 1)
                    nc.vector.tensor_reduce(nmx[:, u % 4:u % 4 + 1], psum[:, 2 * c * 512:2 * c * 512 + TM],
                                            AX.X, ALU.max, negate=True).then_inc(max_done, 1)

            def difference(turn):
                par = turn % 2
                dve.wait_ge(exp_done, 2 * turn + 2)
                rz_ = rzs[:, 4 * par:4 * par + 2]
                dchain.link(nc.vector.reciprocal(rz_, zs[:, 2 * par:2 * par + 2]))
                dchain.link(nc.vector.tensor_tensor(rz_[:, 1:2], rz_[:, 1:2], NLAM, ALU.mult))
                dchain.link(nc.vector.tensor_scalar(pr[:, 2 * par + 1, :], pr[:, 2 * par + 1, :],
                                                    rz_[:, 1:2], None, ALU.mult))
                if turn >= 2:
                    dve.wait_ge(turn_done, turn - 1)
                nc.vector.scalar_tensor_tensor(out=pa[:, par, :], in0=pr[:, 2 * par, :],
                                               scalar=rz_[:, 0:1], in1=pr[:, 2 * par + 1, :],
                                               op0=ALU.mult, op1=ALU.add).then_inc(diff_done, 1)

            for turn in range(HEADS * TT):
                if turn >= 1:
                    difference(turn - 1)
                scores_max(turn)
                if 1 <= turn <= HEADS:
                    gate_sums(turn - 1)
                li = turn - PREWORK
                if li == 0:
                    dve.wait_ge(gate_out, HEADS)
                if 0 <= li < NL:
                    exponents(0, li)
                if li == 1:
                    dve.wait_ge(zeroed, 1)
                if 1 <= li <= NL:
                    queries(0, li - 1)
            difference(HEADS * TT - 1)

            def head_inverse(k):
                dve.wait_ge(ostd_out, k + 1)
                nc.vector.reciprocal(gstd[:, k, :], gstd[:, k, :]).then_inc(oinv_out, 1)

            def head_norms(k, w):
                for h in range(HEADS):
                    dve.wait_ge(oinv_spread, k * HEADS + h + 1)
                    o, x = otmp[:, h, :], k * HEADS + h
                    dchain.link(nc.vector.scalar_tensor_tensor(out=o, in0=o, scalar=w, in1=bank(h),
                                                               op0=ALU.mult, op1=ALU.mult))
                    if k:
                        dchain.link(nc.vector.tensor_tensor(o, o, sgr[:, h, :], ALU.mult))
                    dchain.link(nc.vector.tensor_copy(xh[:, x, 0:T], o))
                    last = nc.vector.tensor_tensor(xl[:, x, 0:T], o, xh[:, x, 0:T], ALU.subtract)
                    if k or h == HEADS - 1:
                        last.then_inc(mixl_out, 1)

            for h in range(HEADS):
                def level_out(li):
                    u = h * (NS + 2) + li + 1
                    dve.wait_ge(lev_done, u + 1)
                    if li < 0 and h >= 1:
                        dve.wait_ge(gav_done, h)
                    if u >= 1:
                        dve.wait_ge(lev_out, u)
                    src = v3(bank(4 + u % 3), TT)
                    if li < NS:
                        mk = masks[:, li + 1:li + 2, :].to_broadcast([P, TT, P])
                        nc.vector.copy_predicated(Adiag, mk, src).then_inc(lev_out, 1)
                    else:
                        for j in range(TT):
                            i = j ^ 1
                            a = nc.vector.tensor_copy(A[:, j, i * P:(i + 1) * P], src[:, j, :])
                        a.then_inc(lev_out, 1)

                if h + 1 < HEADS:
                    exponents(h + 1, 0)
                for li in range(NL):
                    level_out(li - 1)
                    if li == META_AT:
                        if h >= 1:
                            dve.wait_ge(wide_done, h)
                        nc.vector.tensor_tensor(Em[0:DH, T:TM],
                                                B[0:DH, h, TM - 1:TM].to_broadcast([DH, M]), B[0:DH, h, T:TM],
                                                ALU.subtract).then_inc(em_in, 1)
                    if li == META_AT + 1:
                        dve.wait_ge(em_exp, h + 1)
                        nc.vector.tensor_tensor(KTm[0:DH, :], gk[0:DH, h, T:TM], Em[0:DH, T:TM],
                                                ALU.mult).then_inc(ktm_out, 1)
                        nc.vector.tensor_tensor(QTm[0:DH, :], gq[0:DH, h, 0:T], Em[0:DH, 0:T],
                                                ALU.mult).then_inc(ktm_out, 1)
                    if h == 0 and li == 0:
                        head_inverse(0)
                    if h == 0 and li == 3:
                        head_norms(0, SUBW)
                    if h + 1 < HEADS:
                        queries(h + 1, li)
                        if li + 1 < NL:
                            exponents(h + 1, li + 1)
            dve.wait_ge(silu_out, HEADS)
            cuts.upto(N_WO + 3)
            head_inverse(1)
            head_norms(1, vec[:, VEC["glan"]:VEC["glan"] + 1])

            for n in range(N_WO, N_PQ):
                cuts.upto(n + 3)
                dve.wait_ge(slab_done, n + 1)
                c = n - N_WO
                nc.vector.scalar_tensor_tensor(out=X[:, c, 0:T], in0=bank(4 + n % 4), scalar=ISW,
                                               in1=X[:, c, 0:T], op0=ALU.mult,
                                               op1=ALU.add).then_inc(res_out, 1)

            Norm("ln2", 3).dve(dve)

            def tiles(ap):
                return v3(ap, TT)

            def each(fn):
                for side in range(2):
                    for t in range(TT):
                        last = fn(side, t)
                return last

            def settled(ins):
                nc.vector.drain()

            def choose(head, sc):
                k8 = lambda side, t, lo: ts[:, side, t * TOP + lo:t * TOP + lo + 8]
                i8 = lambda side, t, lo: ti[:, side, t * TOP + lo:t * TOP + lo + 8]
                sk = lambda side, t: sc[:, side, t * P:(t + 1) * P]
                s2k = lambda side, t: s2[:, side, t * P:(t + 1) * P]
                settled(each(lambda a, t: nc.vector.max(k8(a, t, 0), sk(a, t))))
                settled(each(lambda a, t: nc.vector.match_replace(s2k(a, t), k8(a, t, 0), sk(a, t), LOWEST)))
                settled(each(lambda a, t: nc.vector.max(k8(a, t, 8), s2k(a, t))))
                each(lambda a, t: nc.vector.max_index(i8(a, t, 0), k8(a, t, 0), sk(a, t)))
                settled(each(lambda a, t: nc.vector.max_index(i8(a, t, 8), k8(a, t, 8), s2k(a, t))))
                nc.vector.tensor_copy(tif, ti)
                full = [P, TT, TOP, TOP]
                c4 = cand.rearrange("p t (a b) -> p t a b", a=TOP)
                settled(nc.vector.tensor_tensor(c4, tiles(ts[:, 0, :]).unsqueeze(3).to_broadcast(full),
                                                    tiles(ts[:, 1, :]).unsqueeze(2).to_broadcast(full), ALU.add))
                rng = range(TT)
                settled([nc.vector.max(best[:, t, 0:8], cand[:, t, :]) for t in rng][-1])
                settled([nc.vector.match_replace(cand2[:, t, :], best[:, t, 0:8], cand[:, t, :], LOWEST)
                             for t in rng][-1])
                settled([nc.vector.max(best[:, t, 8:16], cand2[:, t, :]) for t in rng][-1])
                g3 = v3(gsm, TT)
                nc.vector.tensor_tensor(g3, best, best[:, :, 0:1].to_broadcast([P, TT, TOP]),
                                        ALU.subtract).then_inc(gsub_out, 1)
                [nc.vector.max_index(pos[:, t, 0:8], best[:, t, 0:8], cand[:, t, :]) for t in rng]
                settled([nc.vector.max_index(pos[:, t, 8:16], best[:, t, 8:16], cand2[:, t, :])
                             for t in rng][-1])
                pf = pos.rearrange("p a b -> p (a b)")
                nc.vector.tensor_scalar(posab[:, 0, :], pf, 4, None, ALU.logical_shift_right)
                settled(nc.vector.tensor_scalar(posab[:, 1, :], pf, 15, None, ALU.bitwise_and))
                settled(nc.vector.tensor_copy(posf, posab))
                cols = bass.ds(head * TOP, TOP)
                for side in range(2):
                    ins = nc.vector.tensor_tensor(
                        sel4(side), tiles(posf[:, side, :]).unsqueeze(3).to_broadcast(full),
                        io16.unsqueeze(1).unsqueeze(1).to_broadcast(full), ALU.is_equal)
                    if side == 0:
                        ins.then_inc(sel_out, 1)
                settled(ins)
                settled(nc.vector.tensor_tensor(
                    sel4(1), sel4(1), tiles(tif[:, 1, :]).unsqueeze(2).to_broadcast(full), ALU.mult))
                dve.wait_ge(gexp_out, head + 1)
                settled(nc.vector.tensor_reduce(gsum[:, 0:TT], g3, AX.X, ALU.add))
                settled(nc.vector.reciprocal(gsum[:, 8:8 + TT], gsum[:, 0:TT]))
                nc.vector.tensor_tensor(tiles(idx_tok[:, 2, :])[:, :, cols], g3,
                                        gsum[:, 8:8 + TT].unsqueeze(2).to_broadcast([P, TT, TOP]),
                                        ALU.mult)
                for side in (1, 0):
                    if side == 0:
                        dve.wait_ge(sel_times, head + 1)
                    last = nc.vector.tensor_reduce(tiles(idx_tok[:, side, :])[:, :, cols], sel4(side), AX.X, ALU.add)
                last.then_inc(head_done, 1)

            def query_turn(i):
                for hp in range(2):
                    dve.wait_ge(s_out, i * 4 + (2 * hp + 2))
                    nc.vector.tensor_copy(gsum[:, 12 + hp:13 + hp], s_[hp][:, 0, 0:1])
                    choose(i * 2 + hp, s_[hp])

            LOWEST = -3.0e38
            query_turn(0)
            with dve.Fori(1, PH // 2) as i:
                query_turn(i)
            cuts.n += 4 * PH + BEHIND - WOVEN

            dve.wait_ge(idxT_out, 3)
            dchain.link(nc.vector.tensor_copy(gTh, idxT[:, 2, :]))
            nc.vector.tensor_tensor(gTl, idxT[:, 2, :], gTh, ALU.subtract).then_inc(gates_cut, 1)
            dve.wait_ge(low_cut, cuts.n)

            def one_hots(e, b, tok, slab, pair):
                full = [P, OCT, P]
                col = lambda v: idxT[:, v, bass.ds(tok, OCT)].unsqueeze(2).to_broadcast(full)
                numbers = iota.unsqueeze(1).to_broadcast(full)
                if slab:
                    wait(dve, hot_gated, e - 1)
                    if b:
                        wait(dve, hot_low_out, pair)
                    nc.vector.tensor_tensor(hot_slab[b], numbers, col(0), ALU.is_equal).then_inc(hot_slab_out, 1)
                else:
                    wait(dve, g_done, e * 2 - 2)
                    nc.vector.tensor_tensor(hot_row[b], numbers, col(1), ALU.is_equal).then_inc(hot_row_out, 1)
                    if b:
                        dve.wait_ge(hot_slab_out, e + 1)
                        low = gTl[:, bass.ds(tok, OCT)].unsqueeze(2).to_broadcast(full)
                        nc.vector.tensor_tensor(hot_low[b], hot_slab[b], low, ALU.mult).then_inc(hot_low_out, 1)

            def tile_turn(t, octets=True):
                for s in range(SLOTS):
                    if octets:
                        for slab, b in ((1, 0), (1, 1), (0, 0), (0, 1)):
                            one_hots(t * OCT + (2 * s + b), b, t * NT + (2 * s + b) * OCT, slab,
                                     t * (OCT // 2) + s)
                    cuts.ahead(t + (N_U + BEHIND) // SLOTS, s)

            tile_turn(0)
            with dve.Fori(1, GT) as t:
                tile_turn(t)

            def gated(g, par, s, inputs):
                if s == 0:
                    dve.wait_ge(g_in[par], (g // 2) * 16 + 16 if isinstance(g, int) else g * 8 + (16 - 8 * par))
                if inputs:
                    dve.wait_ge(gelu_out, g * GRP + (s + 1))
                else:
                    dve.wait_ge(act_in[s], g * 16 + 16)
                tl = lambda ap: v3(ap, GT)
                wait(dve, a_cut, g * GRP + (s - 1))
                nc.vector.tensor_tensor(tl(at_s[:, s % 2, :]), tl(act_s[:, s, :]),
                                        GB[par][:, :, s * NT:(s + 1) * NT], ALU.mult).then_inc(gated_out, 1)
                dve.wait_ge(gated_out, g * GRP + (s + 1))
                wait(dve, b_done, (g - 1) * KC)
                x = par * GRP + s
                dchain.link(nc.vector.tensor_copy(Ah[:, x, :], at_s[:, s % 2, :]))
                nc.vector.tensor_tensor(Al[:, x, :], at_s[:, s % 2, :], Ah[:, x, :],
                                        ALU.subtract).then_inc(a_cut, 1)

            def expert_group(g, par, inputs=True, outputs=True, last=False):
                gp = g - 1
                for s in range(GRP):
                    if inputs:
                        cuts.ahead(g + N_U // SLOTS, s)
                    if not last:
                        dve.wait_ge(vhigh_cut, g * GRP + (s + 1))
                        nc.vector.scalar_tensor_tensor(
                            out=vl[:, par * GRP + s, :], in0=vraw[:, s, :], scalar=WS,
                            in1=vh[:, par * GRP + s, :], op0=ALU.mult, op1=ALU.subtract).then_inc(vlow_cut, 1)
                        gated(g, par, s, inputs)
                    if outputs:
                        if s == 0:
                            wait(dve, acc_out, gp * KC)
                        for c in (2 * s, 2 * s + 1):
                            dve.wait_ge(b_done, gp * KC + (c + 1))
                            nc.vector.scalar_tensor_tensor(
                                out=X[:, c, 0:T], in0=bank(2 + c % 4), scalar=ISW, in1=X[:, c, 0:T],
                                op0=ALU.mult, op1=ALU.add).then_inc(acc_out, 1)

            for t in range(GT, TURNS - 1):
                tile_turn(t, octets=False)
            expert_group(0, 0, inputs=False, outputs=False)
            tile_turn(TURNS - 1, octets=False)
            cuts.n += EARLY - BEHIND
            expert_group(1, 1, inputs=False)
            expert_group(2, 0, inputs=False)
            with dve.Fori(1, EG // 2) as o:
                dchain.enter((o - 1) * (2 * GRP))
                expert_group(o * 2 + 1, 1, inputs=False)
                expert_group(o * 2 + 2, 0, inputs=False)
                dchain.leave(2 * GRP, EG // 2 - 1)
            with dve.Fori(EG // 2, GROUPS // 2 - 1) as o:
                dchain.enter((o - EG // 2) * (2 * GRP))
                expert_group(o * 2 + 1, 1)
                expert_group(o * 2 + 2, 0)
                dchain.leave(2 * GRP, GROUPS // 2 - 1 - EG // 2)
            expert_group(GROUPS - 1, 1)
            expert_group(GROUPS, 0, inputs=False, last=True)
            cuts.n += NK - EARLY
            Norm("final1", 6).dve(dve, dst=X, done=final1_out)

            Norm("mixn", 7).dve(dve)

            nc.vector.tensor_scalar(PSC, vec[:, VEC["pscale"]:VEC["pscale"] + KC], ISW, None,
                                    ALU.mult).then_inc(psc_out, 1)

            def cut_onto(src, h_, l_, done):
                dchain.link(nc.vector.tensor_copy(h_, src))
                nc.vector.tensor_tensor(l_, src, h_, ALU.subtract).then_inc(done, 1)

            for n in range(N_POOL, N_WP):
                c = n - N_POOL
                cuts.upto(n + 3)
                dve.wait_ge(window_out, WIN_STEPS[c + 1])
                z, src = zp[c % 2][:, 16:16 + T], win[c % 2][(c // 2) % 2]
                w = WINDOWS[c // 2]
                tmp = win[c % 2][(c // 2 + 1) % 2][:, 0:T]
                nc.vector.scalar_tensor_tensor(out=tmp[:, w:T], in0=src[:, 16 + w:16 + T], scalar=1.0 / w,
                                               in1=z[:, w:T], op0=ALU.mult, op1=ALU.subtract)
                dchain.link(nc.vector.tensor_tensor(tmp[:, 0:w], src[:, 16:16 + w], icnt[:, 0:w], ALU.mult))
                dchain.link(nc.vector.tensor_tensor(tmp[:, 0:w], tmp[:, 0:w], z[:, 0:w], ALU.subtract))
                cut_onto(tmp, ph_[:, c, :], pl_[:, c, :], pool_cut)
                dve.wait_ge(pool_cut, c + 1)
            for n in range(N_WP, N_SV):
                cuts.upto(n + 3)
                for c in (2 * (n - N_WP), 2 * (n - N_WP) + 1):
                    dve.wait_ge(y_high, c + 1)
                    nc.vector.tensor_tensor(yl[:, c, :], V2[:, c, :], yh[:, c, :], ALU.subtract).then_inc(y_cut, 1)
            cuts.upto(N_SV + 11)
            dve.wait_ge(vstd_out, 1)
            dchain.link(nc.vector.reciprocal(vrs[:, 4:8], vrs[:, 0:4]))
            for t in range(TT):
                nc.vector.tensor_scalar(V2[:, 2 * t:2 * t + 2, :], V2[:, 2 * t:2 * t + 2, :], vrs[:, 4 + t:5 + t],
                                        None, ALU.mult).then_inc(v_normed, 1)
            dve.wait_ge(small_in, 32)
            for n in range(N_SU, N_GA):
                h = n - N_SU
                cuts.upto(n + 3)
                dve.wait_ge(mix_done, h + 1)
                m = mtmp[:, h % 2, :]
                col = vec[:, VEC["sgun"] + h:VEC["sgun"] + h + 1]
                nc.vector.scalar_tensor_tensor(
                    out=v3(m, TT), in0=v3(bank(6 + h % 2), TT), scalar=col,
                    in1=bsp[:, h * P:(h + 1) * P].unsqueeze(1).to_broadcast([P, TT, P]), op0=ALU.mult,
                    op1=ALU.add).then_inc(mix_read, 1)
                dve.wait_ge(mix_read, h + 1)
                dve.wait_ge(u_out, h + 1)
                dchain.link(nc.vector.tensor_tensor(m, m, U2[:, h, :], ALU.mult))
                cut_onto(m, ph_[:, h, :], pl_[:, h, :], sgu_cut)
            for n in range(N_GA, N_WO2):
                i = n - N_GA
                b, c = i // 2, i // 2 % KC
                cuts.upto(n + 3)
                if i % 2:
                    dve.wait_ge(slab_done, n + 1)
                    dve.wait_ge(gsig_out, b + 1)
                    dst = V2[:, c, :] if b < KC else mtmp[:, b % 2, :]
                    nc.vector.scalar_tensor_tensor(out=dst, in0=bank(n % 4), scalar=ISW, in1=gat[:, b % 2, :],
                                                   op0=ALU.mult, op1=ALU.mult).then_inc(branch_out, 1)
                    if b >= KC:
                        dve.wait_ge(branch_out, b + 1)
                        dchain.link(nc.vector.tensor_tensor(V2[:, c, :], V2[:, c, :], mtmp[:, b % 2, :], ALU.add))
                        cut_onto(V2[:, c, :], yh[:, c, :], yl[:, c, :], m_cut)
            for n in range(N_WO2, N_UP):
                cuts.upto(n + 3)
                dve.wait_ge(slab_done, n + 1)
                c = n - N_WO2
                nc.vector.scalar_tensor_tensor(out=X[:, c, 0:T], in0=bank(n % 4), scalar=ISW,
                                               in1=X[:, c, 0:T], op0=ALU.mult,
                                               op1=ALU.add).then_inc(res2_out, 1)

            Norm("ffnn", 7).dve(dve)

            def conv(i, f, pair, side):
                s = 2 * pair + side
                dst = cv[:, 3 * pair + side, :]
                cw = lambda tap: vec[:, bass.ds(f + (VEC["convw"] + tap * 2 * FC + side * FC), 1)]
                cb = vec[:, bass.ds(f + (VEC["convb"] + side * FC), 1)]
                dve.wait_ge(up_out, i * SLOTS + (s + 1))
                dchain.link(nc.vector.tensor_scalar(dst, upb[s][:, 2:2 + T], cw(2), cb, ALU.mult, ALU.add))
                dchain.link(nc.vector.scalar_tensor_tensor(out=dst, in0=upb[s][:, 1:1 + T], scalar=cw(1), in1=dst,
                                                           op0=ALU.mult, op1=ALU.add))
                return nc.vector.scalar_tensor_tensor(out=dst, in0=upb[s][:, 0:T], scalar=cw(0), in1=dst,
                                                      op0=ALU.mult, op1=ALU.add)

            def up_turn(i):
                for pair in range(2):
                    f = i * 2 + pair
                    cuts.ahead(i + N_UP // SLOTS, 2 * pair)
                    a = conv(i, f, pair, 0)
                    a.then_inc(conv_out, 1)
                    cuts.ahead(i + N_UP // SLOTS, 2 * pair + 1)
                    conv(i, f, pair, 1).then_inc(conv_out, 1)
                    dve.wait_ge(conv_out, i * SLOTS + (2 * pair + 2))
                    dve.wait_ge(cgelu_out, i * 2 + (pair + 1))
                    p_ = cv[:, 3 * pair + 2, :]
                    dchain.link(nc.vector.tensor_tensor(p_, p_, cv[:, 3 * pair + 1, :], ALU.mult))
                    fi = bass.ds(f, 1)
                    flat = lambda x: x[:, fi, :].rearrange("p a n -> p (a n)")
                    cut_onto(p_, flat(ggh), flat(ggl), ffn_cut)

            first = dchain.n
            up_turn(0)
            per = dchain.n - first
            with dve.Fori(1, FC // 2) as i:
                dchain.enter((i - 1) * per)
                up_turn(i)
                dchain.leave(per, FC // 2 - 1)
            cuts.n += 2 * FC
            cuts.upto(N_DN + 6)
            with dve.Fori(1, FC // SLOTS) as i:
                for s in range(SLOTS):
                    cuts.ahead(i + N_DN // SLOTS, s)
            cuts.n += (FC // SLOTS - 1) * SLOTS
            dve.wait_ge(p_high, 1)
            nc.vector.tensor_tensor(ptl, prw, pth, ALU.subtract).then_inc(p_low, 1)
            cuts.upto(N_PP + 2)
            dve.wait_ge(slab_done, N_PP)
            for c in range(KC):
                nc.vector.scalar_tensor_tensor(out=X[:, c, 0:T], in0=bank(c), scalar=ISW,
                                               in1=X[:, c, 0:T], op0=ALU.mult,
                                               op1=ALU.add).then_inc(down_out, 1)
            cuts.upto(N_PG + 1)
            Norm("plen", 0).dve(dve)
            for n in range(N_PG, N_END):
                cuts.upto(n + 3)
                c = n - N_PG
                dve.wait_ge(pple_out, c + 1)
                dve.wait_ge(psig_out, c + 1)
                dchain.link(nc.vector.tensor_tensor(ptmp[:, c % 2, :], yout[:, c, :], pgs[:, c, :], ALU.mult))
                nc.vector.tensor_tensor(X[:, c, 0:T], X[:, c, 0:T], ptmp[:, c % 2, :],
                                        ALU.add).then_inc(ple_out, 1)
            Norm("final2", 0).dve(dve, dst=yout, done=y_out)

        @block.gpsimd
        def _(pool):
            nc.gpsimd.memset(EPSC, EPS).then_inc(pool_step, 1)
            pool.wait_ge(slab_done, N_WO)
            pool.wait_ge(gate_out, HEADS)
            nc.gpsimd.memset(kt8, 0.0)
            nc.gpsimd.memset(qt8, 0.0)
            nc.gpsimd.memset(rtmp, 0.0).then_inc(zeroed, 1)
            pool.wait_ge(zeroed, 1)
            for h in range(HEADS):
                for li in range(NL):
                    decayed(pool, nc.gpsimd, h, li, gk, KT, 0, kt_out)
            Norm("ln2", 3).add_squares(pool)
            pool.wait_ge(low_cut, LOW_POOL)
            def choice_turn(i, head=None):
                for s in range(SLOTS):
                    n = s + SLOTS - 1
                    cut_low_scaled(pool, i + (N_PQ // SLOTS + n // SLOTS), n % SLOTS)
                    if s == 2 and head is not None:
                        pool.wait_ge(sel_out, head + 1)
                        numbers = v3(tif[:, 0, :], TT).unsqueeze(2).to_broadcast([P, TT, TOP, TOP])
                        nc.gpsimd.tensor_tensor(sel4(0), sel4(0), numbers, ALU.mult).then_inc(sel_times, 1)

            choice_turn(0)
            with pool.Fori(1, PH + 1) as i:
                choice_turn(i, i - 1)
            for i in range(PH + 1, (N_U + BEHIND - N_PQ) // SLOTS):
                choice_turn(i)
            pool.wait_ge(gates_cut, 1)

            def gate_octet(e, b, tok):
                pool.wait_ge(hot_slab_out, e + 1)
                wait(pool, g_done, e * 2 - 2)
                for src, dst in ((gTh, hot_high), (gTl, hot_low))[:2 - b]:
                    last = nc.gpsimd.tensor_tensor(
                        dst[b], hot_slab[b], src[:, bass.ds(tok, OCT)].unsqueeze(2).to_broadcast([P, OCT, P]),
                        ALU.mult)
                last.then_inc(hot_gated, 1)

            gate_octet(0, 0, 0)
            gate_octet(1, 1, OCT)
            with pool.Fori(1, T // OCT // 2) as o:
                for b in range(2):
                    gate_octet(o * 2 + b, b, o * (2 * OCT) + b * OCT)
            pool.wait_ge(final1_out, KC)
            for z in zp:
                nc.gpsimd.memset(z[:, 0:16], 0.0).then_inc(pads, 1)
            for c in range(KC):
                pool.wait_ge(zpool_out, c + 1)
                if c == 0:
                    pool.wait_ge(pads, 2)
                if c >= 2:
                    pool.wait_ge(pool_cut, c - 1)
                src = zp[c % 2]
                for kk in range(c // 2 + 1):
                    w, n = 2 ** kk, WIN_STEPS[c] + kk
                    lo, dst = 2 * w - 1, win[c % 2][kk % 2]
                    if kk:
                        pool.wait_ge(window_out, n)
                    nc.gpsimd.tensor_tensor(dst[:, lo:16 + T], src[:, lo:16 + T], src[:, lo - w:16 + T - w],
                                            ALU.add).then_inc(window_out, 1)
                    src = dst
            pool.wait_ge(small_in, 32)
            w3 = v3(wsT, 8)
            nc.gpsimd.affine_select(out=w3, in_=w3, compare_op=ALU.is_ge, fill=0.0, base=0,
                                    pattern=[[0, 8], [1, P]], channel_multiplier=-1).then_inc(masked, 1)
            Norm("ffnn", 7).add_squares(pool)
            pool.wait_ge(res2_out, KC)
            for z in upb:
                nc.gpsimd.memset(z[:, 0:2], 0.0).then_inc(pads, 1)
            Norm("final2", 0).add_squares(pool)


def tables():
    inv = np.power(np.float32(500000.0), -np.arange(0, 2 * ROPE, 2, dtype=np.float32) / np.float32(2 * ROPE))
    pos = np.concatenate([np.arange(M, TM), np.arange(M)]).astype(np.float32)
    ang = (pos[:, None] * inv[None, :].astype(np.float32)).astype(np.float32)
    ropec, ropes = np.ones((P, TM), np.float32), np.zeros((P, TM), np.float32)
    perm = np.zeros((P, P), np.float32)
    for c in range(2):
        for i in range(ROPE):
            a, b = DH * c + i, DH * c + ROPE + i
            ropec[a] = ropec[b] = np.cos(ang[:, i])
            ropes[a], ropes[b] = -np.sin(ang[:, i]), np.sin(ang[:, i])
            perm[a, b] = perm[b, a] = 1.0
    i = np.arange(P)
    masks = np.zeros((P, len(SMALL) + 1, P), np.uint32)
    masks[:, 0] = np.eye(P, dtype=np.uint32)
    for n, s in enumerate(SMALL):
        masks[:, n + 1] = (i[:, None] // (2 * s) == i[None] // (2 * s)) & (i[:, None] // s != i[None] // s)
    return {
        "ident": np.eye(P, dtype=np.float32), "ones": np.ones((P, P), np.float32),
        "iota": np.tile(i.astype(np.float32), (P, 1)), "perm": perm, "masks": masks, "ropec": ropec,
        "ropes": ropes, "icnt": np.tile(1.0 / np.arange(1, 17, dtype=np.float32), (P, 1)).astype(np.float32),
        "strip": np.tile(((np.arange(P + 96) // 32) == 3).astype(np.float32), (P, 1)),
        "io16": np.tile(np.arange(16, dtype=np.float32), (P, 1)),
    }


def layout(a):
    f = {n: np.asarray(v) for n, v in a.items()}

    def chunks(w):
        kk, n = w.shape
        return w.reshape(kk // P, P, n // P, P).transpose(2, 1, 0, 3).reshape(n // P, P, -1)

    def rows(w):
        return w.reshape(4, 2, P, 512).transpose(0, 2, 1, 3).reshape(4, P, 1024)

    def wide(s):
        return np.concatenate([s, np.zeros((*s.shape[:2], D - s.shape[2]), np.float32)], 2) if s.shape[2] < D else s

    wi = f["w_in"][0]
    cut = np.split(wi, np.cumsum([512, 512, 512, 256, 256, 512, 512, 16])[:].tolist(), axis=1)
    dq, dk, dvw, gqw, gkw, gvw, grw, zf, zb = cut
    w2i = f["w_in_2"][0]
    pool, zu, zv, ga, gb = (w2i[:, i * D:(i + 1) * D] for i in range(5))
    up = chunks(f["w_up_2"][0])
    woven = lambda x, y: np.stack([x, y], 1).reshape(-1, P, x.shape[2])
    wp = f["w_pool_2"][0].reshape(4, 2, P, 2, P).transpose(0, 2, 3, 1, 4).reshape(4, P, 512)
    u = f["peer_u"][0].reshape(NK, NK, KC, P).transpose(0, 3, 2, 1).reshape(NK, P, D)
    two = lambda x: x.reshape(-1, 2, P, D)
    queries = np.concatenate([two(chunks(f["peer_w_q"][0])), two(u[:WOVEN])], 1).reshape(-1, P, D)
    parts = [chunks(dq), chunks(dk), rows(dvw), rows(gvw), chunks(gqw), chunks(gkw), chunks(grw),
             chunks(f["w_out"][0]), queries, u[WOVEN:], chunks(pool), wide(wp),
             rows(zv[:, :512]), rows(zv[:, 512:]), chunks(zu), woven(chunks(ga), chunks(f["w_branch_a_2"][0])),
             woven(chunks(gb), chunks(f["w_branch_b_2"][0])), chunks(f["w_out_2"][0]), woven(up[:FC], up[FC:]),
             f["w_down_2"][0].reshape(FC, P, D),
             chunks(f["w_ple_2"][0]).reshape(2, 4, P, 256).transpose(0, 2, 1, 3).reshape(2, P, D),
             chunks(f["w_ple_gate_2"][0])]
    w = np.concatenate(parts, 0)
    assert w.shape[0] == N_END, (w.shape, N_END)

    col = lambda v: v.reshape(-1, P).T
    pad = lambda v: np.concatenate([v, np.zeros(P - v.size, np.float32)])
    vecs = [col(f[n].reshape(-1)) for n in ("ln1_w", "ln2_w", "final_norm_w", "mix_norm_2", "pool_scale_2",
                                            "sgu_norm_2", "ffn_norm_2", "ple_norm_2", "final_norm_2")]
    vecs += [col(f["conv_w_2"][0].reshape(-1)), col(f["conv_b_2"][0]), f["da_subln_w"].T, f["gla_norm_w"].T]
    gf, gbk = f["gla_gate_b_f"][0].reshape(HEADS, DH), f["gla_gate_b_b"][0].reshape(HEADS, DH)
    vecs += [np.concatenate([gf, gbk], 1).T]
    vecs += [np.stack([pad(f[n][0]) for n in ("da_lambda_q1", "da_lambda_k1", "da_lambda_q2", "da_lambda_k2")], 1)]
    w2 = np.zeros((32, HEADS, P), np.float32)
    w2[:16, :, :DH] = f["gla_gate_w2_f"][0].reshape(16, HEADS, DH)
    w2[16:, :, DH:] = f["gla_gate_w2_b"][0].reshape(16, HEADS, DH)
    fm = lambda x: x.T.reshape(-1, P, x.shape[0]).transpose(1, 0, 2)
    out = {
        "xT": fm(f["x"][0]), "metaT": fm(f["meta_tokens"]), "vec": np.concatenate(vecs, 1), "w": w,
        "w2": w2, "wz": np.concatenate([zf, zb], 1).reshape(KC, P, 32).transpose(1, 0, 2).reshape(P, KC * 32),
        "keysT": f["peer_sub_keys"][0].reshape(2 * PH, NK, P).transpose(2, 0, 1),
        "v": f["peer_v"][0].reshape(NK, P, D),
        "wsT": f["w_spatial_2"][0].transpose(2, 0, 1).reshape(P, 8 * P), "bsp": f["b_spatial_2"][0].reshape(1, D),
        "pT": fm(f["p_2"][0, 0]), **tables(),
    }
    return {n: np.ascontiguousarray(v) for n, v in out.items()}


def kernel(**inputs):
    import concourse.bacc as bacc
    from concourse.bass_utils import run_bass_kernel_spmd

    nc = bacc.Bacc("TRN2", target_bir_lowering=False, num_devices=1)
    arrays = layout(inputs)
    io = {n: nc.dram_tensor(f"in_{n}", v.shape, mybir.dt.from_np(v.dtype), kind="ExternalInput").ap()
          for n, v in arrays.items()}
    out = nc.dram_tensor("out", (P, KC, T), mybir.dt.float32, kind="ExternalOutput").ap()
    build(nc, io, out)
    r = run_bass_kernel_spmd(nc, [{f"in_{n}": v for n, v in arrays.items()}], core_ids=[0])
    y = r.results[0]["out"]
    return np.ascontiguousarray(y.transpose(2, 1, 0)).reshape(1, T, D)
```
